# Optimizing a Trainium2 kernel written in Bass

```python
import jax
import jax.numpy as jnp
from jax import lax
import numpy as np

D_MODEL = 1024
BATCH = 1
SEQ = 512
DEPTH = 2

D_MIX = D_MODEL
RET_HEADS = 8
RET_DK = 64
RET_DV = 64
RET_CHUNK = 128
ROPE_BASE = 10000.0
NSA_HEADS = 8
NSA_KV_HEADS = 2
NSA_GROUP = NSA_HEADS // NSA_KV_HEADS
NSA_DH = 64
CMP_BLOCK = 32
CMP_STRIDE = 16
CMP_HIDDEN = 4 * NSA_DH
SLC_BLOCK = 64
SLC_TOPN = 16
WINDOW = 512
Q_BLOCK = 128
D_FF = 2816
CONV_WIDTH = 3
RMS_EPS = 1e-6
SEL_FORCE = 1e3
NEG_INF = -1e30
IN_SPLITS = (RET_HEADS * RET_DK, RET_HEADS * RET_DK, RET_HEADS * RET_DV, RET_HEADS * RET_DV, NSA_HEADS * NSA_DH, 6 * NSA_KV_HEADS * NSA_DH, 3 * NSA_HEADS)
IN_COLS = 2 * RET_HEADS * RET_DK + 2 * RET_HEADS * RET_DV + NSA_HEADS * NSA_DH + 6 * NSA_KV_HEADS * NSA_DH + 3 * NSA_HEADS

kernel_name = 'hybrid_retnet_nsa_convffn_sandwich'

def rms_norm(x, g):
    xf = x.astype(jnp.float32)
    y = xf * lax.rsqrt(jnp.mean(xf * xf, axis=-1, keepdims=True) + RMS_EPS)
    return (y * g.astype(jnp.float32)).astype(x.dtype)

def masked_softmax(s, mask):
    s = jnp.where(mask, s.astype(jnp.float32), NEG_INF)
    m = jnp.max(s, axis=-1, keepdims=True)
    e = jnp.where(mask, jnp.exp(s - m), 0.0)
    return e / jnp.maximum(jnp.sum(e, axis=-1, keepdims=True), 1e-30)

def rotary(x, pos):
    half = x.shape[-1] // 2
    inv = 1.0 / (ROPE_BASE ** jnp.linspace(0.0, 1.0, half, dtype=jnp.float32))
    ang = pos.astype(jnp.float32)[:, None] * inv[None, :]
    cos = jnp.cos(ang)[:, None, :].astype(x.dtype)
    sin = jnp.sin(ang)[:, None, :].astype(x.dtype)
    x1, x2 = x[..., :half], x[..., half:]
    return jnp.concatenate([x1 * cos - x2 * sin, x1 * sin + x2 * cos], axis=-1)

def retention(q, k, v, g):
    B, T, _ = q.shape
    H, C = RET_HEADS, RET_CHUNK
    N = T // C
    pos = jnp.arange(T)
    q = rotary(q.reshape(B, T, H, RET_DK), pos)
    k = rotary(k.reshape(B, T, H, RET_DK), pos) * (RET_DK ** -0.5)
    v = v.reshape(B, T, H, RET_DV)
    to_chunks = lambda a: a.reshape(B, N, C, H, a.shape[-1]).transpose(0, 3, 1, 2, 4)
    q, k, v = to_chunks(q), to_chunks(k), to_chunks(v)
    log_g = jnp.log(1.0 - 2.0 ** (-5.0 - jnp.arange(H, dtype=jnp.float32)))
    i = jnp.arange(C, dtype=jnp.float32)
    diff = i[:, None] - i[None, :]
    dmask = jnp.where(diff >= 0, jnp.exp(jnp.maximum(diff, 0.0)[None] * log_g[:, None, None]), 0.0).astype(q.dtype)
    zeta = jnp.exp((C - 1 - i)[None, :] * log_g[:, None]).astype(q.dtype)
    xi = jnp.exp((i + 1)[None, :] * log_g[:, None]).astype(q.dtype)
    chunk_decay = jnp.exp(C * log_g).astype(q.dtype)
    scores = jnp.einsum('bhncd,bhnsd->bhncs', q, k) * dmask[None, :, None]
    o_inner = jnp.einsum('bhncs,bhnse->bhnce', scores, v)
    kv = jnp.einsum('bhncd,bhnce->bhnde', k, v * zeta[None, :, None, :, None])

    def step(state, kv_n):
        return chunk_decay[None, :, None, None] * state + kv_n, state

    _, states = lax.scan(step, jnp.zeros_like(kv[:, :, 0]), jnp.moveaxis(kv, 2, 0))
    states = jnp.moveaxis(states, 0, 2)
    o_cross = jnp.einsum('bhncd,bhnde->bhnce', q * xi[None, :, None, :, None], states)
    o = (o_inner + o_cross).astype(jnp.float32)
    o = o * lax.rsqrt(jnp.mean(o * o, axis=-1, keepdims=True) + RMS_EPS)
    o = o.transpose(0, 2, 3, 1, 4).reshape(B, T, H * RET_DV).astype(g.dtype)
    return jax.nn.silu(g) * o

def compress(k, pos_emb, w1, b1, w2, b2):
    T = k.shape[2]
    nc = (T - CMP_BLOCK) // CMP_STRIDE + 1
    idx = jnp.arange(nc)[:, None] * CMP_STRIDE + jnp.arange(CMP_BLOCK)[None, :]
    blk = k[:, :, idx, :] + pos_emb
    z = blk.reshape(blk.shape[0], blk.shape[1], nc, CMP_BLOCK * NSA_DH)
    return jax.nn.gelu(z @ w1 + b1) @ w2 + b2

def nsa(nq, nkv, ngate, kpos, kw1, kb1, kw2, kb2, vpos, vw1, vb1, vw2, vb2):
    B, T, _ = nq.shape
    Hk, G, dh = NSA_KV_HEADS, NSA_GROUP, NSA_DH
    q = nq.reshape(B, T, Hk, G, dh).transpose(0, 2, 3, 1, 4)
    kv = nkv.reshape(B, T, 6, Hk, dh).transpose(2, 0, 3, 1, 4)
    gates = jax.nn.sigmoid(ngate.astype(jnp.float32)).reshape(B, T, Hk, G, 3).astype(nq.dtype)
    kc = compress(kv[0], kpos, kw1, kb1, kw2, kb2)
    vc = compress(kv[1], vpos, vw1, vb1, vw2, vb2)
    nc = kc.shape[2]
    ns = T // SLC_BLOCK
    n_sel = min(SLC_TOPN, ns)
    ks_blk = kv[2].reshape(B, Hk, ns, SLC_BLOCK, dh)
    vs_blk = kv[3].reshape(B, Hk, ns, SLC_BLOCK, dh)
    kw_p = jnp.pad(kv[4], ((0, 0), (0, 0), (WINDOW, 0), (0, 0)))
    vw_p = jnp.pad(kv[5], ((0, 0), (0, 0), (WINDOW, 0), (0, 0)))
    ci = jnp.arange(nc)
    sj = jnp.arange(ns)
    c_start = ci * CMP_STRIDE
    overlap = ((c_start[:, None] < (sj[None, :] + 1) * SLC_BLOCK) & (c_start[:, None] + CMP_BLOCK > sj[None, :] * SLC_BLOCK)).astype(jnp.float32)
    bi = jnp.arange(B)[:, None, None, None]
    hi = jnp.arange(Hk)[None, :, None, None]
    scale = dh ** -0.5
    nb = T // Q_BLOCK

    def block(b):
        s0 = b * Q_BLOCK
        t = s0 + jnp.arange(Q_BLOCK)
        qb = lax.dynamic_slice_in_dim(q, s0, Q_BLOCK, axis=3) * scale
        gb = lax.dynamic_slice_in_dim(gates, s0, Q_BLOCK, axis=1).transpose(0, 2, 3, 1, 4)
        sc = jnp.einsum('bhgqd,bhcd->bhgqc', qb, kc)
        mc = (c_start + CMP_BLOCK - 1)[None, :] <= t[:, None]
        pc = masked_softmax(sc, mc)
        o_cmp = jnp.einsum('bhgqc,bhcd->bhgqd', pc.astype(vc.dtype), vc)
        imp = jnp.einsum('bhqc,cs->bhqs', jnp.sum(pc, axis=2), overlap)
        cur = t // SLC_BLOCK
        forced = (sj[None, :] == 0) | (sj[None, :] == cur[:, None]) | (sj[None, :] == cur[:, None] - 1)
        causal_blk = sj[None, :] * SLC_BLOCK <= t[:, None]
        score = jnp.where(causal_blk, imp + jnp.where(forced, SEL_FORCE, 0.0), NEG_INF)
        _, sel = lax.top_k(score, n_sel)
        kg = ks_blk[bi, hi, sel]
        vg = vs_blk[bi, hi, sel]
        ss = jnp.einsum('bhgqd,bhqnkd->bhgqnk', qb, kg).reshape(B, Hk, G, Q_BLOCK, n_sel * SLC_BLOCK)
        pos_s = (sel[..., None] * SLC_BLOCK + jnp.arange(SLC_BLOCK)).reshape(B, Hk, 1, Q_BLOCK, n_sel * SLC_BLOCK)
        ps = masked_softmax(ss, pos_s <= t[:, None]).reshape(B, Hk, G, Q_BLOCK, n_sel, SLC_BLOCK)
        o_slc = jnp.einsum('bhgqnk,bhqnkd->bhgqd', ps.astype(vg.dtype), vg)
        kwb = lax.dynamic_slice_in_dim(kw_p, s0, Q_BLOCK + WINDOW, axis=2)
        vwb = lax.dynamic_slice_in_dim(vw_p, s0, Q_BLOCK + WINDOW, axis=2)
        pw = s0 - WINDOW + jnp.arange(Q_BLOCK + WINDOW)
        mw = (pw[None, :] <= t[:, None]) & (pw[None, :] > t[:, None] - WINDOW) & (pw[None, :] >= 0)
        pwin = masked_softmax(jnp.einsum('bhgqd,bhkd->bhgqk', qb, kwb), mw)
        o_win = jnp.einsum('bhgqk,bhkd->bhgqd', pwin.astype(vwb.dtype), vwb)
        return gb[..., 0:1] * o_cmp + gb[..., 1:2] * o_slc + gb[..., 2:3] * o_win

    o = lax.map(block, jnp.arange(nb))
    return o.transpose(1, 0, 4, 2, 3, 5).reshape(B, T, NSA_HEADS * dh)

def conv_ffn(h, w_up, conv_w, conv_b, w_down):
    u = h @ w_up
    u = lax.conv_general_dilated(u, conv_w[:, None, :], (1,), [(CONV_WIDTH - 1, 0)], dimension_numbers=('NWC', 'WIO', 'NWC'), feature_group_count=u.shape[-1]) + conv_b
    a, v = jnp.split(u, 2, axis=-1)
    return (jax.nn.gelu(a) * v) @ w_down

def setup_inputs(seed: int = 0) -> dict:
    key = jax.random.key(seed)
    ks = jax.random.split(key, 24)
    nrm = lambda k, shape, s: jax.random.normal(k, shape, jnp.float32) * s
    gain = lambda k: 1.0 + 0.05 * jax.random.normal(k, (DEPTH, D_MODEL), jnp.float32)
    L = CMP_BLOCK * NSA_DH
    return {
        'x': nrm(ks[0], (BATCH, SEQ, D_MODEL), 1.0),
        'ln_mix_pre': gain(ks[1]),
        'ln_mix_post': gain(ks[2]),
        'ln_ffn_pre': gain(ks[3]),
        'ln_ffn_post': gain(ks[4]),
        'w_in': nrm(ks[5], (DEPTH, D_MODEL, IN_COLS), D_MODEL ** -0.5),
        'w_out': nrm(ks[6], (DEPTH, D_MIX, D_MODEL), D_MIX ** -0.5),
        'cmp_k_pos': nrm(ks[7], (DEPTH, CMP_BLOCK, NSA_DH), 0.1),
        'cmp_k_w1': nrm(ks[8], (DEPTH, L, CMP_HIDDEN), L ** -0.5),
        'cmp_k_b1': nrm(ks[9], (DEPTH, CMP_HIDDEN), 0.01),
        'cmp_k_w2': nrm(ks[10], (DEPTH, CMP_HIDDEN, NSA_DH), CMP_HIDDEN ** -0.5),
        'cmp_k_b2': nrm(ks[11], (DEPTH, NSA_DH), 0.01),
        'cmp_v_pos': nrm(ks[12], (DEPTH, CMP_BLOCK, NSA_DH), 0.1),
        'cmp_v_w1': nrm(ks[13], (DEPTH, L, CMP_HIDDEN), L ** -0.5),
        'cmp_v_b1': nrm(ks[14], (DEPTH, CMP_HIDDEN), 0.01),
        'cmp_v_w2': nrm(ks[15], (DEPTH, CMP_HIDDEN, NSA_DH), CMP_HIDDEN ** -0.5),
        'cmp_v_b2': nrm(ks[16], (DEPTH, NSA_DH), 0.01),
        'ffn_w_up': nrm(ks[17], (DEPTH, D_MODEL, 2 * D_FF), D_MODEL ** -0.5),
        'ffn_conv_w': nrm(ks[18], (DEPTH, CONV_WIDTH, 2 * D_FF), CONV_WIDTH ** -0.5),
        'ffn_conv_b': nrm(ks[19], (DEPTH, 2 * D_FF), 0.01),
        'ffn_w_down': nrm(ks[20], (DEPTH, D_FF, D_MODEL), D_FF ** -0.5),
    }

def reference(x, ln_mix_pre, ln_mix_post, ln_ffn_pre, ln_ffn_post, w_in, w_out, cmp_k_pos, cmp_k_w1, cmp_k_b1, cmp_k_w2, cmp_k_b2, cmp_v_pos, cmp_v_w1, cmp_v_b1, cmp_v_w2, cmp_v_b2, ffn_w_up, ffn_conv_w, ffn_conv_b, ffn_w_down):
    bounds = np.cumsum(IN_SPLITS)[:-1].tolist()
    for l in range(DEPTH):
        h = rms_norm(x, ln_mix_pre[l])
        proj = h @ w_in[l]
        rq, rk, rv, rg, nq, nkv, ngate = jnp.split(proj, bounds, axis=-1)
        y_ret = retention(rq, rk, rv, rg)
        y_nsa = nsa(nq, nkv, ngate, cmp_k_pos[l], cmp_k_w1[l], cmp_k_b1[l], cmp_k_w2[l], cmp_k_b2[l], cmp_v_pos[l], cmp_v_w1[l], cmp_v_b1[l], cmp_v_w2[l], cmp_v_b2[l])
        mix = jnp.concatenate([y_ret, y_nsa], axis=-1) @ w_out[l]
        x = x + rms_norm(mix, ln_mix_post[l])
        h = rms_norm(x, ln_ffn_pre[l])
        f = conv_ffn(h, ffn_w_up[l], ffn_conv_w[l], ffn_conv_b[l], ffn_w_down[l])
        x = x + rms_norm(f, ln_ffn_post[l])
    return x


_drawn_inputs = setup_inputs


def setup_inputs(seed=0):
    import zlib

    import numpy as np

    out = dict(_drawn_inputs(seed))
    spreads = {}
    factors = {'cmp_k_pos': 6.716,
     'cmp_k_b1': 64.0,
     'cmp_k_b2': 64.0,
     'cmp_v_b1': 8.0,
     'cmp_v_b2': 4.471,
     'ffn_conv_b': 4.197}
    for name, (base, spread) in spreads.items():
        noise = np.random.default_rng([zlib.crc32(name.encode()), seed]).standard_normal(out[name].shape)
        drawn = base * np.exp(spread * noise) if base else spread * noise
        out[name] = jnp.asarray(drawn.astype(out[name].dtype))
    for name, factor in factors.items():
        out[name] = (out[name] * factor).astype(out[name].dtype)
    return out
```

```python
from contextlib import ExitStack

import numpy as np

import concourse.bass as bass
from concourse import mybir

F32 = mybir.dt.float32
F32R = mybir.dt.float32r
BF16 = mybir.dt.bfloat16
ACT = mybir.ActivationFunctionType
ALU = mybir.AluOpType
AXX = mybir.AxisListType.X

P = 128
DEPTH, SEQ, D = 2, 512, 1024
T = SEQ // P
KD = D // P
RH, DK = 8, 64
NH, NKV, DH = 8, 2, 64
G = NH // NKV
CB, CS = 32, 16
NC = (SEQ - CB) // CS + 1
NCP = 32
HID = 4 * DH
FF = 2816
KF = FF // P
EPS = 1e-6
NEG = -1e30
NEG_GUARD = -1e29
SM = DH ** -0.5

CW = 1024
RING = 4
C_T = 0
C_TV = C_T + 16
NTV = 2 * NKV * DH + 3 * NH
C_F0 = C_TV + 4
C_F1 = C_F0 + 1
C_W1K = C_F1 + 1
C_W1V = C_W1K + 4
C_F2 = C_W1V + 4
C_WO = C_F2 + 6
C_UP = C_WO + 8
C_DN = C_UP + 2 * KF
NCH = C_DN + KF

O_COS, O_SIN, O_NSIN = 0, 128, 256
O_DM = 384
O_XI = O_DM + RH * P
O_ZE = O_XI + 4 * P
O_BD = O_ZE + RH
O_DE = O_BD + P
O_ID = O_DE + 4
O_CA = O_ID + P
O_CM = O_CA + P
NCONST = O_CM + T * NCP

Q_POS = 0
Q_B1 = Q_POS + 2 * 16
Q_W2 = Q_B1 + 4
Q_B2K = Q_W2 + 4 * DH
Q_CV = Q_B2K + 2
NPAR = Q_CV + 2 * KF * 4


MIDDLE = [("turn", 0), ("chunk", C_F0), ("score", 0), ("chunk", C_F1), ("out", 0), ("turn", 1),
          ("chunk", C_W1K), ("chunk", C_W1K + 1), ("norm", 0), ("score", 1), ("chunk", C_W1K + 2),
          ("chunk", C_W1K + 3), ("out", 1), ("turn", 2), ("norm", 1), ("chunk", C_W1V), ("score", 2),
          ("chunk", C_W1V + 1), ("out", 2), ("turn", 3), ("norm", 2), ("chunk", C_W1V + 2), ("score", 3),
          ("chunk", C_W1V + 3), ("out", 3), ("norm", 3)]
RET_NORM_AFTER = {C_W1K + 1: 0, C_W1V + 1: 1, C_W1V + 3: 2, C_F2 + 1: 3}


def build(nc, x_in, wstream, gains, pars, b2v_in, consts, x_out):
    ctx = ExitStack()
    with ctx:
        def sb(name, shape, dt=F32, stack=ctx):
            return stack.enter_context(nc.sbuf_tensor(name, shape, dt))

        sems = {}

        def sem(name, per_layer, start=0):
            s = ctx.enter_context(nc.semaphore(name))
            sems[name] = (s, per_layer, start)
            return s

        def upto(s, layer, count):
            per, start = next((n, f) for q, n, f in sems.values() if q is s)
            assert count + start > 0, s
            return layer * per + (count + start)

        const = sb("const", [P, NCONST])
        ident_b = sb("ident_b", [P, P], BF16)
        causal_b = sb("causal_b", [P, P], BF16)
        cmask_b = sb("cmask_b", [P, T * NCP], BF16)
        x = sb("x", [P, T, D])
        act_hi = sb("act_hi", [P, KD, SEQ], F32R)
        act_lo = sb("act_lo", [P, KD, SEQ], F32R)
        raw = sb("raw", [P, RING, CW])
        w_hi = sb("w_hi", [P, RING, CW], F32R)
        w_lo = sb("w_lo", [P, RING, CW], F32R)
        g_mix_pre = sb("g_mix_pre", [P, D])
        g_rest = sb("g_rest", [P, 3, D])
        par = sb("par", [P, NPAR])
        b2v = sb("b2v", [NCP, DH])
        junk = sb("junk", [P, D], BF16)
        gate = sb("gate", [P, T, 3 * NH])
        sq_sum = sb("sq_sum", [P, 2])
        mean_eps = sb("mean_eps", [P, RH])
        rstd = sb("rstd", [P, RH])
        minus_half = sb("minus_half", [P, RH])
        eps1 = sb("eps1", [P, 1])
        eps4 = sb("eps4", [P, RH])
        head_ms = sb("head_ms", [P, RH])
        s_max = sb("s_max", [P, 2, G])
        s_bias = sb("s_bias", [P, 2, G])
        s_sum = sb("s_sum", [P, 2, G])
        s_rec = sb("s_rec", [P, 2, G])
        c_stat = sb("c_stat", [P, NH * T])
        c_rec = sb("c_rec", [P, NH * T])
        VS = sb("VS", [P, T, 2 * NKV, 2 * DH], F32R)
        KcH = sb("KcH", [P, NKV * NCP], F32R)
        KcL = sb("KcL", [P, NKV * NCP], F32R)
        VcS = sb("VcS", [NCP, NKV, 2 * DH], F32R)
        kcf = sb("kcf", [DH, NKV * NCP])
        vcf = sb("vcf", [NCP, NKV, DH])
        with ExitStack() as ret:
            qr = sb("qr", [P, T, RH * DK], F32, ret)
            kr = sb("kr", [P, T, RH * DK], F32, ret)
            rv = sb("rv", [P, T, RH * DK], F32, ret)
            sg = sb("sg", [P, T, RH * DK], F32, ret)
            qT = sb("qT", [P, 4, P], F32, ret)
            qxT = sb("qxT", [P, 4, P], F32, ret)
            kT = sb("kT", [P, 4, P], F32, ret)
            stm = sb("stm", [P, RH, P], F32, ret)
            vz = sb("vz", [P, RH * DK], F32, ret)
            state = sb("state", [P, 4, P], F32, ret)
            kvt = sb("kvt", [P, 4, P], F32, ret)
            rtmp = sb("rtmp", [P, RH * DK], F32, ret)
            th = sb("th", [P, RH * DK], F32, ret)
            osq = sb("osq", [P, RH * DK], F32, ret)
            with ExitStack() as early:
                h = sb("h", [P, 2, D], F32, early)
            zf = sb("zf", [P, 16, NKV, NCP], F32, ret)
            z_hi = sb("z_hi", [P, 16 * NKV * NCP], F32R, ret)
            z_lo = sb("z_lo", [P, 16 * NKV * NCP], F32R, ret)
            hid = sb("hid", [P, 2, 2, NKV * NCP], F32, ret)
        with ExitStack() as att:
            E = sb("E", [P, 2, G, SEQ], F32, att)
            QS = sb("QS", [P, NH, SEQ], F32R, att)
            KH = sb("KH", [P, 2 * NKV, SEQ], F32R, att)
            KL = sb("KL", [P, 2 * NKV, SEQ], F32R, att)
            pt_h = sb("pt_h", [P, 2, G * P], F32R, att)
            pt_l = sb("pt_l", [P, 2, G * P], F32R, att)
            o_a = sb("o_a", [DH, G * P], F32, att)
            o_f = sb("o_f", [P, 2, P], F32, att)
            cE = sb("cE", [P, T * NKV * G, NCP], F32, att)
        with ExitStack() as ffn:
            gff = sb("gff", [P, KF, SEQ], F32, ffn)
            cv = sb("cv", [P, 2, 2, SEQ], F32, ffn)
        bank = ctx.enter_context(nc.psum_tensor("bank", [P, 8, 512], F32))

        cos = const[:, O_COS:O_SIN].rearrange("p (t f) -> p t f", t=T)
        sin = const[:, O_SIN:O_NSIN].rearrange("p (t f) -> p t f", t=T)
        nsin = const[:, O_NSIN:O_DM].rearrange("p (t f) -> p t f", t=T)
        dmask = const[:, O_DM:O_XI].rearrange("p (h c) -> p h c", h=RH)
        xi = const[:, O_XI:O_ZE].rearrange("p (a c) -> p a c", a=4)
        zeta = const[:, O_ZE:O_BD]
        bdiag = const[:, O_BD:O_DE]
        decay = const[:, O_DE:O_ID]
        ident = const[:, O_ID:O_CA]
        r32 = lambda ap: ap.bitcast(F32)

        AHEAD = 8
        raw_loaded = [sem(f"raw_loaded{s}", 16 * len(range(s, NCH, RING))) for s in range(RING)]
        hi_ready = sem("hi_ready", NCH)
        lo_ready = sem("lo_ready", NCH, start=RING)
        w_used = sem("w_used", NCH, start=RING)
        const_loaded = sem("const_loaded", 0)
        const_cast = sem("const_cast", 0)
        half_set = sem("half_set", 0)
        mixpre_loaded = sem("mixpre_loaded", 16)
        par_loaded = sem("par_loaded", 48)
        sq_done = sem("sq_done", 24)
        rstd_step = sem("rstd_step", 48, start=1)
        h_ready = sem("h_ready", 8, start=1)
        h_turned = sem("h_turned", 8)
        act_h = sem("act_h", 16)
        act_l = sem("act_l", 16)
        x_step = sem("x_step", 24, start=1)
        t_done = sem("t_done", 15)
        rot_step = sem("rot_step", 32, start=1)
        rv_ready = sem("rv_ready", 4)
        th_ready = sem("th_ready", 4)
        sg_ready = sem("sg_ready", 4)
        vg_act = sem("vg_act", 8)
        vg_dve = sem("vg_dve", 8)
        z_step = sem("z_step", 17)
        z_h = sem("z_h", 2)
        z_l = sem("z_l", 2)
        w1_done = sem("w1_done", 2)
        hid_ready = sem("hid_ready", 4)
        kc_done = sem("kc_done", 1)
        vc_done = sem("vc_done", 1)
        kc_f = sem("kc_f", 1)
        kc_h = sem("kc_h", 2)
        kc_l = sem("kc_l", 2)
        vc_f = sem("vc_f", 1)
        vc_h = sem("vc_h", 1)
        vc_l = sem("vc_l", 1)
        qk_turned = sem("qk_turned", 8)
        qk_copied = sem("qk_copied", 8)
        qx_ready = sem("qx_ready", 4)
        st_done = sem("st_done", 8)
        st_masked = sem("st_masked", 8)
        vz_ready = sem("vz_ready", 3)
        kv_done = sem("kv_done", 3)
        ro_done = sem("ro_done", 4)
        state_step = sem("state_step", 7)
        osq_ready = sem("osq_ready", 4)
        head_sum = sem("head_sum", 4)
        y_step = sem("y_step", 8)
        y_turned = sem("y_turned", 4)
        y_h = sem("y_h", 4)
        y_l = sem("y_l", 4)
        k_h = sem("k_h", 8)
        k_l = sem("k_l", 8)
        q_h = sem("q_h", 8)
        q_l = sem("q_l", 8)
        cs_done = sem("cs_done", 2)
        c_step = sem("c_step", 9)
        c_exp = sem("c_exp", 1)
        NU = T * NKV * 2
        s_done = sem("s_done", NU)
        m_step = sem("m_step", 2 * NU)
        e_done = sem("e_done", G * NU)
        r_step = sem("r_step", 3 * NU)
        p_scaled = sem("p_scaled", G * NU)
        NI = T * NKV + 2 * NKV * T * (T + 1) // 2
        pt_done = sem("pt_done", NI)
        pth = sem("pth", NI)
        ptl = sem("ptl", NI)
        pv_done = sem("pv_done", NI)
        oa_done = sem("oa_done", T * NKV)
        of_done = sem("of_done", 2 * T * NKV)
        oh_done = sem("oh_done", 2 * T * NKV)
        ol_done = sem("ol_done", 2 * T * NKV)
        wo_done = sem("wo_done", 6)
        cv0 = sem("cv0", 2 * KF)
        cv_step = sem("cv_step", 4 * KF, start=AHEAD)
        gelu_done = sem("gelu_done", KF)
        g_ready = sem("g_ready", KF, start=1)
        gh = sem("gh", KF)
        gl = sem("gl", KF)
        dn_done = sem("dn_done", T - 1)
        stored = sem("stored", 0)

        UNITS = [(i, g, b) for i in range(T) for g in range(NKV) for b in range(2)]
        ITEMS = []
        for n, (i, g, b) in enumerate(UNITS):
            if b == 0:
                ITEMS.append((None, i * NKV + g, 0))
            ITEMS += [(n, i * NKV + g, j) for j in range(i + 1)]
        assert len(ITEMS) == NI
        LAST_OF_V = {v: max(k for k, it in enumerate(ITEMS) if it[1] == v) for v in range(T * NKV)}
        items_of = lambda n: [k for k, it in enumerate(ITEMS)
                              if it[0] == n or (it[0] is None and UNITS[n][2] == 0
                                                and it[1] == UNITS[n][0] * NKV + UNITS[n][1])]
        RS_PRE1 = lambda t: 2 * t
        RS_RET = lambda n: 8 + 2 * n
        RS_POST1 = lambda t: 16 + 5 * t
        RS_PRE2 = lambda t: 19 + 5 * t
        RS_POST2 = lambda t: 36 + 3 * t
        SQ_PRE1 = lambda t: t
        SQ_POST1 = lambda t: 4 + 3 * t
        SQ_PRE2 = lambda t: 6 + 3 * t
        SQ_POST2 = lambda t: 16 + 2 * t

        def slot_free(eng, s, layer, c):
            before = c - RING if c >= RING else max(range(c, NCH, RING)) - NCH
            eng.wait_ge(s, layer * NCH + (before + 1 + RING))

        def chunk_used(eng, layer, c):
            eng.wait_ge(w_used, layer * NCH + (c + 1 + RING))

        def tile_done(eng, layer, done, block_no, t, last_chunk):
            if t < T - 1:
                eng.wait_ge(done, upto(done, layer, (T - 1) * block_no + t + 1))
            else:
                chunk_used(eng, layer, last_chunk)

        block = ctx.enter_context(nc.Block())

        @block.sync
        def _(sp):
            sp.dma_start(const[:], consts).then_inc(const_loaded, 16)
            for t in range(T):
                sp.dma_start(x[:, t, :], x_in[t * P:(t + 1) * P, :]).then_inc(const_loaded, 16)
            sp.dma_start(g_mix_pre[:], gains[0, 0:1, 0:D].broadcast_to([P, D])).then_inc(mixpre_loaded, 16)

            def load(layer, c, s, quad=None):
                if quad is None:
                    slot_free(sp, lo_ready, layer, c)
                    sp.dma_start(raw[:, s, :], wstream[layer, c]).then_inc(raw_loaded[s], 16)
                else:
                    sp.wait_ge(lo_ready, layer * NCH + quad * RING + (s + 1))
                    sp.dma_start(raw[:, s, :], wstream[layer, quad * RING + s]).then_inc(raw_loaded[s], 16)

            with sp.Fori(0, DEPTH) as l:
                for c in range(RING):
                    load(l, c, c)
                sp.wait_ge(x_step, upto(x_step, l, 0))
                sp.dma_start(par[:], pars[l]).then_inc(par_loaded, 16)
                sp.dma_start(b2v[:], b2v_in[l, 0:1, :].broadcast_to([NCP, DH])).then_inc(par_loaded, 16)
                sp.dma_start(g_rest[:].rearrange("p a d -> p (a d)"),
                             gains[l, 1:2, :].broadcast_to([P, 3 * D])).then_inc(par_loaded, 16)
                with sp.Fori(1, C_UP // RING) as quad:
                    for s in range(RING):
                        load(l, None, s, quad)
                sp.wait_ge(h_ready, upto(h_ready, l, 4))
                sp.dma_start(g_mix_pre[:], gains[l + 1, 0:1, 0:D].broadcast_to([P, D]))\
                    .then_inc(mixpre_loaded, 16)
                with sp.Fori(C_UP // RING, NCH // RING) as quad:
                    for s in range(RING):
                        load(l, None, s, quad)
                for c in range(NCH // RING * RING, NCH):
                    load(l, c, c % RING)
            for t in range(T):
                sp.wait_ge(x_step, upto(x_step, DEPTH - 1, 12 + 3 * (t + 1)))
                sp.dma_start(x_out[t * P:(t + 1) * P, :], x[:, t, :]).then_inc(stored, 16)
            sp.wait_ge(stored, 16 * T)
            sp.wait_ge(mixpre_loaded, 16 * (DEPTH + 1))

        @block.gpsimd
        def _(pool):
            pool.sem_inc(lo_ready, RING)
            pool.sem_inc(rstd_step, 1)
            nc.gpsimd.memset(minus_half[:], -0.5).then_inc(half_set, 1)
            nc.gpsimd.memset(eps1[:], EPS).then_inc(half_set, 1)
            nc.gpsimd.memset(eps4[:], 4.0 * EPS).then_inc(half_set, 1)
            pool.wait_ge(half_set, 3)

            def split_lo(layer, c):
                s = c % RING
                pool.wait_ge(hi_ready, upto(hi_ready, layer, c + 1))
                slot_free(pool, w_used, layer, c)
                nc.gpsimd.tensor_tensor(w_lo[:, s, :], raw[:, s, :], r32(w_hi[:, s, :]), ALU.subtract)\
                    .then_inc(lo_ready, 1)

            def split_lo_quad(layer, quad):
                for s in range(RING):
                    pool.wait_ge(hi_ready, layer * NCH + quad * RING + (s + 1))
                    pool.wait_ge(w_used, layer * NCH + quad * RING + (s + 1))
                    nc.gpsimd.tensor_tensor(w_lo[:, s, :], raw[:, s, :], r32(w_hi[:, s, :]),
                                            ALU.subtract).then_inc(lo_ready, 1)

            def inv_root(layer, step, n, source, eps):
                nc.gpsimd.tensor_tensor(mean_eps[:, 0:n], source, eps, ALU.add).then_inc(rstd_step, 1)
                pool.wait_ge(rstd_step, upto(rstd_step, layer, step + 1))
                nc.gpsimd.tensor_tensor(rstd[:, 0:n], mean_eps[:, 0:n], minus_half[:, 0:n], ALU.pow)\
                    .then_inc(rstd_step, 1)

            def inv_root_pre(layer, step, sq, rstd_free):
                rstd_free()
                pool.wait_ge(rstd_step, upto(rstd_step, layer, step))
                pool.wait_ge(sq_done, upto(sq_done, layer, sq + 1))
                inv_root(layer, step, 1, sq_sum[:, 0:1], eps1[:])

            def inv_root_post(layer, step, sq, rstd_free):
                rstd_free()
                pool.wait_ge(rstd_step, upto(rstd_step, layer, step))
                pool.wait_ge(sq_done, upto(sq_done, layer, sq + 2))
                nc.gpsimd.tensor_tensor(mean_eps[:, 1:2], sq_sum[:, 0:1], sq_sum[:, 1:2], ALU.add)\
                    .then_inc(rstd_step, 1)
                pool.wait_ge(rstd_step, upto(rstd_step, layer, step + 1))
                inv_root(layer, step + 1, 1, mean_eps[:, 1:2], eps1[:])

            with pool.Fori(0, DEPTH) as l:
                for t in range(T):
                    inv_root_pre(l, RS_PRE1(t), SQ_PRE1(t),
                                 (lambda t=t: pool.wait_ge(h_ready, upto(h_ready, l, t))) if t else
                                 (lambda: pool.wait_ge(x_step, upto(x_step, l, 0))))
                    split_lo(l, t)
                with pool.Fori(1, C_F0 // RING) as quad:
                    split_lo_quad(l, quad)
                for c in range(C_F0, C_F2 + 4):
                    split_lo(l, c)
                    if c in RET_NORM_AFTER:
                        n = RET_NORM_AFTER[c]
                        pool.wait_ge(head_sum, upto(head_sum, l, n + 1))
                        pool.wait_ge(rstd_step, upto(rstd_step, l, RS_RET(n)))
                        if n:
                            pool.wait_ge(y_step, upto(y_step, l, 2 * n - 1))
                        else:
                            pool.wait_ge(h_ready, upto(h_ready, l, 4))
                        inv_root(l, RS_RET(n), RH, head_ms[:], eps4[:])
                for c in range(C_F2 + 4, C_WO + RING):
                    split_lo(l, c)
                for c in range(C_WO + RING, C_UP + 3):
                    split_lo(l, c)
                for t in range(T):
                    inv_root_post(l, RS_POST1(t), SQ_POST1(t),
                                  (lambda t=t: pool.wait_ge(h_ready, upto(h_ready, l, 4 + t))) if t else
                                  (lambda: pool.wait_ge(y_step, upto(y_step, l, 8))))
                    inv_root_pre(l, RS_PRE2(t), SQ_PRE2(t),
                                 lambda t=t: pool.wait_ge(x_step, upto(x_step, l, 3 * t + 2)))
                split_lo(l, C_UP + 3)
                with pool.Fori(C_UP // RING + 1, NCH // RING) as quad:
                    split_lo_quad(l, quad)
                for c in range(NCH // RING * RING, NCH):
                    split_lo(l, c)
                for t in range(T):
                    inv_root_post(l, RS_POST2(t), SQ_POST2(t),
                                  (lambda t=t: pool.wait_ge(x_step, upto(x_step, l, 12 + 3 * (t - 1) + 2))) if t else
                                  (lambda: pool.wait_ge(h_ready, upto(h_ready, l, 8))))

        @block.scalar
        def _(act):
            def hi(layer, c):
                s = c % RING
                act.wait_ge(raw_loaded[s], upto(raw_loaded[s], layer, 16 * (c // RING + 1)))
                slot_free(act, w_used, layer, c)
                nc.scalar.activation(w_hi[:, s, :], raw[:, s, :], ACT.Copy).then_inc(hi_ready, 1)

            def hi_quad(layer, quad, s):
                act.wait_ge(raw_loaded[s], layer * sems[f"raw_loaded{s}"][1] + quad * 16 + 16)
                act.wait_ge(w_used, layer * NCH + quad * RING + (s + 1))
                nc.scalar.activation(w_hi[:, s, :], raw[:, s, :], ACT.Copy).then_inc(hi_ready, 1)

            def square_pre(layer, t, sq, rs_before):
                rs_before()
                nc.scalar.activation(junk[:], x[:, t, :], ACT.Square, scale=D ** -0.5,
                                     accum_out=sq_sum[:, 0:1]).then_inc(sq_done, 1)

            def square_post(layer, t, sq, rs_before):
                rs_before()
                for half in range(2):
                    act.wait_ge(sq_done, upto(sq_done, layer, sq + half))
                    nc.scalar.activation(junk[:, 0:512], bank[:, t + 4 * half, :], ACT.Square, scale=D ** -0.5,
                                         accum_out=sq_sum[:, half:half + 1]).then_inc(sq_done, 1)

            def act_halves(layer, n, t):
                act.wait_ge(h_turned, upto(h_turned, layer, n + 1))
                for k2 in range(2):
                    nc.scalar.activation(act_hi[:, 4 * k2:4 * k2 + 4, t * P:(t + 1) * P],
                                         bank[:, t + 4 * k2, :].rearrange("p (k c) -> p k c", k=4),
                                         ACT.Copy).then_inc(act_h, 1)

            act.wait_ge(const_loaded, 16 * (1 + T))
            with act.Fori(0, DEPTH) as l:
                for t in range(T):
                    if t:
                        square_pre(l, t, SQ_PRE1(t), lambda: act.wait_ge(rstd_step, upto(rstd_step, l, RS_PRE1(t - 1) + 1)))
                    else:
                        square_pre(l, t, SQ_PRE1(t), lambda: act.wait_ge(x_step, upto(x_step, l, 0)))
                    hi(l, t)
                    if t:
                        act_halves(l, t - 1, t - 1)
                act_halves(l, T - 1, T - 1)
                for blk in range(5):
                    for c in range(4 * blk + 4, 4 * blk + 8):
                        hi(l, c)
                    if blk == 2:
                        for t in range(T):
                            tile_done(act, l, t_done, 2, t, 11)
                            nc.scalar.activation(rv[:, t, :], bank[:, 4 + t, :], ACT.Copy).then_inc(rv_ready, 1)
                    if blk == 3:
                        for t in range(T):
                            tile_done(act, l, t_done, 3, t, 15)
                            if t:
                                act.wait_ge(sg_ready, upto(sg_ready, l, t))
                            nc.scalar.activation(th[:], bank[:, t, :], ACT.Tanh, scale=0.5).then_inc(th_ready, 1)
                    if blk == 4:
                        for t in range(T):
                            tile_done(act, l, t_done, 4, t, 19)
                            nc.scalar.activation(
                                VS[:, t, :, 0:DH], bank[:, 4 + t, 0:4 * DH].rearrange("p (a d) -> p a d", a=4),
                                ACT.Copy).then_inc(vg_act, 1)
                            nc.scalar.activation(gate[:, t, :], bank[:, 4 + t, 4 * DH:NTV], ACT.Tanh, scale=0.5)\
                                .then_inc(vg_act, 1)

                def turned_copies(n):
                    for m, dst in ((0, qT), (1, kT)):
                        act.wait_ge(qk_turned, upto(qk_turned, l, 2 * n + m + 1))
                        if n and m == 0:
                            act.wait_ge(ro_done, upto(ro_done, l, n))
                        nc.scalar.activation(dst[:].rearrange("p a c -> p (a c)"), bank[:, 2 + m, :], ACT.Copy)\
                            .then_inc(qk_copied, 1)

                def out_squares(n):
                    act.wait_ge(ro_done, upto(ro_done, l, n + 1))
                    if n:
                        act.wait_ge(head_sum, upto(head_sum, l, n))
                    nc.scalar.activation(osq[:], bank[:, 6, :], ACT.Square, scale=2.0 * DK ** -0.5).then_inc(osq_ready, 1)

                def z_round(s):
                    act.wait_ge(z_step, upto(z_step, l, 1 + 8 * (s + 1)))
                    if s:
                        chunk_used(act, l, C_W1K + 3)
                    nc.scalar.activation(z_hi[:], zf[:].rearrange("p m g c -> p (m g c)"), ACT.Copy)\
                        .then_inc(z_h, 1)

                def hidden(s):
                    for m in range(2):
                        if m == 0:
                            act.wait_ge(w1_done, upto(w1_done, l, s + 1))
                        else:
                            chunk_used(act, l, (C_W1K, C_W1V)[s] + 3)
                        nc.scalar.activation(hid[:, s, m, :], bank[:, m, 0:NKV * NCP],
                                             ACT.Gelu_apprx_tanh,
                                             bias=par[:, Q_B1 + 2 * s + m:Q_B1 + 2 * s + m + 1])\
                            .then_inc(hid_ready, 1)

                act.wait_ge(par_loaded, upto(par_loaded, l, 48))
                for what, n in MIDDLE:
                    if what == "chunk" and n + RING < C_F2 + 2:
                        hi(l, n + RING)
                    if what == "turn":
                        turned_copies(n)
                    if what == "out":
                        out_squares(n)
                    if what == "chunk" and n == C_F0:
                        z_round(0)
                    if what == "chunk" and n == C_W1K + 3:
                        hidden(0)
                        z_round(1)
                    if what == "chunk" and n == C_W1V + 3:
                        hidden(1)
                act.wait_ge(kc_done, upto(kc_done, l, 1))
                nc.scalar.activation(kcf[:], bank[0:DH, 6, 0:NKV * NCP], ACT.Identity,
                                     bias=par[0:DH, Q_B2K:Q_B2K + 1]).then_inc(kc_f, 1)
                act.wait_ge(kc_f, upto(kc_f, l, 1))
                for half in range(2):
                    nc.scalar.activation(KcH[half * DH:(half + 1) * DH, :], kcf[:], ACT.Copy).then_inc(kc_h, 1)
                act.wait_ge(vc_f, upto(vc_f, l, 1))
                nc.scalar.activation(VcS[:, :, 0:DH], vcf[:], ACT.Copy).then_inc(vc_h, 1)
                act.wait_ge(y_step, upto(y_step, l, 8))
                for f in range(2):
                    hi(l, C_F2 + f + 2)
                    chunk_used(act, l, C_F2 + f)
                    for g in range(NKV):
                        for half in range(2):
                            nc.scalar.activation(KH[half * DH:(half + 1) * DH, 2 * f + g, :],
                                                 bank[g * DH:(g + 1) * DH, 2 + f, :], ACT.Copy).then_inc(k_h, 1)
                for f in range(4):
                    hi(l, C_F2 + f + 4)
                    chunk_used(act, l, C_F2 + 2 + f)
                    for m in range(2):
                        nc.scalar.activation(QS[m * DH:(m + 1) * DH, 2 * f + m, :],
                                             bank[m * DH:(m + 1) * DH, f % 2, :], ACT.Copy).then_inc(q_h, 1)
                hi(l, C_WO + 2)
                hi(l, C_WO + 3)
                for n in range(T):
                    act.wait_ge(y_turned, upto(y_turned, l, n + 1))
                    nc.scalar.activation(act_hi[:, 0:4, n * P:(n + 1) * P],
                                         bank[:, n, :].rearrange("p (k c) -> p k c", k=4), ACT.Copy)\
                        .then_inc(y_h, 1)

                act.wait_ge(c_step, upto(c_step, l, 4))
                nc.scalar.activation(cE[:], cE[:], ACT.Exp, scale=SM).then_inc(c_exp, 1)

                def exps(n, heads):
                    i = UNITS[n][0]
                    for r in heads:
                        act.wait_ge(m_step, upto(m_step, l, 2 * n + 2))
                        if n >= 2:
                            act.wait_ge(pt_done, upto(pt_done, l, items_of(n - 2)[-1] + 1))
                            act.wait_ge(r_step, upto(r_step, l, 3 * (n - 2) + 1))
                        nc.scalar.activation(E[:, n % 2, r, 0:P * (i + 1)], bank[:, r, 0:P * (i + 1)],
                                             ACT.Exp, bias=s_bias[:, n % 2, r:r + 1], scale=SM,
                                             accum_out=s_sum[:, n % 2, r:r + 1]).then_inc(e_done, 1)

                def p_round(k):
                    rows = NCP if ITEMS[k][0] is None else P
                    act.wait_ge(pt_done, upto(pt_done, l, k + 1))
                    if k >= 2:
                        act.wait_ge(pv_done, upto(pv_done, l, k - 1))
                    nc.scalar.activation(pt_h[0:rows, k % 2, :], bank[0:rows, 4 + k % 2, :], ACT.Copy)\
                        .then_inc(pth, 1)

                def out_first(v):
                    act.wait_ge(pv_done, upto(pv_done, l, LAST_OF_V[v] + 1))
                    if v:
                        act.wait_ge(of_done, upto(of_done, l, 2 * v))
                    nc.scalar.activation(o_a[:], bank[0:DH, 6 + v % 2, :], ACT.Copy).then_inc(oa_done, 1)

                def out_round(v):
                    i, g = v // NKV, v % NKV
                    for m in range(2):
                        act.wait_ge(of_done, upto(of_done, l, 2 * v + m + 1))
                        nc.scalar.activation(
                            act_hi[m * DH:(m + 1) * DH, 4 + 2 * g:6 + 2 * g, i * P:(i + 1) * P],
                            o_f[m * DH:(m + 1) * DH, :, :], ACT.Copy).then_inc(oh_done, 1)

                exps(0, range(G))
                for n in range(NU):
                    ks = items_of(n)
                    done = 0
                    for m, k in enumerate(ks):
                        p_round(k)
                        if n + 1 < NU:
                            goal = G * (m + 1) // len(ks)
                            exps(n + 1, range(done, goal))
                            done = goal
                        if k - 2 in LAST_OF_V.values() and k >= 2:
                            out_first(ITEMS[k - 2][1])
                        if k - 3 in LAST_OF_V.values() and k >= 3:
                            out_round(ITEMS[k - 3][1])
                out_first(T * NKV - 1)
                out_round(T * NKV - 1)

                for c in range(C_WO + RING, C_UP + 3):
                    hi(l, c)
                for t in range(T):
                    tile_done(act, l, wo_done, 1, t, C_WO + 7)
                    square_post(l, t, SQ_POST1(t),
                                (lambda: act.wait_ge(rstd_step, upto(rstd_step, l, RS_PRE2(t - 1) + 1))) if t else
                                (lambda: act.wait_ge(rstd_step, upto(rstd_step, l, RS_PRE1(3) + 1))))
                    act.wait_ge(x_step, upto(x_step, l, 3 * t + 3))
                    square_pre(l, t, SQ_PRE2(t), lambda: act.wait_ge(rstd_step, upto(rstd_step, l, RS_POST1(t) + 1)))
                    if t:
                        act_halves(l, 4 + t - 1, t - 1)
                act_halves(l, 4 + T - 1, T - 1)
                hi(l, C_UP + 3)

                def conv_first(it, p, s):
                    act.wait_ge(w_used, l * NCH + it * RING + (C_UP + 2 * p + s + 1 + RING))
                    act.wait_ge(g_ready, l * KF + it * 2 + 1)
                    col = it * 2 + (s * KF + p)
                    w2 = par[:, Q_CV:Q_CV + 8 * KF].rearrange("p (n q) -> p n q", q=4)
                    nc.scalar.activation(cv[:, p, s, :], bank[:, 2 * p + s, :], ACT.Identity,
                                         bias=w2[:, bass.ds(col, 1), 3], scale=w2[:, bass.ds(col, 1), 2])\
                        .then_inc(cv0, 1)

                def gelu(it, p):
                    act.wait_ge(cv_step, l * (4 * KF) + it * 8 + (4 * p + 2 + AHEAD))
                    nc.scalar.activation(cv[:, p, 0, :], cv[:, p, 0, :], ACT.Gelu_apprx_tanh)\
                        .then_inc(gelu_done, 1)

                with act.Fori(0, KF // 2) as it:
                    for p in range(2):
                        for s in range(2):
                            conv_first(it, p, s)
                            hi_quad(l, it + (C_UP // RING + 1), 2 * p + s)
                        gelu(it, p)
                for k in range(KF):
                    if k >= KD:
                        act.wait_ge(w_used, upto(w_used, l, C_DN + k - KD + 1))
                    else:
                        act.wait_ge(w_used, upto(w_used, l, C_DN))
                    act.wait_ge(g_ready, upto(g_ready, l, k + 1))
                    nc.scalar.activation(act_hi[:, k % KD, :], gff[:, k, :], ACT.Copy).then_inc(gh, 1)
                    if C_DN + k + RING - 3 < NCH and k >= 3:
                        hi(l, C_DN + k + RING - 3)
                for t in range(T):
                    tile_done(act, l, dn_done, 0, t, NCH - 1)
                    square_post(l, t, SQ_POST2(t),
                                (lambda: act.wait_ge(rstd_step, upto(rstd_step, l, RS_POST2(t - 1) + 1))) if t else
                                (lambda: act.wait_ge(rstd_step, upto(rstd_step, l, RS_PRE2(3) + 1))))

        @block.vector
        def _(dve):
            def minus(out, a, b):
                return nc.vector.tensor_tensor(out, a, b, ALU.subtract)

            def normalise(layer, n, t, gain, rs):
                if n % 4 >= 2:
                    dve.wait_ge(h_turned, upto(h_turned, layer, n - 1))
                dve.wait_ge(rstd_step, upto(rstd_step, layer, rs + 2))
                nc.vector.scalar_tensor_tensor(out=h[:, t % 2, :], in0=x[:, t, :], scalar=rstd[:, 0:1],
                                               in1=gain, op0=ALU.mult, op1=ALU.mult).then_inc(h_ready, 1)

            def act_rests(layer, n, t):
                for k2 in range(2):
                    dve.wait_ge(act_h, upto(act_h, layer, 2 * n + k2 + 1))
                    minus(act_lo[:, 4 * k2:4 * k2 + 4, t * P:(t + 1) * P],
                          bank[:, t + 4 * k2, :].rearrange("p (k c) -> p k c", k=4),
                          r32(act_hi[:, 4 * k2:4 * k2 + 4, t * P:(t + 1) * P])).then_inc(act_l, 1)

            def add_branch(layer, base, t, gain, rs, slot):
                dve.wait_ge(rstd_step, upto(rstd_step, layer, rs + 3))
                for half in range(2):
                    cols = slice(512 * half, 512 * half + 512)
                    nc.vector.scalar_tensor_tensor(out=h[:, slot, cols], in0=bank[:, t + 4 * half, :],
                                                   scalar=rstd[:, 0:1], in1=gain[:, cols],
                                                   op0=ALU.mult, op1=ALU.mult).then_inc(x_step, 1)
                dve.wait_ge(x_step, upto(x_step, layer, base + 2))
                nc.vector.tensor_tensor(x[:, t, :], x[:, t, :], h[:, slot, :], ALU.add).then_inc(x_step, 1)

            dve.sem_inc(cv_step, AHEAD)
            for s in (x_step, rot_step, h_ready, g_ready):
                dve.sem_inc(s, 1)
            dve.wait_ge(const_loaded, 16 * (1 + T))
            nc.vector.tensor_copy(ident_b[:], ident).then_inc(const_cast, 1)
            nc.vector.tensor_copy(causal_b[:], const[:, O_CA:O_CM]).then_inc(const_cast, 1)
            nc.vector.tensor_copy(cmask_b[:], const[:, O_CM:NCONST]).then_inc(const_cast, 1)

            with dve.Fori(0, DEPTH) as l:
                dve.wait_ge(mixpre_loaded, upto(mixpre_loaded, l, 16))
                dve.wait_ge(x_step, upto(x_step, l, 0))
                for t in range(T):
                    normalise(l, t, t, g_mix_pre[:], RS_PRE1(t))
                    if t:
                        act_rests(l, t - 1, t - 1)
                act_rests(l, T - 1, T - 1)

                def rotate(m, dst, t, b):
                    at = 16 * m + 4 * t
                    src = bank[:, b, :].rearrange("p (h a f) -> p h a f", h=RH, a=2)
                    tmp = rtmp[:].rearrange("p (h a f) -> p h a f", h=RH, a=2)
                    wide = lambda tab: tab[:, t, :].unsqueeze(1).broadcast_to([P, RH, DK // 2])
                    tile_done(dve, l, t_done, m, t, 4 * m + 3)
                    nc.vector.tensor_tensor(
                        dst[:, t, :].rearrange("p (h f) -> p h f", f=DK // 2),
                        bank[:, b, :].rearrange("p (h f) -> p h f", f=DK // 2),
                        cos[:, t, :].unsqueeze(1).broadcast_to([P, 2 * RH, DK // 2]), ALU.mult)\
                        .then_inc(rot_step, 1)
                    dve.wait_ge(rot_step, upto(rot_step, l, at))
                    nc.vector.tensor_tensor(tmp[:, :, 0, :], src[:, :, 1, :], wide(nsin), ALU.mult)\
                        .then_inc(rot_step, 1)
                    nc.vector.tensor_tensor(tmp[:, :, 1, :], src[:, :, 0, :], wide(sin), ALU.mult)\
                        .then_inc(rot_step, 1)
                    dve.wait_ge(rot_step, upto(rot_step, l, at + 3))
                    nc.vector.tensor_tensor(dst[:, t, :], dst[:, t, :], rtmp[:], ALU.add).then_inc(rot_step, 1)

                for t in range(T):
                    rotate(0, qr, t, 4 + t)
                for t in range(T):
                    rotate(1, kr, t, t)
                for t in range(T):
                    dve.wait_ge(th_ready, upto(th_ready, l, t + 1))
                    nc.vector.scalar_tensor_tensor(out=sg[:, t, :], in0=th[:], scalar=1.0, in1=bank[:, t, :],
                                                   op0=ALU.add, op1=ALU.mult).then_inc(sg_ready, 1)
                for t in range(T):
                    dve.wait_ge(vg_act, upto(vg_act, l, 2 * t + 2))
                    minus(VS[:, t, :, DH:2 * DH], bank[:, 4 + t, 0:4 * DH].rearrange("p (a d) -> p a d", a=4),
                          r32(VS[:, t, :, 0:DH])).then_inc(vg_dve, 1)
                    nc.vector.tensor_scalar(gate[:, t, :], gate[:, t, :], 0.5, 0.5, ALU.mult, ALU.add)\
                        .then_inc(vg_dve, 1)

                def turned(n):
                    dve.wait_ge(qk_copied, upto(qk_copied, l, 2 * n + 1))
                    if n:
                        dve.wait_ge(ro_done, upto(ro_done, l, n))
                    nc.vector.tensor_tensor(qxT[:], bank[:, 2, :].rearrange("p (a c) -> p a c", a=4), xi,
                                            ALU.mult).then_inc(qx_ready, 1)
                    if n < T - 1:
                        if n:
                            dve.wait_ge(kv_done, upto(kv_done, l, n))
                        else:
                            dve.wait_ge(rv_ready, upto(rv_ready, l, 4))
                        nc.vector.tensor_tensor(vz[:].rearrange("p (h e) -> p h e", h=RH),
                                                rv[:, n, :].rearrange("p (h e) -> p h e", h=RH),
                                                zeta.unsqueeze(2).broadcast_to([P, RH, DK]), ALU.mult)\
                            .then_inc(vz_ready, 1)

                def mask_scores(n):
                    if n:
                        dve.wait_ge(ro_done, upto(ro_done, l, n))
                    for a in range(2):
                        dve.wait_ge(st_done, upto(st_done, l, 2 * n + a + 1))
                        nc.vector.tensor_tensor(stm[:, a:RH:2, :],
                                                bank[:, 4 + a, :].rearrange("p (h c) -> p h c", h=4),
                                                dmask[:, a:RH:2, :], ALU.mult).then_inc(st_masked, 1)

                def states(n):
                    if n == T - 1:
                        return
                    dve.wait_ge(kv_done, upto(kv_done, l, n + 1))
                    kv = bank[:, 7, :].rearrange("p (a c) -> p a c", a=4)
                    bd = bdiag.unsqueeze(1).broadcast_to([P, 4, P])
                    if n == 0:
                        nc.vector.tensor_tensor(state[:], kv, bd, ALU.mult).then_inc(state_step, 1)
                        return
                    at = 3 * n - 2
                    dve.wait_ge(state_step, upto(state_step, l, at))
                    nc.vector.tensor_tensor(kvt[:], kv, bd, ALU.mult).then_inc(state_step, 1)
                    dve.wait_ge(ro_done, upto(ro_done, l, n + 1))
                    nc.vector.tensor_tensor(state[:], state[:], decay.unsqueeze(2).broadcast_to([P, 4, P]),
                                            ALU.mult).then_inc(state_step, 1)
                    dve.wait_ge(state_step, upto(state_step, l, at + 2))
                    nc.vector.tensor_tensor(state[:], state[:], kvt[:], ALU.add).then_inc(state_step, 1)

                def head_norms(n):
                    dve.wait_ge(osq_ready, upto(osq_ready, l, n + 1))
                    if n:
                        dve.wait_ge(rstd_step, upto(rstd_step, l, RS_RET(n - 1) + 1))
                    nc.vector.reduce_sum(head_ms[:], osq[:].rearrange("p (h e) -> p h e", h=RH), AXX)\
                        .then_inc(head_sum, 1)

                def outputs(n):
                    dve.wait_ge(rstd_step, upto(rstd_step, l, RS_RET(n) + 2))
                    y = qr[:, n, :].rearrange("p (h e) -> p h e", h=RH)
                    nc.vector.tensor_tensor(y, bank[:, 6, :].rearrange("p (h e) -> p h e", h=RH),
                                            rstd[:].unsqueeze(2).broadcast_to([P, RH, DK]), ALU.mult)\
                        .then_inc(y_step, 1)
                    dve.wait_ge(y_step, upto(y_step, l, 2 * n + 1))
                    nc.vector.tensor_tensor(qr[:, n, :], qr[:, n, :], sg[:, n, :], ALU.mult).then_inc(y_step, 1)

                def z_build(s):
                    if s == 0:
                        nc.vector.memset(zf[:, :, :, NC:NCP], 0.0).then_inc(z_step, 1)
                    else:
                        dve.wait_ge(z_l, upto(z_l, l, 1))
                    chunk_used(dve, l, C_F0 + s)
                    for half in range(2):
                        rows = slice(half * DH, (half + 1) * DH)
                        for g in range(NKV):
                            src = bank[g * DH:(g + 1) * DH, s, :].rearrange("p (c m a) -> p m a c", m=8, a=2)
                            for m8 in range(2):
                                pos = par[rows, Q_POS + 16 * s + 8 * m8:Q_POS + 16 * s + 8 * m8 + 8]
                                nc.vector.tensor_tensor(
                                    zf[rows, 8 * m8:8 * m8 + 8, g, 0:NC], src[:, :, half, m8:m8 + NC],
                                    pos.unsqueeze(2).broadcast_to([DH, 8, NC]), ALU.add).then_inc(z_step, 1)

                def z_rest(s):
                    dve.wait_ge(z_step, upto(z_step, l, 1 + 8 * (s + 1)))
                    dve.wait_ge(z_h, upto(z_h, l, s + 1))
                    minus(z_lo[:], zf[:].rearrange("p m g c -> p (m g c)"), r32(z_hi[:])).then_inc(z_l, 1)

                dve.wait_ge(par_loaded, upto(par_loaded, l, 48))
                for what, n in MIDDLE:
                    if what == "turn":
                        turned(n)
                    if what == "score":
                        mask_scores(n)
                    if what == "out":
                        states(n)
                        head_norms(n)
                    if what == "norm":
                        outputs(n)
                    if what == "chunk" and n == C_F0:
                        z_build(0)
                        z_rest(0)
                    if what == "chunk" and n == C_F1:
                        z_build(1)
                    if what == "chunk" and n == C_W1K + 3:
                        z_rest(1)
                dve.wait_ge(vc_done, upto(vc_done, l, 1))
                nc.vector.tensor_tensor(vcf[:], bank[0:NCP, 7, 0:NKV * DH].rearrange("p (g d) -> p g d", g=NKV),
                                        b2v[:].unsqueeze(1).broadcast_to([NCP, NKV, DH]), ALU.add)\
                    .then_inc(vc_f, 1)
                dve.wait_ge(kc_h, upto(kc_h, l, 2))
                for half in range(2):
                    minus(KcL[half * DH:(half + 1) * DH, :], kcf[:], r32(KcH[0:DH, :])).then_inc(kc_l, 1)
                dve.wait_ge(vc_h, upto(vc_h, l, 1))
                minus(VcS[:, :, DH:2 * DH], vcf[:], r32(VcS[:, :, 0:DH])).then_inc(vc_l, 1)
                for f in range(2):
                    for g in range(NKV):
                        for half in range(2):
                            if g + half == 0:
                                dve.wait_ge(k_h, upto(k_h, l, 4 * (f + 1)))
                            rows = slice(half * DH, (half + 1) * DH)
                            minus(KL[rows, 2 * f + g, :], bank[g * DH:(g + 1) * DH, 2 + f, :],
                                  r32(KH[rows, 2 * f + g, :])).then_inc(k_l, 1)
                for f in range(4):
                    for m in range(2):
                        if m == 0:
                            dve.wait_ge(q_h, upto(q_h, l, 2 * (f + 1)))
                        minus(QS[(1 - m) * DH:(2 - m) * DH, 2 * f + m, :], bank[m * DH:(m + 1) * DH, f % 2, :],
                              r32(QS[m * DH:(m + 1) * DH, 2 * f + m, :])).then_inc(q_l, 1)
                for n in range(T):
                    dve.wait_ge(y_h, upto(y_h, l, n + 1))
                    minus(act_lo[:, 0:4, n * P:(n + 1) * P], bank[:, n, :].rearrange("p (k c) -> p k c", k=4),
                          r32(act_hi[:, 0:4, n * P:(n + 1) * P])).then_inc(y_l, 1)

                NR = T * NKV * G
                for a in range(2):
                    dve.wait_ge(cs_done, upto(cs_done, l, a + 1))
                    nc.vector.reduce_max(c_stat[:, a * 16:a * 16 + 16],
                                         bank[:, 4 + a, :].rearrange("p (r c) -> p r c", c=NCP), AXX)\
                        .then_inc(c_step, 1)
                dve.wait_ge(c_step, upto(c_step, l, 2))
                nc.vector.tensor_scalar(c_stat[:], c_stat[:], NEG_GUARD, None, ALU.max).then_inc(c_step, 1)
                dve.wait_ge(c_step, upto(c_step, l, 3))
                for a in range(2):
                    last = nc.vector.tensor_tensor(
                        cE[:, a * 16:a * 16 + 16, :], bank[:, 4 + a, :].rearrange("p (r c) -> p r c", c=NCP),
                        c_stat[:, a * 16:a * 16 + 16].unsqueeze(2).broadcast_to([P, 16, NCP]), ALU.subtract)
                last.then_inc(c_step, 1)
                dve.wait_ge(c_exp, upto(c_exp, l, 1))
                nc.vector.reduce_sum(c_rec[:], cE[:], AXX).then_inc(c_step, 1)
                dve.wait_ge(c_step, upto(c_step, l, 5))
                nc.vector.tensor_scalar(c_rec[:], c_rec[:], 1e-30, None, ALU.max).then_inc(c_step, 1)
                dve.wait_ge(c_step, upto(c_step, l, 6))
                nc.vector.reciprocal(c_rec[:], c_rec[:]).then_inc(c_step, 1)
                dve.wait_ge(c_step, upto(c_step, l, 7))
                nc.vector.tensor_tensor(c_rec[:].rearrange("p (t h) -> p t h", t=T),
                                        c_rec[:].rearrange("p (t h) -> p t h", t=T),
                                        gate[:].rearrange("p t (h b) -> p t h b", b=3)[:, :, :, 0], ALU.mult)\
                    .then_inc(c_step, 1)
                dve.wait_ge(c_step, upto(c_step, l, 8))
                nc.vector.tensor_tensor(cE[:], cE[:], c_rec[:].unsqueeze(2).broadcast_to([P, NR, NCP]),
                                        ALU.mult).then_inc(c_step, 1)

                def maxima(n):
                    i = UNITS[n][0]
                    dve.wait_ge(s_done, upto(s_done, l, n + 1))
                    nc.vector.reduce_max(s_max[:, n % 2, :], bank[:, 0:G, 0:P * (i + 1)], AXX)\
                        .then_inc(m_step, 1)
                    dve.wait_ge(m_step, upto(m_step, l, 2 * n + 1))
                    if n >= 2:
                        dve.wait_ge(e_done, upto(e_done, l, G * (n - 1)))
                    nc.vector.tensor_scalar(s_bias[:, n % 2, :], s_max[:, n % 2, :], NEG_GUARD, -SM,
                                            ALU.max, ALU.mult).then_inc(m_step, 1)

                def factors(n):
                    i, g, b = UNITS[n]
                    dve.wait_ge(e_done, upto(e_done, l, G * (n + 1)))
                    if n >= 2:
                        dve.wait_ge(p_scaled, upto(p_scaled, l, G * (n - 1)))
                    rec = s_rec[:, n % 2, :]
                    nc.vector.tensor_scalar(rec, s_sum[:, n % 2, :], 1e-30, None, ALU.max).then_inc(r_step, 1)
                    dve.wait_ge(r_step, upto(r_step, l, 3 * n + 1))
                    nc.vector.reciprocal(rec, rec).then_inc(r_step, 1)
                    dve.wait_ge(r_step, upto(r_step, l, 3 * n + 2))
                    gs = gate[:, i, :].rearrange("p (h b) -> p h b", b=3)[:, G * g:G * g + G, b + 1]
                    nc.vector.tensor_tensor(rec, rec, gs, ALU.mult).then_inc(r_step, 1)
                    dve.wait_ge(r_step, upto(r_step, l, 3 * n + 3))
                    for r in range(G):
                        e = E[:, n % 2, r, 0:P * (i + 1)]
                        nc.vector.tensor_scalar(e, e, s_rec[:, n % 2, r:r + 1], None, ALU.mult)\
                            .then_inc(p_scaled, 1)

                def p_rest(k):
                    rows = NCP if ITEMS[k][0] is None else P
                    dve.wait_ge(pth, upto(pth, l, k + 1))
                    minus(pt_l[0:rows, k % 2, :], bank[0:rows, 4 + k % 2, :], r32(pt_h[0:rows, k % 2, :]))\
                        .then_inc(ptl, 1)

                def out_sum(v):
                    i, g = v // NKV, v % NKV
                    dve.wait_ge(oa_done, upto(oa_done, l, v + 1))
                    if v:
                        dve.wait_ge(ol_done, upto(ol_done, l, 2 * v))
                        dve.wait_ge(oh_done, upto(oh_done, l, 2 * v))
                    for m in range(2):
                        view = lambda ap: ap.rearrange("p (a b c) -> p a b c", a=2, b=2)[:, :, m, :]
                        nc.vector.tensor_tensor(o_f[m * DH:(m + 1) * DH, :, :],
                                                view(bank[DH:P, 6 + v % 2, :]), view(o_a[:]), ALU.add)\
                            .then_inc(of_done, 1)

                def out_rest(v):
                    i, g = v // NKV, v % NKV
                    for m in range(2):
                        rows = slice(m * DH, (m + 1) * DH)
                        dst = (rows, slice(4 + 2 * g, 6 + 2 * g), slice(i * P, (i + 1) * P))
                        dve.wait_ge(oh_done, upto(oh_done, l, 2 * v + m + 1))
                        minus(act_lo[dst], o_f[rows, :, :], r32(act_hi[dst])).then_inc(ol_done, 1)

                maxima(0)
                factors(0)
                for n in range(NU):
                    if n + 1 < NU:
                        maxima(n + 1)
                    for k in items_of(n):
                        p_rest(k)
                        if k - 2 in LAST_OF_V.values() and k >= 2:
                            out_sum(ITEMS[k - 2][1])
                        if k - 3 in LAST_OF_V.values() and k >= 3:
                            out_rest(ITEMS[k - 3][1])
                    if n + 1 < NU:
                        factors(n + 1)
                out_sum(T * NKV - 1)
                out_rest(T * NKV - 1)

                for t in range(T):
                    if t >= 1:
                        dve.wait_ge(h_turned, upto(h_turned, l, 4 + t))
                    add_branch(l, 3 * t, t, g_rest[:, 0, :], RS_POST1(t), (t + 1) % 2)
                    if t:
                        dve.wait_ge(x_step, upto(x_step, l, 3 * t + 3))
                    else:
                        dve.wait_ge(x_step, upto(x_step, l, 3))
                    dve.wait_ge(rstd_step, upto(rstd_step, l, RS_PRE2(t) + 2))
                    nc.vector.scalar_tensor_tensor(out=h[:, t % 2, :], in0=x[:, t, :], scalar=rstd[:, 0:1],
                                                   in1=g_rest[:, 1, :], op0=ALU.mult, op1=ALU.mult)\
                        .then_inc(h_ready, 1)
                    if t:
                        act_rests(l, 4 + t - 1, t - 1)
                act_rests(l, 4 + T - 1, T - 1)

                taps = par[:, Q_CV:Q_CV + 8 * KF].rearrange("p (n q) -> p n q", q=4)
                with dve.Fori(0, KF // 2) as it:
                    for p in range(2):
                        for s in range(2):
                            col = it * 2 + (s * KF + p)
                            y = cv[:, p, s, :]
                            u = bank[:, 2 * p + s, :]
                            dve.wait_ge(cv0, l * (2 * KF) + it * 4 + (2 * p + s + 1))
                            nc.vector.scalar_tensor_tensor(
                                out=y[:, 1:SEQ], in0=u[:, 0:SEQ - 1], scalar=taps[:, bass.ds(col, 1), 1],
                                in1=y[:, 1:SEQ], op0=ALU.mult, op1=ALU.add).then_inc(cv_step, 1)
                            dve.wait_ge(cv_step, l * (4 * KF) + it * 8 + (4 * p + 2 * s + 1 + AHEAD))
                            nc.vector.scalar_tensor_tensor(
                                out=y[:, 2:SEQ], in0=u[:, 0:SEQ - 2], scalar=taps[:, bass.ds(col, 1), 0],
                                in1=y[:, 2:SEQ], op0=ALU.mult, op1=ALU.add).then_inc(cv_step, 1)
                        dve.wait_ge(cv_step, l * (4 * KF) + it * 8 + (4 * p + 4 + AHEAD))
                        dve.wait_ge(gelu_done, l * KF + it * 2 + (p + 1))
                        nc.vector.tensor_tensor(gff[:, bass.ds(it * 2 + p, 1), :].rearrange("p a c -> p (a c)"),
                                                cv[:, p, 0, :], cv[:, p, 1, :], ALU.mult).then_inc(g_ready, 1)
                for k in range(KF):
                    dve.wait_ge(gh, upto(gh, l, k + 1))
                    minus(act_lo[:, k % KD, :], gff[:, k, :], r32(act_hi[:, k % KD, :])).then_inc(gl, 1)
                for t in range(T):
                    if t:
                        dve.wait_ge(x_step, upto(x_step, l, 12 + 3 * t))
                    add_branch(l, 12 + 3 * t, t, g_rest[:, 2, :], RS_POST2(t), t % 2)

        @block.tensor
        def _(pe):
            mm = nc.tensor.matmul

            def arrived(layer, c):
                pe.wait_ge(lo_ready, upto(lo_ready, layer, c + 1))

            def passes(a, b):
                return ((a[0], b[0]), (a[0], b[1]), (a[1], b[0]))

            def turn_h(layer, n, t):
                pe.wait_ge(h_ready, upto(h_ready, layer, n + 1))
                for k in range(KD):
                    last = nc.tensor.transpose(bank[:, t + 4 * (k // 4), (k % 4) * P:(k % 4 + 1) * P],
                                               h[:, t % 2, k * P:(k + 1) * P], ident)
                last.then_inc(h_turned, 1)

            def token_block(layer, first, width, b0, done, before):
                for c in range(4):
                    arrived(layer, first + c)
                    for t in range(T):
                        if c == 0:
                            before(t)
                        for kk in range(2):
                            k = 2 * c + kk
                            s = (first + c) % RING
                            cols = slice(kk * width, (kk + 1) * width)
                            rows = (act_hi[:, k, t * P:(t + 1) * P], act_lo[:, k, t * P:(t + 1) * P])
                            w = (w_hi[:, s, cols], w_lo[:, s, cols])
                            for n, (a, b) in enumerate(passes(rows, w)):
                                last = mm(bank[:, b0 + t, 0:width], a, b, start=(k == 0 and n == 0),
                                          stop=(k == KD - 1 and n == 2))
                        if t == T - 1:
                            last.then_inc(w_used, 1)
                        elif c == 3:
                            last.then_inc(done, 1)

            def feature_tile(layer, c, b):
                s = c % RING
                arrived(layer, c)
                for k in range(KD):
                    cols = slice(k * P, (k + 1) * P)
                    for n, (a, v) in enumerate(passes((w_hi[:, s, cols], w_lo[:, s, cols]),
                                                      (act_hi[:, k, :], act_lo[:, k, :]))):
                        last = mm(bank[:, b, :], a, v, start=(k == 0 and n == 0), stop=(k == KD - 1 and n == 2))
                last.then_inc(w_used, 1)

            pe.sem_inc(w_used, RING)
            pe.wait_ge(const_loaded, 16 * (1 + T))
            pe.wait_ge(const_cast, 3)
            with pe.Fori(0, DEPTH) as l:
                pe.wait_ge(x_step, upto(x_step, l, 0))
                for t in range(T):
                    turn_h(l, t, t)
                def before_t(blk):
                    def f(t):
                        if blk == 0:
                            pe.wait_ge(act_l, upto(act_l, l, 2 * t + 2))
                        if blk == 1:
                            pe.wait_ge(act_l, upto(act_l, l, 8))
                        if blk == 2:
                            pe.wait_ge(rot_step, upto(rot_step, l, 4 * t + 3))
                        if blk == 3:
                            pe.wait_ge(rot_step, upto(rot_step, l, 16 + 4 * t + 3))
                        if blk == 4:
                            pe.wait_ge(rv_ready, upto(rv_ready, l, t + 1))
                    return f
                for blk in range(4):
                    token_block(l, C_T + 4 * blk, 512, 4 if blk % 2 == 0 else 0, t_done, before_t(blk))
                token_block(l, C_TV, NTV, 4, t_done, before_t(4))

                def turn_qk(n):
                    pe.wait_ge(sg_ready, upto(sg_ready, l, 4))
                    if n:
                        pe.wait_ge(qk_copied, upto(qk_copied, l, 2 * n))
                        pe.wait_ge(qx_ready, upto(qx_ready, l, n))
                    else:
                        pe.wait_ge(rot_step, upto(rot_step, l, 32))
                    for m, src in ((0, qr), (1, kr)):
                        for a in range(4):
                            last = nc.tensor.transpose(bank[:, 2 + m, a * P:(a + 1) * P],
                                                       src[:, n, a * P:(a + 1) * P], ident)
                        last.then_inc(qk_turned, 1)

                def scores(n):
                    pe.wait_ge(qk_copied, upto(qk_copied, l, 2 * n + 2))
                    if n:
                        pe.wait_ge(st_masked, upto(st_masked, l, 2 * n))
                    else:
                        pe.wait_ge(vg_dve, upto(vg_dve, l, 8))
                    for hd in range(RH):
                        rows = slice((hd % 2) * DK, (hd % 2 + 1) * DK)
                        last = mm(bank[:, 4 + hd % 2, (hd // 2) * P:(hd // 2 + 1) * P],
                                  kT[rows, hd // 2, :], qT[rows, hd // 2, :], start=True, stop=True)
                        if hd >= RH - 2:
                            last.then_inc(st_done, 1)

                def ret_out(n):
                    if n:
                        pe.wait_ge(state_step, upto(state_step, l, 3 * n - 2))
                    if n < T - 1:
                        pe.wait_ge(vz_ready, upto(vz_ready, l, n + 1))
                        for a in range(4):
                            last = mm(bank[:, 7, a * P:(a + 1) * P], kr[:, n, a * P:(a + 1) * P],
                                      vz[:, a * P:(a + 1) * P], start=True, stop=True)
                        last.then_inc(kv_done, 1)
                    pe.wait_ge(rv_ready, upto(rv_ready, l, n + 1))
                    pe.wait_ge(st_masked, upto(st_masked, l, 2 * n + 2))
                    pe.wait_ge(qx_ready, upto(qx_ready, l, n + 1))
                    if n:
                        pe.wait_ge(y_step, upto(y_step, l, 2 * n - 1))
                    for a in range(4):
                        if n:
                            mm(bank[:, 6, a * P:(a + 1) * P], qxT[:, a, :], state[:, a, :], start=True,
                               stop=False, skip_group_check=True)
                        for m in range(2):
                            hd = 2 * a + m
                            last = mm(bank[:, 6, hd * DK:(hd + 1) * DK], stm[:, hd, :],
                                      rv[:, n, hd * DK:(hd + 1) * DK], start=(n == 0), stop=True,
                                      skip_group_check=True)
                    last.then_inc(ro_done, 1)

                def first_layer(s, c):
                    j = c - (C_W1K, C_W1V)[s]
                    arrived(l, c)
                    if j == 0:
                        pe.wait_ge(z_l, upto(z_l, l, s + 1))
                        if s == 0:
                            pe.wait_ge(z_step, upto(z_step, l, 17))
                        else:
                            pe.wait_ge(hid_ready, upto(hid_ready, l, 2))
                    for m in range(2):
                        for kk in range(4):
                            k = 4 * j + kk
                            cols = slice(kk * HID + m * P, kk * HID + (m + 1) * P)
                            zc = slice(k * NKV * NCP, (k + 1) * NKV * NCP)
                            for n, (a, v) in enumerate(passes((w_hi[:, c % RING, cols], w_lo[:, c % RING, cols]),
                                                              (z_hi[:, zc], z_lo[:, zc]))):
                                last = mm(bank[:, m, 0:NKV * NCP], a, v,
                                          start=(k == 0 and n == 0), stop=(k == 15 and n == 2))
                        if j == 3 and m == 0:
                            last.then_inc(w1_done, 1)
                    last.then_inc(w_used, 1)

                for what, n in MIDDLE:
                    if what == "turn":
                        turn_qk(n)
                    if what == "score":
                        scores(n)
                    if what == "out":
                        ret_out(n)
                    if what == "chunk":
                        if n <= C_F1:
                            feature_tile(l, n, n - C_F0)
                        elif n < C_W1V:
                            first_layer(0, n)
                        else:
                            first_layer(1, n)
                pe.wait_ge(par_loaded, upto(par_loaded, l, 48))
                pe.wait_ge(hid_ready, upto(hid_ready, l, 4))
                pe.wait_ge(y_step, upto(y_step, l, 7))
                w2 = par[:, Q_W2:Q_B2K].rearrange("p (s m d) -> p s m d", s=2, m=2)
                for m in range(2):
                    last = mm(bank[0:DH, 6, 0:NKV * NCP], w2[:, 0, m, :], hid[:, 0, m, :], start=(m == 0), stop=(m == 1))
                last.then_inc(kc_done, 1)
                for g in range(NKV):
                    for m in range(2):
                        last = mm(bank[0:NCP, 7, g * DH:(g + 1) * DH], hid[:, 1, m, g * NCP:(g + 1) * NCP],
                                  w2[:, 1, m, :], start=(m == 0), stop=(m == 1))
                last.then_inc(vc_done, 1)
                for f in range(6):
                    if f < 2:
                        pe.wait_ge(qk_copied, upto(qk_copied, l, 8))
                        pe.wait_ge(qx_ready, upto(qx_ready, l, 4))
                    elif f < 4:
                        pe.wait_ge(hid_ready, upto(hid_ready, l, 4))
                    else:
                        pe.wait_ge(q_l, upto(q_l, l, 2 * (f - 3)))
                    feature_tile(l, C_F2 + f, 2 + f if f < 2 else f % 2)
                for n in range(T):
                    pe.wait_ge(y_step, upto(y_step, l, 2 * n + 2))
                    if n == 0:
                        pe.wait_ge(q_l, upto(q_l, l, 6))
                    if n == 1:
                        pe.wait_ge(q_l, upto(q_l, l, 8))
                        pe.wait_ge(k_l, upto(k_l, l, 8))
                    for a in range(4):
                        last = nc.tensor.transpose(bank[:, n, a * P:(a + 1) * P], qr[:, n, a * P:(a + 1) * P], ident)
                    last.then_inc(y_turned, 1)
                pe.wait_ge(kc_l, upto(kc_l, l, 2))
                pe.wait_ge(q_l, upto(q_l, l, 8))
                pe.wait_ge(st_masked, upto(st_masked, l, 8))
                for i in range(T):
                    for hd in range(NH):
                        g = hd // G
                        dst = bank[:, 4 + i // 2, ((i % 2) * NH + hd) * NCP:((i % 2) * NH + hd + 1) * NCP]
                        q = QS[:, hd, i * P:(i + 1) * P]
                        mm(dst, q, KcH[:, g * NCP:(g + 1) * NCP], start=True, stop=False)
                        mm(dst, q, KcL[:, g * NCP:(g + 1) * NCP], start=False, stop=False)
                        last = mm(dst, ident_b[:], cmask_b[:, i * NCP:(i + 1) * NCP], start=False, stop=True)
                    if i % 2:
                        last.then_inc(cs_done, 1)

                def unit_scores(n):
                    i, g, b = UNITS[n]
                    if n:
                        pe.wait_ge(e_done, upto(e_done, l, G * n))
                    else:
                        pe.wait_ge(y_l, upto(y_l, l, 4))
                        pe.wait_ge(k_l, upto(k_l, l, 8))
                    for r in range(G):
                        q = QS[:, G * g + r, i * P:(i + 1) * P]
                        dst = bank[:, r, 0:P * (i + 1)]
                        mm(bank[:, r, P * i:P * (i + 1)], ident_b[:], causal_b[:], start=True, stop=False,
                           skip_group_check=True)
                        mm(dst, q, KH[:, 2 * b + g, 0:P * (i + 1)], start=False, stop=False, skip_group_check=True)
                        last = mm(dst, q, KL[:, 2 * b + g, 0:P * (i + 1)], start=False, stop=True,
                                  skip_group_check=True)
                    last.then_inc(s_done, 1)

                def turn_p(k):
                    n, v, j = ITEMS[k]
                    if k >= 2:
                        pe.wait_ge(ptl, upto(ptl, l, k - 1))
                    else:
                        pe.wait_ge(c_step, upto(c_step, l, 9))
                    if n is None:
                        for r in range(G):
                            last = nc.tensor.transpose(bank[0:NCP, 4 + k % 2, r * P:(r + 1) * P],
                                                       cE[:, v * G + r, :], ident)
                    else:
                        for r in range(G):
                            if j == 0:
                                pe.wait_ge(p_scaled, upto(p_scaled, l, G * n + r + 1))
                            last = nc.tensor.transpose(bank[:, 4 + k % 2, r * P:(r + 1) * P],
                                                       E[:, n % 2, r, j * P:(j + 1) * P], ident)
                    last.then_inc(pt_done, 1)

                def product(k):
                    n, v, j = ITEMS[k]
                    first = n is None
                    o = bank[:, 6 + v % 2, :]
                    if first:
                        if v >= 2:
                            pe.wait_ge(of_done, upto(of_done, l, 2 * (v - 1)))
                        elif v == 1:
                            pe.wait_ge(vc_f, upto(vc_f, l, 1))
                        else:
                            pe.wait_ge(kc_f, upto(kc_f, l, 1))
                            pe.wait_ge(vc_l, upto(vc_l, l, 1))
                        g = v % NKV
                        w, rows = VcS[:, g, :], NCP
                    else:
                        i, g, b = UNITS[n]
                        w, rows = VS[:, j, 2 * b + g, :], P
                    pe.wait_ge(ptl, upto(ptl, l, k + 1))
                    mm(o, w, pt_h[0:rows, k % 2, :], start=first, stop=False)
                    mm(o, w, pt_l[0:rows, k % 2, :], start=False, stop=(k == LAST_OF_V[v])).then_inc(pv_done, 1)

                unit_scores(0)
                for n in range(NU):
                    if n + 1 < NU:
                        unit_scores(n + 1)
                    for k in items_of(n):
                        turn_p(k)
                        if k:
                            product(k - 1)
                product(NI - 1)

                for half in range(2):
                    def before(t, half=half):
                        if half == 0 and t == 0:
                            pe.wait_ge(ol_done, upto(ol_done, l, 2 * T * NKV))
                            pe.wait_ge(e_done, upto(e_done, l, G * NU))
                            pe.wait_ge(ptl, upto(ptl, l, NI))
                    token_block(l, C_WO + 4 * half, 512, 4 * half, wo_done, before)
                for t in range(T):
                    pe.wait_ge(x_step, upto(x_step, l, 3 * t + 2))
                    turn_h(l, 4 + t, t)
                with pe.Fori(0, KF // 2) as it:
                    for s in range(RING):
                        pe.wait_ge(act_l, upto(act_l, l, 16))
                        pe.wait_ge(lo_ready, l * NCH + it * RING + (C_UP + s + 1 + RING))
                        pe.wait_ge(cv_step, l * (4 * KF) + it * 8 + (2 * s + 2))
                        for k in range(KD):
                            cols = slice(k * P, (k + 1) * P)
                            for n, (a, v) in enumerate(passes((w_hi[:, s, cols], w_lo[:, s, cols]),
                                                              (act_hi[:, k, :], act_lo[:, k, :]))):
                                last = mm(bank[:, s, :], a, v, start=(k == 0 and n == 0),
                                          stop=(k == KD - 1 and n == 2))
                        last.then_inc(w_used, 1)
                pe.wait_ge(cv_step, upto(cv_step, l, 4 * KF))
                for k in range(KF):
                    s = (C_DN + k) % RING
                    arrived(l, C_DN + k)
                    pe.wait_ge(gl, upto(gl, l, k + 1))
                    for t in range(T):
                        rows = (act_hi[:, k % KD, t * P:(t + 1) * P], act_lo[:, k % KD, t * P:(t + 1) * P])
                        for half in range(2):
                            cols = slice(512 * half, 512 * half + 512)
                            for n, (a, b) in enumerate(passes(rows, (w_hi[:, s, cols], w_lo[:, s, cols]))):
                                last = mm(bank[:, t + 4 * half, :], a, b, start=(k == 0 and n == 0),
                                          stop=(k == KF - 1 and n == 2))
                        if k == KF - 1 and t < T - 1:
                            last.then_inc(dn_done, 1)
                    last.then_inc(w_used, 1)


def _constants():
    f = np.float32
    out = np.zeros((P, NCONST), f)
    inv = f(1.0) / f(10000.0) ** np.linspace(0.0, 1.0, DK // 2, dtype=f)
    ang = (np.arange(SEQ, dtype=f)[:, None] * inv[None, :]).astype(f)
    tab = lambda a: a.astype(f).reshape(T, P, DK // 2).transpose(1, 0, 2).reshape(P, -1)
    out[:, O_COS:O_SIN], out[:, O_SIN:O_NSIN], out[:, O_NSIN:O_DM] = tab(np.cos(ang)), tab(np.sin(ang)), tab(-np.sin(ang))
    log_g = np.log(f(1.0) - f(2.0) ** (f(-5.0) - np.arange(RH, dtype=f))).astype(f)
    i = np.arange(P, dtype=f)
    diff = i[None, :] - i[:, None]
    scale = f(DK ** -0.5)
    dm = np.where(diff >= 0, np.exp(np.maximum(diff, 0)[None] * log_g[:, None, None]), 0).astype(f)
    out[:, O_DM:O_XI] = (dm * scale).transpose(1, 0, 2).reshape(P, -1)
    xi = np.exp((i + 1)[None, :] * log_g[:, None]).astype(f)
    out[:, O_XI:O_ZE] = np.repeat(xi.reshape(4, 2, 1, P), DK, axis=2).reshape(4, P, P).transpose(1, 0, 2).reshape(P, -1)
    out[:, O_ZE:O_BD] = np.exp((P - 1 - i)[:, None] * log_g[None, :])
    out[:DK, O_BD:O_BD + DK] = scale
    out[DK:, O_BD + DK:O_DE] = scale
    out[:, O_DE:O_ID] = np.repeat(np.exp(P * log_g).astype(f).reshape(4, 2), DK, axis=1).T
    out[:, O_ID:O_CA] = np.eye(P, dtype=f)
    out[:, O_CA:O_CM] = np.where(np.arange(P)[None, :] <= np.arange(P)[:, None], 0, NEG)
    tok = np.arange(SEQ).reshape(T, P).T[:, :, None]
    c = np.arange(NCP)[None, None, :]
    out[:, O_CM:] = np.where((c < NC) & (c * CS + CB - 1 <= tok), 0, NEG).reshape(P, -1)
    return out


def _stream(w_in, w_out, kw1, vw1, w_up, w_down):
    st = np.zeros((DEPTH, NCH, P, CW), np.float32)

    def token(c0, w):
        n = w.shape[-1]
        st[:, c0:c0 + 4, :, :2 * n] = w.reshape(DEPTH, 4, 2, P, n).transpose(0, 1, 3, 2, 4).reshape(DEPTH, 4, P, 2 * n)

    def feature(c, w):
        st[:, c] = w.reshape(DEPTH, KD, P, P).transpose(0, 2, 1, 3).reshape(DEPTH, P, CW)

    r = RH * DK
    for b in range(4):
        token(C_T + 4 * b, w_in[:, :, b * r:(b + 1) * r])
    nq, kv = 4 * r, 4 * r + NH * DH
    col = lambda s: w_in[:, :, kv + s * NKV * DH:kv + (s + 1) * NKV * DH]
    token(C_TV, np.concatenate([col(3), col(5), w_in[:, :, kv + 6 * NKV * DH:]], axis=-1))
    feature(C_F0, col(0))
    feature(C_F1, col(1))
    for c0, w in ((C_W1K, kw1), (C_W1V, vw1)):
        st[:, c0:c0 + 4] = w.reshape(DEPTH, 4, 4, P, HID).transpose(0, 1, 3, 2, 4).reshape(DEPTH, 4, P, CW)
    feature(C_F2, col(2))
    feature(C_F2 + 1, col(4))
    for f in range(4):
        feature(C_F2 + 2 + f, w_in[:, :, nq + f * P:nq + (f + 1) * P])
    for half in range(2):
        token(C_WO + 4 * half, w_out[:, :, half * 512:(half + 1) * 512])
    for n in range(KF):
        feature(C_UP + 2 * n, w_up[:, :, n * P:(n + 1) * P])
        feature(C_UP + 2 * n + 1, w_up[:, :, FF + n * P:FF + (n + 1) * P])
    st[:, C_DN:] = w_down.reshape(DEPTH, KF, P, D)
    return st


def _parameters(kpos, vpos, kb1, vb1, kw2, vw2, kb2, conv_w, conv_b):
    out = np.zeros((DEPTH, P, NPAR), np.float32)
    for s, pos in enumerate((kpos, vpos)):
        out[:, :, Q_POS + 16 * s:Q_POS + 16 * s + 16] = pos.reshape(DEPTH, 16, P).transpose(0, 2, 1)
    for s, b in enumerate((kb1, vb1)):
        out[:, :, Q_B1 + 2 * s:Q_B1 + 2 * s + 2] = b.reshape(DEPTH, 2, P).transpose(0, 2, 1)
    for s, w in enumerate((kw2, vw2)):
        out[:, :, Q_W2 + 2 * DH * s:Q_W2 + 2 * DH * (s + 1)] = w.reshape(DEPTH, 2, P, DH).transpose(0, 2, 1, 3).reshape(DEPTH, P, -1)
    out[:, :DH, Q_B2K] = kb2
    taps = np.concatenate([conv_w, conv_b[:, None]], axis=1)
    out[:, :, Q_CV:] = taps.reshape(DEPTH, 4, 2 * KF, P).transpose(0, 3, 2, 1).reshape(DEPTH, P, -1)
    return out


def kernel(x, ln_mix_pre, ln_mix_post, ln_ffn_pre, ln_ffn_post, w_in, w_out, cmp_k_pos, cmp_k_w1, cmp_k_b1,
           cmp_k_w2, cmp_k_b2, cmp_v_pos, cmp_v_w1, cmp_v_b1, cmp_v_w2, cmp_v_b2, ffn_w_up, ffn_conv_w,
           ffn_conv_b, ffn_w_down):
    import concourse.bacc as bacc
    from concourse.bass_utils import run_bass_kernel_spmd

    a = lambda v: np.asarray(v)
    gains = np.zeros((DEPTH + 1, 2, 3 * D), np.float32)
    gains[:DEPTH, 0, :D] = a(ln_mix_pre)
    gains[:DEPTH, 1, :D], gains[:DEPTH, 1, D:2 * D] = a(ln_mix_post), a(ln_ffn_pre)
    gains[:DEPTH, 1, 2 * D:] = a(ln_ffn_post)
    arrays = {
        "x_in": a(x).reshape(SEQ, D),
        "wstream": _stream(a(w_in), a(w_out), a(cmp_k_w1), a(cmp_v_w1), a(ffn_w_up), a(ffn_w_down)),
        "gains": gains,
        "pars": _parameters(a(cmp_k_pos), a(cmp_v_pos), a(cmp_k_b1), a(cmp_v_b1), a(cmp_k_w2), a(cmp_v_w2),
                            a(cmp_k_b2), a(ffn_conv_w), a(ffn_conv_b)),
        "b2v_in": a(cmp_v_b2).reshape(DEPTH, 1, DH),
        "consts": _constants(),
    }
    nc = bacc.Bacc("TRN2", target_bir_lowering=False, num_devices=1)
    args = {n: nc.dram_tensor(n, v.shape, mybir.dt.from_np(v.dtype), kind="ExternalInput").ap()
            for n, v in arrays.items()}
    x_out = nc.dram_tensor("x_out", (SEQ, D), F32, kind="ExternalOutput").ap()
    build(nc, **args, x_out=x_out)
    r = run_bass_kernel_spmd(nc, [arrays], core_ids=[0])
    return r.results[0]["x_out"].reshape(1, SEQ, D)
```

```python
from contextlib import ExitStack

import numpy as np

import concourse.bass as bass
from concourse import mybir

F32 = mybir.dt.float32
F32R = mybir.dt.float32r
BF16 = mybir.dt.bfloat16
ACT = mybir.ActivationFunctionType
ALU = mybir.AluOpType
AXX = mybir.AxisListType.X

P = 128
DEPTH, SEQ, D = 2, 512, 1024
T = SEQ // P
KD = D // P
RH, DK = 8, 64
NH, NKV, DH = 8, 2, 64
G = NH // NKV
CB, CS = 32, 16
NC = (SEQ - CB) // CS + 1
NCP = 32
HID = 4 * DH
FF = 2816
KF = FF // P
EPS = 1e-6
NEG = -1e30
NEG_GUARD = -1e29
SM = DH ** -0.5
EB = 3

CW = 1024
RING = 4
C_T = 0
C_TV = C_T + 16
NTV = 2 * NKV * DH + 3 * NH
C_F0 = C_TV + 4
C_F1 = C_F0 + 1
C_W1K = C_F1 + 1
C_W1V = C_W1K + 4
C_F2 = C_W1V + 4
C_WO = C_F2 + 6
C_UP = C_WO + 8
C_DN = C_UP + 2 * KF
NCH = C_DN + KF

O_COS, O_SIN, O_NSIN = 0, 128, 256
O_DM = 384
O_XI = O_DM + RH * P
O_ZE = O_XI + 4 * P
O_BD = O_ZE + RH
O_DE = O_BD + P
O_ID = O_DE + 4
O_CA = O_ID + P
O_CM = O_CA + P
NCONST = O_CM + T * NCP

Q_POS = 0
Q_B1 = Q_POS + 2 * 16
Q_W2 = Q_B1 + 4
Q_B2K = Q_W2 + 4 * DH
Q_CV = Q_B2K + 2
NPAR = Q_CV + 2 * KF * 4


MIDDLE = [("turn", 0), ("chunk", C_F0), ("score", 0), ("chunk", C_F1), ("out", 0), ("turn", 1),
          ("chunk", C_W1K), ("chunk", C_W1K + 1), ("norm", 0), ("score", 1), ("chunk", C_W1K + 2),
          ("chunk", C_W1K + 3), ("out", 1), ("turn", 2), ("norm", 1), ("chunk", C_W1V), ("score", 2),
          ("chunk", C_W1V + 1), ("out", 2), ("turn", 3), ("norm", 2), ("chunk", C_W1V + 2), ("score", 3),
          ("chunk", C_W1V + 3), ("out", 3), ("norm", 3)]
RET_NORM_AFTER = {C_W1K + 1: 0, C_W1V + 1: 1, C_W1V + 3: 2, C_F2 + 1: 3}


def build(nc, x_in, wstream, gains, pars, b2v_in, consts, x_out):
    ctx = ExitStack()
    with ctx:
        def sb(name, shape, dt=F32, stack=ctx):
            return stack.enter_context(nc.sbuf_tensor(name, shape, dt))

        sems = {}

        def sem(name, per_layer, start=0):
            s = ctx.enter_context(nc.semaphore(name))
            sems[name] = (s, per_layer, start)
            return s

        def upto(s, layer, count):
            per, start = next((n, f) for q, n, f in sems.values() if q is s)
            assert count + start > 0, s
            return layer * per + (count + start)

        const = sb("const", [P, NCONST])
        ident_b = sb("ident_b", [P, P], BF16)
        causal_b = sb("causal_b", [P, P], BF16)
        cmask_b = sb("cmask_b", [P, T * NCP], BF16)
        x = sb("x", [P, T, D])
        act_hi = sb("act_hi", [P, KD, SEQ], F32R)
        act_lo = sb("act_lo", [P, KD, SEQ], F32R)
        raw = sb("raw", [P, RING, CW])
        w_hi = sb("w_hi", [P, RING, CW], F32R)
        w_lo = sb("w_lo", [P, RING, CW], F32R)
        g_mix_pre = sb("g_mix_pre", [P, D])
        g_rest = sb("g_rest", [P, 3, D])
        par = sb("par", [P, NPAR])
        b2v = sb("b2v", [NCP, DH])
        gate = sb("gate", [P, T, 3 * NH])
        sq_sum = sb("sq_sum", [P, 24])
        mean = sb("mean", [P, 4 * T])
        mean_eps = sb("mean_eps", [P, 4 * T])
        rstd = sb("rstd", [P, 4 * T])
        head_eps = sb("head_eps", [P, RH])
        head_rstd = sb("head_rstd", [P, RH])
        minus_half = sb("minus_half", [P, RH])
        eps1 = sb("eps1", [P, 1])
        eps4 = sb("eps4", [P, RH])
        head_ms = sb("head_ms", [P, RH])
        s_max = sb("s_max", [P, EB, G])
        s_bias = sb("s_bias", [P, EB, G])
        s_sum = sb("s_sum", [P, EB, G])
        s_rec = sb("s_rec", [P, EB, G])
        c_stat = sb("c_stat", [P, NH * T])
        c_rec = sb("c_rec", [P, NH * T])
        VS = sb("VS", [P, T, 2 * NKV, 2 * DH], F32R)
        KcH = sb("KcH", [P, NKV * NCP], F32R)
        KcL = sb("KcL", [P, NKV * NCP], F32R)
        VcS = sb("VcS", [NCP, NKV, 2 * DH], F32R)
        kcf = sb("kcf", [DH, NKV * NCP])
        vcf = sb("vcf", [NCP, NKV, DH])
        with ExitStack() as ret:
            qr = sb("qr", [P, T, RH * DK], F32, ret)
            kr = sb("kr", [P, T, RH * DK], F32, ret)
            rv = sb("rv", [P, T, RH * DK], F32, ret)
            sg = sb("sg", [P, T, RH * DK], F32, ret)
            qT = sb("qT", [P, 4, P], F32, ret)
            qxT = sb("qxT", [P, 4, P], F32, ret)
            kT = sb("kT", [P, 4, P], F32, ret)
            stm = sb("stm", [P, RH, P], F32, ret)
            vz = sb("vz", [P, RH * DK], F32, ret)
            state = sb("state", [P, 4, P], F32, ret)
            kvt = sb("kvt", [P, 4, P], F32, ret)
            rtmp = sb("rtmp", [P, RH * DK], F32, ret)
            th = sb("th", [P, RH * DK], F32, ret)
            osq = sb("osq", [P, RH * DK], F32, ret)
            with ExitStack() as early:
                h = sb("h", [P, 2, D], F32, early)
                mix = sb("mix", [P, D], F32, early)
                junk = sb("junk", [P, D], BF16, early)
            zf = sb("zf", [P, 16, NKV, NCP], F32, ret)
            z_hi = sb("z_hi", [P, 16 * NKV * NCP], F32R, ret)
            z_lo = sb("z_lo", [P, 16 * NKV * NCP], F32R, ret)
            hid = sb("hid", [P, 2, 2, NKV * NCP], F32, ret)
        with ExitStack() as att:
            E = sb("E", [P, EB, G, SEQ], F32, att)
            QS = sb("QS", [P, NH, SEQ], F32R, att)
            KH = sb("KH", [P, 2 * NKV, SEQ], F32R, att)
            KL = sb("KL", [P, 2 * NKV, SEQ], F32R, att)
            pt_h = sb("pt_h", [P, 2, G * P], F32R, att)
            pt_l = sb("pt_l", [P, 2, G * P], F32R, att)
            o_a = sb("o_a", [DH, G * P], F32, att)
            o_f = sb("o_f", [P, 2, P], F32, att)
            cE = sb("cE", [P, T * NKV * G, NCP], F32, att)
        with ExitStack() as ffn:
            gff = sb("gff", [P, KF, SEQ], F32, ffn)
            cv = sb("cv", [P, 2, 2, SEQ], F32, ffn)
        bank = ctx.enter_context(nc.psum_tensor("bank", [P, 8, 512], F32))

        cos = const[:, O_COS:O_SIN].rearrange("p (t f) -> p t f", t=T)
        sin = const[:, O_SIN:O_NSIN].rearrange("p (t f) -> p t f", t=T)
        nsin = const[:, O_NSIN:O_DM].rearrange("p (t f) -> p t f", t=T)
        dmask = const[:, O_DM:O_XI].rearrange("p (h c) -> p h c", h=RH)
        xi = const[:, O_XI:O_ZE].rearrange("p (a c) -> p a c", a=4)
        zeta = const[:, O_ZE:O_BD]
        bdiag = const[:, O_BD:O_DE]
        decay = const[:, O_DE:O_ID]
        ident = const[:, O_ID:O_CA]
        r32 = lambda ap: ap.bitcast(F32)

        AHEAD = 8
        raw_loaded = [sem(f"raw_loaded{s}", 16 * len(range(s, NCH, RING))) for s in range(RING)]
        hi_ready = sem("hi_ready", NCH)
        lo_ready = sem("lo_ready", NCH, start=RING)
        w_used = sem("w_used", NCH, start=RING)
        const_loaded = sem("const_loaded", 0)
        const_cast = sem("const_cast", 0)
        half_set = sem("half_set", 0)
        mixpre_loaded = sem("mixpre_loaded", 16)
        par_loaded = sem("par_loaded", 48)
        sq_done = sem("sq_done", 24, start=1)
        rstd_step = sem("rstd_step", 48, start=1)
        h_ready = sem("h_ready", 8, start=1)
        h_turned = sem("h_turned", 8)
        act_h = sem("act_h", 16)
        act_l = sem("act_l", 16)
        x_step = sem("x_step", 24, start=13)
        t_done = sem("t_done", 15)
        rot_step = sem("rot_step", 32, start=1)
        rv_ready = sem("rv_ready", 4)
        th_ready = sem("th_ready", 4)
        sg_ready = sem("sg_ready", 4)
        vg_act = sem("vg_act", 8)
        vg_dve = sem("vg_dve", 8)
        z_step = sem("z_step", 17)
        z_h = sem("z_h", 2)
        z_l = sem("z_l", 2)
        w1_done = sem("w1_done", 2)
        hid_ready = sem("hid_ready", 4)
        kc_done = sem("kc_done", 1)
        vc_done = sem("vc_done", 1)
        kc_f = sem("kc_f", 1)
        kc_h = sem("kc_h", 2)
        kc_l = sem("kc_l", 2)
        vc_f = sem("vc_f", 1)
        vc_h = sem("vc_h", 1)
        vc_l = sem("vc_l", 1)
        qk_turned = sem("qk_turned", 8)
        qk_copied = sem("qk_copied", 8)
        qx_ready = sem("qx_ready", 4)
        st_done = sem("st_done", 8)
        st_masked = sem("st_masked", 8)
        vz_ready = sem("vz_ready", 3)
        kv_done = sem("kv_done", 3)
        ro_done = sem("ro_done", 4)
        state_step = sem("state_step", 7)
        osq_ready = sem("osq_ready", 4)
        head_sum = sem("head_sum", 4)
        y_step = sem("y_step", 8)
        y_turned = sem("y_turned", 4)
        y_h = sem("y_h", 4)
        y_l = sem("y_l", 4)
        k_h = sem("k_h", 8)
        k_l = sem("k_l", 8)
        q_h = sem("q_h", 8)
        q_l = sem("q_l", 8)
        cs_done = sem("cs_done", 2)
        c_step = sem("c_step", 9)
        c_exp = sem("c_exp", 1)
        NU = T * NKV * 2
        s_done = sem("s_done", 2 * NU)
        m_step = sem("m_step", 4 * NU)
        e_done = sem("e_done", G * NU)
        r_step = sem("r_step", 6 * NU)
        p_scaled = sem("p_scaled", G * NU)
        NI = T * NKV + 2 * NKV * T * (T + 1) // 2
        pt_done = sem("pt_done", NI)
        pth = sem("pth", NI)
        ptl = sem("ptl", NI)
        pv_done = sem("pv_done", NI)
        oa_done = sem("oa_done", T * NKV)
        of_done = sem("of_done", 2 * T * NKV)
        oh_done = sem("oh_done", T * NKV)
        ol_done = sem("ol_done", T * NKV)
        wo_done = sem("wo_done", 6)
        cv0 = sem("cv0", 2 * KF)
        cv_step = sem("cv_step", 4 * KF, start=AHEAD)
        gelu_done = sem("gelu_done", KF)
        g_ready = sem("g_ready", KF, start=1)
        gh = sem("gh", KF)
        gl = sem("gl", KF)
        dn_done = sem("dn_done", T - 1)
        stored = sem("stored", 0)

        Y_BANK = (4, 5, 2, 3)

        UNITS = [(i, g, b) for i in range(T) for g in range(NKV) for b in range(2)]
        ITEMS = []
        UNIT_ITEMS = []
        for n, (i, g, b) in enumerate(UNITS):
            at = len(ITEMS)
            ITEMS += [(n, i * NKV + g, j) for j in range(i + 1)]
            if b == 1:
                ITEMS.append((None, i * NKV + g, 0))
            UNIT_ITEMS.append(range(at, len(ITEMS)))
        assert len(ITEMS) == NI
        FIRST_OF_V = {v: min(k for k, it in enumerate(ITEMS) if it[1] == v) for v in range(T * NKV)}
        LAST_OF_V = {v: max(k for k, it in enumerate(ITEMS) if it[1] == v) for v in range(T * NKV)}
        last_turn = lambda n: max(k for k, it in enumerate(ITEMS) if it[0] == n)

        SCORES_AT = {}
        for n in range(2, NU):
            for p in range(2):
                before = UNIT_ITEMS[n - 2]
                SCORES_AT[n, p] = max([before[0] + p * (len(before) // 2)]
                                      + [SCORES_AT[q] + 1 for q in ((n - 1, p),) if q in SCORES_AT])
                assert SCORES_AT[n, p] + 2 <= UNIT_ITEMS[n][0]
        pairs_at = lambda k: [q for q, at in SCORES_AT.items() if at == k]

        RS_PRE1 = lambda t: 2 * t
        RS_RET = lambda n: 8 + 2 * n
        RS_POST2 = lambda t: 36 + 3 * t
        SQ_PRE1 = lambda t: t
        SQ_POST2 = lambda t: 16 + 2 * t
        MID_NORMS = [("post", 0), ("post", 1), ("pre", 0), ("post", 2), ("pre", 1), ("post", 3), ("pre", 2), ("pre", 3)]
        RS_MID, SQ_MID, rs, sq = {}, {}, 16, 4
        for what in MID_NORMS:
            RS_MID[what], SQ_MID[what] = rs, sq
            rs, sq = (rs + 3, sq + 2) if what[0] == "post" else (rs + 2, sq + 1)

        def slot_free(eng, s, layer, c):
            before = c - RING if c >= RING else max(range(c, NCH, RING)) - NCH
            eng.wait_ge(s, layer * NCH + (before + 1 + RING))

        def chunk_used(eng, layer, c):
            eng.wait_ge(w_used, layer * NCH + (c + 1 + RING))

        def tile_done(eng, layer, done, block_no, t, last_chunk):
            if t < T - 1:
                eng.wait_ge(done, upto(done, layer, (T - 1) * block_no + t + 1))
            else:
                chunk_used(eng, layer, last_chunk)

        block = ctx.enter_context(nc.Block())

        @block.sync
        def _(sp):
            sp.dma_start(const[:], consts).then_inc(const_loaded, 16)
            for t in range(T):
                sp.dma_start(x[:, t, :], x_in[t * P:(t + 1) * P, :]).then_inc(const_loaded, 16)
            sp.dma_start(g_mix_pre[:], gains[0, 0:1, 0:D].broadcast_to([P, D])).then_inc(mixpre_loaded, 16)

            def load(layer, c, s, quad=None):
                if quad is None:
                    slot_free(sp, lo_ready, layer, c)
                    sp.dma_start(raw[:, s, :], wstream[layer, c]).then_inc(raw_loaded[s], 16)
                else:
                    sp.wait_ge(lo_ready, layer * NCH + quad * RING + (s + 1))
                    sp.dma_start(raw[:, s, :], wstream[layer, quad * RING + s]).then_inc(raw_loaded[s], 16)

            with sp.Fori(0, DEPTH) as l:
                for c in range(RING):
                    load(l, c, c)
                sp.wait_ge(x_step, upto(x_step, l, 0))
                sp.dma_start(par[:], pars[l]).then_inc(par_loaded, 16)
                sp.dma_start(b2v[:], b2v_in[l, 0:1, :].broadcast_to([NCP, DH])).then_inc(par_loaded, 16)
                sp.dma_start(g_rest[:].rearrange("p a d -> p (a d)"),
                             gains[l, 1:2, :].broadcast_to([P, 3 * D])).then_inc(par_loaded, 16)
                with sp.Fori(1, C_UP // RING) as quad:
                    for s in range(RING):
                        load(l, None, s, quad)
                sp.wait_ge(h_ready, upto(h_ready, l, 4))
                sp.dma_start(g_mix_pre[:], gains[l + 1, 0:1, 0:D].broadcast_to([P, D]))\
                    .then_inc(mixpre_loaded, 16)
                with sp.Fori(C_UP // RING, NCH // RING) as quad:
                    for s in range(RING):
                        load(l, None, s, quad)
                for c in range(NCH // RING * RING, NCH):
                    load(l, c, c % RING)
            for t in range(T):
                sp.wait_ge(x_step, upto(x_step, DEPTH - 1, 12 + 3 * (t + 1)))
                sp.dma_start(x_out[t * P:(t + 1) * P, :], x[:, t, :]).then_inc(stored, 16)
            sp.wait_ge(stored, 16 * T)
            sp.wait_ge(mixpre_loaded, 16 * (DEPTH + 1))

        @block.gpsimd
        def _(pool):
            pool.sem_inc(lo_ready, RING)
            pool.sem_inc(rstd_step, 1)
            nc.gpsimd.memset(minus_half[:], -0.5).then_inc(half_set, 1)
            nc.gpsimd.memset(eps1[:], EPS).then_inc(half_set, 1)
            nc.gpsimd.memset(eps4[:], 4.0 * EPS).then_inc(half_set, 1)
            pool.wait_ge(half_set, 3)

            def split_lo(layer, c):
                s = c % RING
                pool.wait_ge(hi_ready, upto(hi_ready, layer, c + 1))
                slot_free(pool, w_used, layer, c)
                nc.gpsimd.tensor_tensor(w_lo[:, s, :], raw[:, s, :], r32(w_hi[:, s, :]), ALU.subtract)\
                    .then_inc(lo_ready, 1)

            def split_lo_quad(layer, quad):
                for s in range(RING):
                    pool.wait_ge(hi_ready, layer * NCH + quad * RING + (s + 1))
                    pool.wait_ge(w_used, layer * NCH + quad * RING + (s + 1))
                    nc.gpsimd.tensor_tensor(w_lo[:, s, :], raw[:, s, :], r32(w_hi[:, s, :]),
                                            ALU.subtract).then_inc(lo_ready, 1)

            def inv_root(layer, step, source, eps, with_eps, out):
                nc.gpsimd.tensor_tensor(with_eps, source, eps, ALU.add).then_inc(rstd_step, 1)
                pool.wait_ge(rstd_step, upto(rstd_step, layer, step + 1))
                nc.gpsimd.tensor_tensor(out, with_eps, minus_half[:, 0:out.shape[-1]], ALU.pow)\
                    .then_inc(rstd_step, 1)

            def inv_root_pre(layer, step, sq, col):
                pool.wait_ge(sq_done, upto(sq_done, layer, sq + 1))
                inv_root(layer, step, sq_sum[:, sq:sq + 1], eps1[:], mean_eps[:, col:col + 1], rstd[:, col:col + 1])

            def inv_root_post(layer, step, sq, col):
                pool.wait_ge(sq_done, upto(sq_done, layer, sq + 2))
                nc.gpsimd.tensor_tensor(mean[:, col:col + 1], sq_sum[:, sq:sq + 1], sq_sum[:, sq + 1:sq + 2],
                                        ALU.add).then_inc(rstd_step, 1)
                pool.wait_ge(rstd_step, upto(rstd_step, layer, step + 1))
                inv_root(layer, step + 1, mean[:, col:col + 1], eps1[:], mean_eps[:, col:col + 1],
                         rstd[:, col:col + 1])

            with pool.Fori(0, DEPTH) as l:
                for t in range(T):
                    inv_root_pre(l, RS_PRE1(t), SQ_PRE1(t), 4 * t)
                    split_lo(l, t)
                with pool.Fori(1, C_F0 // RING) as quad:
                    split_lo_quad(l, quad)
                for c in range(C_F0, C_F2 + 4):
                    split_lo(l, c)
                    if c in RET_NORM_AFTER:
                        n = RET_NORM_AFTER[c]
                        pool.wait_ge(head_sum, upto(head_sum, l, n + 1))
                        if n:
                            pool.wait_ge(y_step, upto(y_step, l, 2 * n - 1))
                            pool.wait_ge(rstd_step, upto(rstd_step, l, RS_RET(n)))
                        inv_root(l, RS_RET(n), head_ms[:], eps4[:], head_eps[:], head_rstd[:])
                for c in range(C_F2 + 4, C_WO + RING):
                    split_lo(l, c)
                def scale(n, p):
                    i = UNITS[n][0]
                    pool.wait_ge(r_step, upto(r_step, l, 6 * n + 3 * p + 3))
                    for r in (2 * p, 2 * p + 1):
                        e = E[:, n % EB, r, 0:P * (i + 1)]
                        nc.gpsimd.tensor_tensor(e, e, s_rec[:, n % EB, r:r + 1].broadcast_to([P, P * (i + 1)]),
                                                ALU.mult).then_inc(p_scaled, 1)

                def out_rest(v):
                    i, g = v // NKV, v % NKV
                    dst = (slice(None), slice(4 + 2 * g, 6 + 2 * g), slice(i * P, (i + 1) * P))
                    pool.wait_ge(oh_done, upto(oh_done, l, v + 1))
                    nc.gpsimd.tensor_tensor(act_lo[dst], o_f[:], r32(act_hi[dst]), ALU.subtract).then_inc(ol_done, 1)

                for n in range(2):
                    for p in range(2):
                        scale(n, p)
                for n in range(NU):
                    for k in UNIT_ITEMS[n]:
                        if k - 3 in LAST_OF_V.values():
                            out_rest(ITEMS[k - 3][1])
                        for unit, p in pairs_at(k - 2):
                            scale(unit, p)
                out_rest(T * NKV - 1)
                for c in range(C_WO + RING, C_UP):
                    split_lo(l, c)
                for what, t in MID_NORMS:
                    if (what, t) == ("post", T - 1):
                        split_lo(l, C_UP)
                    if what == "post":
                        inv_root_post(l, RS_MID[what, t], SQ_MID[what, t], 4 * t + 1)
                    else:
                        inv_root_pre(l, RS_MID[what, t], SQ_MID[what, t], 4 * t + 2)
                for c in range(C_UP + 1, C_UP + RING):
                    split_lo(l, c)
                with pool.Fori(C_UP // RING + 1, NCH // RING) as quad:
                    split_lo_quad(l, quad)
                for c in range(NCH // RING * RING, NCH):
                    split_lo(l, c)
                for t in range(T):
                    inv_root_post(l, RS_POST2(t), SQ_POST2(t), 4 * t + 3)

        @block.scalar
        def _(act):
            def hi(layer, c):
                s = c % RING
                act.wait_ge(raw_loaded[s], upto(raw_loaded[s], layer, 16 * (c // RING + 1)))
                slot_free(act, w_used, layer, c)
                nc.scalar.activation(w_hi[:, s, :], raw[:, s, :], ACT.Copy).then_inc(hi_ready, 1)

            def hi_quad(layer, quad, s):
                act.wait_ge(raw_loaded[s], layer * sems[f"raw_loaded{s}"][1] + quad * 16 + 16)
                act.wait_ge(w_used, layer * NCH + quad * RING + (s + 1))
                nc.scalar.activation(w_hi[:, s, :], raw[:, s, :], ACT.Copy).then_inc(hi_ready, 1)

            def square_pre(layer, t, sq):
                act.wait_ge(sq_done, upto(sq_done, layer, sq))
                nc.scalar.activation(junk[:], x[:, t, :], ACT.Square, scale=D ** -0.5,
                                     accum_out=sq_sum[:, sq:sq + 1]).then_inc(sq_done, 1)

            def square_post(layer, t, sq):
                for half in range(2):
                    act.wait_ge(sq_done, upto(sq_done, layer, sq + half))
                    nc.scalar.activation(junk[:, 0:512], bank[:, t + 4 * half, :], ACT.Square, scale=D ** -0.5,
                                         accum_out=sq_sum[:, sq + half:sq + half + 1]).then_inc(sq_done, 1)

            def act_halves(layer, n, t):
                act.wait_ge(h_turned, upto(h_turned, layer, n + 1))
                for k2 in range(2):
                    nc.scalar.activation(act_hi[:, 4 * k2:4 * k2 + 4, t * P:(t + 1) * P],
                                         bank[:, t + 4 * k2, :].rearrange("p (k c) -> p k c", k=4),
                                         ACT.Copy).then_inc(act_h, 1)

            act.sem_inc(sq_done, 1)
            act.wait_ge(const_loaded, 16 * (1 + T))
            with act.Fori(0, DEPTH) as l:
                for t in range(T):
                    act.wait_ge(x_step, upto(x_step, l, 3 * (t + 1) - 12))
                    square_pre(l, t, SQ_PRE1(t))
                    hi(l, t)
                    if t:
                        act_halves(l, t - 1, t - 1)
                act_halves(l, T - 1, T - 1)
                for blk in range(5):
                    for c in range(4 * blk + 4, 4 * blk + 8):
                        hi(l, c)
                    if blk == 2:
                        for t in range(T):
                            tile_done(act, l, t_done, 2, t, 11)
                            nc.scalar.activation(rv[:, t, :], bank[:, 4 + t, :], ACT.Copy).then_inc(rv_ready, 1)
                    if blk == 3:
                        for t in range(T):
                            tile_done(act, l, t_done, 3, t, 15)
                            if t:
                                act.wait_ge(sg_ready, upto(sg_ready, l, t))
                            nc.scalar.activation(th[:], bank[:, t, :], ACT.Tanh, scale=0.5).then_inc(th_ready, 1)
                    if blk == 4:
                        for t in range(T):
                            tile_done(act, l, t_done, 4, t, 19)
                            nc.scalar.activation(
                                VS[:, t, :, 0:DH], bank[:, 4 + t, 0:4 * DH].rearrange("p (a d) -> p a d", a=4),
                                ACT.Copy).then_inc(vg_act, 1)
                            nc.scalar.activation(gate[:, t, :], bank[:, 4 + t, 4 * DH:NTV], ACT.Tanh, scale=0.5)\
                                .then_inc(vg_act, 1)

                def turned_copies(n):
                    for m, dst in ((0, qT), (1, kT)):
                        act.wait_ge(qk_turned, upto(qk_turned, l, 2 * n + m + 1))
                        if n and m == 0:
                            act.wait_ge(ro_done, upto(ro_done, l, n))
                        nc.scalar.activation(dst[:].rearrange("p a c -> p (a c)"), bank[:, 2 + m, :], ACT.Copy)\
                            .then_inc(qk_copied, 1)

                def out_squares(n):
                    act.wait_ge(ro_done, upto(ro_done, l, n + 1))
                    if n:
                        act.wait_ge(head_sum, upto(head_sum, l, n))
                    nc.scalar.activation(osq[:], bank[:, 6, :], ACT.Square, scale=2.0 * DK ** -0.5).then_inc(osq_ready, 1)

                def z_round(s):
                    act.wait_ge(z_step, upto(z_step, l, 1 + 8 * (s + 1)))
                    if s:
                        chunk_used(act, l, C_W1K + 3)
                    nc.scalar.activation(z_hi[:], zf[:].rearrange("p m g c -> p (m g c)"), ACT.Copy)\
                        .then_inc(z_h, 1)

                def hidden(s):
                    for m in range(2):
                        if m == 0:
                            act.wait_ge(w1_done, upto(w1_done, l, s + 1))
                        else:
                            chunk_used(act, l, (C_W1K, C_W1V)[s] + 3)
                        nc.scalar.activation(hid[:, s, m, :], bank[:, m, 0:NKV * NCP],
                                             ACT.Gelu_apprx_tanh,
                                             bias=par[:, Q_B1 + 2 * s + m:Q_B1 + 2 * s + m + 1])\
                            .then_inc(hid_ready, 1)

                act.wait_ge(par_loaded, upto(par_loaded, l, 48))
                for what, n in MIDDLE:
                    if what == "chunk" and n + RING < C_F2 + 2:
                        hi(l, n + RING)
                    if what == "turn":
                        turned_copies(n)
                    if what == "out":
                        out_squares(n)
                    if what == "chunk" and n == C_F0:
                        z_round(0)
                    if what == "chunk" and n == C_W1K + 3:
                        hidden(0)
                        z_round(1)
                    if what == "chunk" and n == C_W1V + 3:
                        hidden(1)
                act.wait_ge(kc_done, upto(kc_done, l, 1))
                nc.scalar.activation(kcf[:], bank[0:DH, 6, 0:NKV * NCP], ACT.Identity,
                                     bias=par[0:DH, Q_B2K:Q_B2K + 1]).then_inc(kc_f, 1)
                act.wait_ge(kc_f, upto(kc_f, l, 1))
                for half in range(2):
                    nc.scalar.activation(KcH[half * DH:(half + 1) * DH, :], kcf[:], ACT.Copy).then_inc(kc_h, 1)
                act.wait_ge(vc_f, upto(vc_f, l, 1))
                nc.scalar.activation(VcS[:, :, 0:DH], vcf[:], ACT.Copy).then_inc(vc_h, 1)
                act.wait_ge(y_step, upto(y_step, l, 8))
                for f in range(2):
                    hi(l, C_F2 + f + 2)
                    chunk_used(act, l, C_F2 + f)
                    for g in range(NKV):
                        for half in range(2):
                            nc.scalar.activation(KH[half * DH:(half + 1) * DH, 2 * f + g, :],
                                                 bank[g * DH:(g + 1) * DH, 2 + f, :], ACT.Copy).then_inc(k_h, 1)
                for f in range(4):
                    hi(l, C_F2 + f + 4)
                    chunk_used(act, l, C_F2 + 2 + f)
                    for m in range(2):
                        nc.scalar.activation(QS[m * DH:(m + 1) * DH, 2 * f + m, :],
                                             bank[m * DH:(m + 1) * DH, f % 2, :], ACT.Copy).then_inc(q_h, 1)
                hi(l, C_WO + 2)
                hi(l, C_WO + 3)
                for n in range(T):
                    act.wait_ge(y_turned, upto(y_turned, l, n + 1))
                    nc.scalar.activation(act_hi[:, 0:4, n * P:(n + 1) * P],
                                         bank[:, Y_BANK[n], :].rearrange("p (k c) -> p k c", k=4),
                                         ACT.Copy).then_inc(y_h, 1)

                def exps(n, p):
                    i = UNITS[n][0]
                    act.wait_ge(m_step, upto(m_step, l, 4 * n + 2 * p + 2))
                    if n >= EB:
                        act.wait_ge(pt_done, upto(pt_done, l, last_turn(n - EB) + 1))
                        act.wait_ge(r_step, upto(r_step, l, 6 * (n - EB) + 3 * p + 1))
                    for r in (2 * p, 2 * p + 1):
                        nc.scalar.activation(E[:, n % EB, r, 0:P * (i + 1)], bank[:, r, 0:P * (i + 1)],
                                             ACT.Exp, bias=s_bias[:, n % EB, r:r + 1], scale=SM,
                                             accum_out=s_sum[:, n % EB, r:r + 1]).then_inc(e_done, 1)

                def p_round(k):
                    rows = NCP if ITEMS[k][0] is None else P
                    act.wait_ge(pt_done, upto(pt_done, l, k + 1))
                    if k >= 2:
                        act.wait_ge(pv_done, upto(pv_done, l, k - 1))
                    nc.scalar.activation(pt_h[0:rows, k % 2, :], bank[0:rows, 4 + k % 2, :], ACT.Copy)\
                        .then_inc(pth, 1)

                def out_first(v):
                    act.wait_ge(pv_done, upto(pv_done, l, LAST_OF_V[v] + 1))
                    if v:
                        act.wait_ge(of_done, upto(of_done, l, 2 * v))
                    nc.scalar.activation(o_a[:], bank[0:DH, 6 + v % 2, :], ACT.Copy).then_inc(oa_done, 1)

                def out_round(v):
                    i, g = v // NKV, v % NKV
                    act.wait_ge(of_done, upto(of_done, l, 2 * v + 2))
                    nc.scalar.activation(act_hi[:, 4 + 2 * g:6 + 2 * g, i * P:(i + 1) * P], o_f[:], ACT.Copy)\
                        .then_inc(oh_done, 1)

                for n in range(2):
                    for p in range(2):
                        exps(n, p)
                act.wait_ge(c_step, upto(c_step, l, 4))
                nc.scalar.activation(cE[:], cE[:], ACT.Exp, scale=SM).then_inc(c_exp, 1)
                for n in range(NU):
                    for k in UNIT_ITEMS[n]:
                        p_round(k)
                        for unit, p in pairs_at(k - 1):
                            exps(unit, p)
                        if k - 2 in LAST_OF_V.values():
                            out_first(ITEMS[k - 2][1])
                        if k - 3 in LAST_OF_V.values():
                            out_round(ITEMS[k - 3][1])
                out_first(T * NKV - 1)
                out_round(T * NKV - 1)

                for c in range(C_WO + RING, C_UP):
                    hi(l, c)
                for what, t in MID_NORMS:
                    if (what, t) == ("post", T - 1):
                        for c in range(C_UP, C_UP + 3):
                            hi(l, c)
                    if what == "post":
                        tile_done(act, l, wo_done, 1, t, C_WO + 7)
                        square_post(l, t, SQ_MID[what, t])
                    else:
                        act.wait_ge(x_step, upto(x_step, l, 3 * t + 3))
                        square_pre(l, t, SQ_MID[what, t])
                        if t:
                            act_halves(l, 4 + t - 1, t - 1)
                act_halves(l, 4 + T - 1, T - 1)
                hi(l, C_UP + 3)

                def conv_first(it, p, s):
                    act.wait_ge(w_used, l * NCH + it * RING + (C_UP + 2 * p + s + 1 + RING))
                    act.wait_ge(g_ready, l * KF + it * 2 + 1)
                    col = it * 2 + (s * KF + p)
                    w2 = par[:, Q_CV:Q_CV + 8 * KF].rearrange("p (n q) -> p n q", q=4)
                    nc.scalar.activation(cv[:, p, s, :], bank[:, 2 * p + s, :], ACT.Identity,
                                         bias=w2[:, bass.ds(col, 1), 3], scale=w2[:, bass.ds(col, 1), 2])\
                        .then_inc(cv0, 1)

                def gelu(it, p):
                    act.wait_ge(cv_step, l * (4 * KF) + it * 8 + (4 * p + 2 + AHEAD))
                    nc.scalar.activation(cv[:, p, 0, :], cv[:, p, 0, :], ACT.Gelu_apprx_tanh)\
                        .then_inc(gelu_done, 1)

                with act.Fori(0, KF // 2) as it:
                    for p in range(2):
                        for s in range(2):
                            conv_first(it, p, s)
                            hi_quad(l, it + (C_UP // RING + 1), 2 * p + s)
                        gelu(it, p)
                for k in range(KF):
                    if k >= KD:
                        act.wait_ge(w_used, upto(w_used, l, C_DN + k - KD + 1))
                    else:
                        act.wait_ge(w_used, upto(w_used, l, C_DN))
                    act.wait_ge(g_ready, upto(g_ready, l, k + 1))
                    nc.scalar.activation(act_hi[:, k % KD, :], gff[:, k, :], ACT.Copy).then_inc(gh, 1)
                    if C_DN + k + RING - 3 < NCH and k >= 3:
                        hi(l, C_DN + k + RING - 3)
                for t in range(T):
                    tile_done(act, l, dn_done, 0, t, NCH - 1)
                    square_post(l, t, SQ_POST2(t))

        @block.vector
        def _(dve):
            def minus(out, a, b):
                return nc.vector.tensor_tensor(out, a, b, ALU.subtract)

            def normalise(layer, n, t, gain, rs, col):
                if n % 4 >= 2:
                    dve.wait_ge(h_turned, upto(h_turned, layer, n - 1))
                dve.wait_ge(rstd_step, upto(rstd_step, layer, rs + 2))
                nc.vector.scalar_tensor_tensor(out=h[:, t % 2, :], in0=x[:, t, :], scalar=rstd[:, col:col + 1],
                                               in1=gain, op0=ALU.mult, op1=ALU.mult).then_inc(h_ready, 1)

            def act_rests(layer, n, t):
                for k2 in range(2):
                    dve.wait_ge(act_h, upto(act_h, layer, 2 * n + k2 + 1))
                    minus(act_lo[:, 4 * k2:4 * k2 + 4, t * P:(t + 1) * P],
                          bank[:, t + 4 * k2, :].rearrange("p (k c) -> p k c", k=4),
                          r32(act_hi[:, 4 * k2:4 * k2 + 4, t * P:(t + 1) * P])).then_inc(act_l, 1)

            def add_branch(layer, base, t, gain, rs, col):
                dve.wait_ge(x_step, upto(x_step, layer, base))
                dve.wait_ge(rstd_step, upto(rstd_step, layer, rs + 3))
                for half in range(2):
                    cols = slice(512 * half, 512 * half + 512)
                    nc.vector.scalar_tensor_tensor(out=mix[:, cols], in0=bank[:, t + 4 * half, :],
                                                   scalar=rstd[:, col:col + 1], in1=gain[:, cols],
                                                   op0=ALU.mult, op1=ALU.mult).then_inc(x_step, 1)
                dve.wait_ge(x_step, upto(x_step, layer, base + 2))
                nc.vector.tensor_tensor(x[:, t, :], x[:, t, :], mix[:], ALU.add).then_inc(x_step, 1)

            dve.sem_inc(cv_step, AHEAD)
            for s in (rot_step, h_ready, g_ready):
                dve.sem_inc(s, 1)
            dve.sem_inc(x_step, 13)
            dve.wait_ge(const_loaded, 16 * (1 + T))
            nc.vector.tensor_copy(ident_b[:], ident).then_inc(const_cast, 1)
            nc.vector.tensor_copy(causal_b[:], const[:, O_CA:O_CM]).then_inc(const_cast, 1)
            nc.vector.tensor_copy(cmask_b[:], const[:, O_CM:NCONST]).then_inc(const_cast, 1)

            with dve.Fori(0, DEPTH) as l:
                dve.wait_ge(mixpre_loaded, upto(mixpre_loaded, l, 16))
                for t in range(T):
                    normalise(l, t, t, g_mix_pre[:], RS_PRE1(t), 4 * t)
                    if t:
                        act_rests(l, t - 1, t - 1)
                act_rests(l, T - 1, T - 1)

                def rotate(m, dst, t, b):
                    at = 16 * m + 4 * t
                    src = bank[:, b, :].rearrange("p (h a f) -> p h a f", h=RH, a=2)
                    tmp = rtmp[:].rearrange("p (h a f) -> p h a f", h=RH, a=2)
                    wide = lambda tab: tab[:, t, :].unsqueeze(1).broadcast_to([P, RH, DK // 2])
                    tile_done(dve, l, t_done, m, t, 4 * m + 3)
                    nc.vector.tensor_tensor(
                        dst[:, t, :].rearrange("p (h f) -> p h f", f=DK // 2),
                        bank[:, b, :].rearrange("p (h f) -> p h f", f=DK // 2),
                        cos[:, t, :].unsqueeze(1).broadcast_to([P, 2 * RH, DK // 2]), ALU.mult)\
                        .then_inc(rot_step, 1)
                    dve.wait_ge(rot_step, upto(rot_step, l, at))
                    nc.vector.tensor_tensor(tmp[:, :, 0, :], src[:, :, 1, :], wide(nsin), ALU.mult)\
                        .then_inc(rot_step, 1)
                    nc.vector.tensor_tensor(tmp[:, :, 1, :], src[:, :, 0, :], wide(sin), ALU.mult)\
                        .then_inc(rot_step, 1)
                    dve.wait_ge(rot_step, upto(rot_step, l, at + 3))
                    nc.vector.tensor_tensor(dst[:, t, :], dst[:, t, :], rtmp[:], ALU.add).then_inc(rot_step, 1)

                for t in range(T):
                    rotate(0, qr, t, 4 + t)
                for t in range(T):
                    rotate(1, kr, t, t)
                for t in range(T):
                    dve.wait_ge(th_ready, upto(th_ready, l, t + 1))
                    nc.vector.scalar_tensor_tensor(out=sg[:, t, :], in0=th[:], scalar=1.0, in1=bank[:, t, :],
                                                   op0=ALU.add, op1=ALU.mult).then_inc(sg_ready, 1)
                for t in range(T):
                    dve.wait_ge(vg_act, upto(vg_act, l, 2 * t + 2))
                    minus(VS[:, t, :, DH:2 * DH], bank[:, 4 + t, 0:4 * DH].rearrange("p (a d) -> p a d", a=4),
                          r32(VS[:, t, :, 0:DH])).then_inc(vg_dve, 1)
                    nc.vector.tensor_scalar(gate[:, t, :], gate[:, t, :], 0.5, 0.5, ALU.mult, ALU.add)\
                        .then_inc(vg_dve, 1)

                def turned(n):
                    dve.wait_ge(qk_copied, upto(qk_copied, l, 2 * n + 1))
                    if n:
                        dve.wait_ge(ro_done, upto(ro_done, l, n))
                    nc.vector.tensor_tensor(qxT[:], bank[:, 2, :].rearrange("p (a c) -> p a c", a=4), xi,
                                            ALU.mult).then_inc(qx_ready, 1)
                    if n < T - 1:
                        if n:
                            dve.wait_ge(kv_done, upto(kv_done, l, n))
                        else:
                            dve.wait_ge(rv_ready, upto(rv_ready, l, 4))
                        nc.vector.tensor_tensor(vz[:].rearrange("p (h e) -> p h e", h=RH),
                                                rv[:, n, :].rearrange("p (h e) -> p h e", h=RH),
                                                zeta.unsqueeze(2).broadcast_to([P, RH, DK]), ALU.mult)\
                            .then_inc(vz_ready, 1)

                def mask_scores(n):
                    if n:
                        dve.wait_ge(ro_done, upto(ro_done, l, n))
                    for a in range(2):
                        dve.wait_ge(st_done, upto(st_done, l, 2 * n + a + 1))
                        nc.vector.tensor_tensor(stm[:, a:RH:2, :],
                                                bank[:, 4 + a, :].rearrange("p (h c) -> p h c", h=4),
                                                dmask[:, a:RH:2, :], ALU.mult).then_inc(st_masked, 1)

                def states(n):
                    if n == T - 1:
                        return
                    dve.wait_ge(kv_done, upto(kv_done, l, n + 1))
                    kv = bank[:, 7, :].rearrange("p (a c) -> p a c", a=4)
                    bd = bdiag.unsqueeze(1).broadcast_to([P, 4, P])
                    if n == 0:
                        nc.vector.tensor_tensor(state[:], kv, bd, ALU.mult).then_inc(state_step, 1)
                        return
                    at = 3 * n - 2
                    dve.wait_ge(state_step, upto(state_step, l, at))
                    nc.vector.tensor_tensor(kvt[:], kv, bd, ALU.mult).then_inc(state_step, 1)
                    dve.wait_ge(ro_done, upto(ro_done, l, n + 1))
                    nc.vector.tensor_tensor(state[:], state[:], decay.unsqueeze(2).broadcast_to([P, 4, P]),
                                            ALU.mult).then_inc(state_step, 1)
                    dve.wait_ge(state_step, upto(state_step, l, at + 2))
                    nc.vector.tensor_tensor(state[:], state[:], kvt[:], ALU.add).then_inc(state_step, 1)

                def head_norms(n):
                    dve.wait_ge(osq_ready, upto(osq_ready, l, n + 1))
                    if n:
                        dve.wait_ge(rstd_step, upto(rstd_step, l, RS_RET(n - 1) + 1))
                    nc.vector.reduce_sum(head_ms[:], osq[:].rearrange("p (h e) -> p h e", h=RH), AXX)\
                        .then_inc(head_sum, 1)

                def outputs(n):
                    dve.wait_ge(rstd_step, upto(rstd_step, l, RS_RET(n) + 2))
                    y = qr[:, n, :].rearrange("p (h e) -> p h e", h=RH)
                    nc.vector.tensor_tensor(y, bank[:, 6, :].rearrange("p (h e) -> p h e", h=RH),
                                            head_rstd[:].unsqueeze(2).broadcast_to([P, RH, DK]), ALU.mult)\
                        .then_inc(y_step, 1)
                    dve.wait_ge(y_step, upto(y_step, l, 2 * n + 1))
                    nc.vector.tensor_tensor(qr[:, n, :], qr[:, n, :], sg[:, n, :], ALU.mult).then_inc(y_step, 1)

                def z_build(s):
                    if s == 0:
                        nc.vector.memset(zf[:, :, :, NC:NCP], 0.0).then_inc(z_step, 1)
                    else:
                        dve.wait_ge(z_l, upto(z_l, l, 1))
                    chunk_used(dve, l, C_F0 + s)
                    for half in range(2):
                        rows = slice(half * DH, (half + 1) * DH)
                        for g in range(NKV):
                            src = bank[g * DH:(g + 1) * DH, s, :].rearrange("p (c m a) -> p m a c", m=8, a=2)
                            for m8 in range(2):
                                pos = par[rows, Q_POS + 16 * s + 8 * m8:Q_POS + 16 * s + 8 * m8 + 8]
                                nc.vector.tensor_tensor(
                                    zf[rows, 8 * m8:8 * m8 + 8, g, 0:NC], src[:, :, half, m8:m8 + NC],
                                    pos.unsqueeze(2).broadcast_to([DH, 8, NC]), ALU.add).then_inc(z_step, 1)

                def z_rest(s):
                    dve.wait_ge(z_step, upto(z_step, l, 1 + 8 * (s + 1)))
                    dve.wait_ge(z_h, upto(z_h, l, s + 1))
                    minus(z_lo[:], zf[:].rearrange("p m g c -> p (m g c)"), r32(z_hi[:])).then_inc(z_l, 1)

                dve.wait_ge(par_loaded, upto(par_loaded, l, 48))
                for what, n in MIDDLE:
                    if what == "turn":
                        turned(n)
                    if what == "score":
                        mask_scores(n)
                    if what == "out":
                        states(n)
                        head_norms(n)
                    if what == "norm":
                        outputs(n)
                    if what == "chunk" and n == C_F0:
                        z_build(0)
                        z_rest(0)
                    if what == "chunk" and n == C_F1:
                        z_build(1)
                    if what == "chunk" and n == C_W1K + 3:
                        z_rest(1)
                dve.wait_ge(vc_done, upto(vc_done, l, 1))
                nc.vector.tensor_tensor(vcf[:], bank[0:NCP, 7, 0:NKV * DH].rearrange("p (g d) -> p g d", g=NKV),
                                        b2v[:].unsqueeze(1).broadcast_to([NCP, NKV, DH]), ALU.add)\
                    .then_inc(vc_f, 1)
                dve.wait_ge(kc_h, upto(kc_h, l, 2))
                for half in range(2):
                    minus(KcL[half * DH:(half + 1) * DH, :], kcf[:], r32(KcH[0:DH, :])).then_inc(kc_l, 1)
                dve.wait_ge(vc_h, upto(vc_h, l, 1))
                minus(VcS[:, :, DH:2 * DH], vcf[:], r32(VcS[:, :, 0:DH])).then_inc(vc_l, 1)
                for f in range(2):
                    for g in range(NKV):
                        for half in range(2):
                            if g + half == 0:
                                dve.wait_ge(k_h, upto(k_h, l, 4 * (f + 1)))
                            rows = slice(half * DH, (half + 1) * DH)
                            minus(KL[rows, 2 * f + g, :], bank[g * DH:(g + 1) * DH, 2 + f, :],
                                  r32(KH[rows, 2 * f + g, :])).then_inc(k_l, 1)
                for f in range(4):
                    for m in range(2):
                        if m == 0:
                            dve.wait_ge(q_h, upto(q_h, l, 2 * (f + 1)))
                        minus(QS[(1 - m) * DH:(2 - m) * DH, 2 * f + m, :], bank[m * DH:(m + 1) * DH, f % 2, :],
                              r32(QS[m * DH:(m + 1) * DH, 2 * f + m, :])).then_inc(q_l, 1)
                def y_rest(n):
                    dve.wait_ge(y_h, upto(y_h, l, n + 1))
                    minus(act_lo[:, 0:4, n * P:(n + 1) * P], bank[:, Y_BANK[n], :].rearrange("p (k c) -> p k c", k=4),
                          r32(act_hi[:, 0:4, n * P:(n + 1) * P])).then_inc(y_l, 1)

                for n in range(T):
                    y_rest(n)

                def maxima(n, p):
                    i = UNITS[n][0]
                    heads = slice(2 * p, 2 * p + 2)
                    dve.wait_ge(s_done, upto(s_done, l, 2 * n + p + 1))
                    nc.vector.reduce_max(s_max[:, n % EB, heads], bank[:, heads, 0:P * (i + 1)], AXX)\
                        .then_inc(m_step, 1)
                    dve.wait_ge(m_step, upto(m_step, l, 4 * n + 2 * p + 1))
                    if n >= EB:
                        dve.wait_ge(e_done, upto(e_done, l, G * (n - EB) + 2 * p + 2))
                    nc.vector.tensor_scalar(s_bias[:, n % EB, heads], s_max[:, n % EB, heads], NEG_GUARD, -SM,
                                            ALU.max, ALU.mult).then_inc(m_step, 1)

                def factors(n, p):
                    i, g, b = UNITS[n]
                    at = 6 * n + 3 * p
                    dve.wait_ge(e_done, upto(e_done, l, G * n + 2 * p + 2))
                    if n >= EB:
                        dve.wait_ge(p_scaled, upto(p_scaled, l, G * (n - EB) + 2 * p + 2))
                    rec = s_rec[:, n % EB, 2 * p:2 * p + 2]
                    nc.vector.tensor_scalar(rec, s_sum[:, n % EB, 2 * p:2 * p + 2], 1e-30, None, ALU.max)\
                        .then_inc(r_step, 1)
                    dve.wait_ge(r_step, upto(r_step, l, at + 1))
                    nc.vector.reciprocal(rec, rec).then_inc(r_step, 1)
                    dve.wait_ge(r_step, upto(r_step, l, at + 2))
                    gs = gate[:, i, :].rearrange("p (h b) -> p h b", b=3)[:, G * g + 2 * p:G * g + 2 * p + 2, b + 1]
                    nc.vector.tensor_tensor(rec, rec, gs, ALU.mult).then_inc(r_step, 1)

                def p_rest(k):
                    rows = NCP if ITEMS[k][0] is None else P
                    dve.wait_ge(pth, upto(pth, l, k + 1))
                    minus(pt_l[0:rows, k % 2, :], bank[0:rows, 4 + k % 2, :], r32(pt_h[0:rows, k % 2, :]))\
                        .then_inc(ptl, 1)

                def out_sum(v):
                    i, g = v // NKV, v % NKV
                    dve.wait_ge(oa_done, upto(oa_done, l, v + 1))
                    if v:
                        dve.wait_ge(ol_done, upto(ol_done, l, v))
                    for m in range(2):
                        view = lambda ap: ap.rearrange("p (a b c) -> p a b c", a=2, b=2)[:, :, m, :]
                        nc.vector.tensor_tensor(o_f[m * DH:(m + 1) * DH, :, :],
                                                view(bank[DH:P, 6 + v % 2, :]), view(o_a[:]), ALU.add)\
                            .then_inc(of_done, 1)

                NR = T * NKV * G

                def compressed_maxima(a):
                    dve.wait_ge(cs_done, upto(cs_done, l, a + 1))
                    nc.vector.reduce_max(c_stat[:, a * 16:a * 16 + 16],
                                         bank[:, 6 + a, :].rearrange("p (r c) -> p r c", c=NCP), AXX)\
                        .then_inc(c_step, 1)

                maxima(0, 0)
                maxima(0, 1)
                factors(0, 0)
                compressed_maxima(0)
                factors(0, 1)
                maxima(1, 0)
                compressed_maxima(1)
                dve.wait_ge(c_step, upto(c_step, l, 2))
                nc.vector.tensor_scalar(c_stat[:], c_stat[:], NEG_GUARD, None, ALU.max).then_inc(c_step, 1)
                maxima(1, 1)
                dve.wait_ge(c_step, upto(c_step, l, 3))
                for a in range(2):
                    last = nc.vector.tensor_tensor(
                        cE[:, a * 16:a * 16 + 16, :], bank[:, 6 + a, :].rearrange("p (r c) -> p r c", c=NCP),
                        c_stat[:, a * 16:a * 16 + 16].unsqueeze(2).broadcast_to([P, 16, NCP]), ALU.subtract)
                last.then_inc(c_step, 1)
                factors(1, 0)
                factors(1, 1)
                dve.wait_ge(c_exp, upto(c_exp, l, 1))
                nc.vector.reduce_sum(c_rec[:], cE[:], AXX).then_inc(c_step, 1)
                dve.wait_ge(c_step, upto(c_step, l, 5))
                nc.vector.tensor_scalar(c_rec[:], c_rec[:], 1e-30, None, ALU.max).then_inc(c_step, 1)
                dve.wait_ge(c_step, upto(c_step, l, 6))
                nc.vector.reciprocal(c_rec[:], c_rec[:]).then_inc(c_step, 1)
                dve.wait_ge(c_step, upto(c_step, l, 7))
                nc.vector.tensor_tensor(c_rec[:].rearrange("p (t h) -> p t h", t=T),
                                        c_rec[:].rearrange("p (t h) -> p t h", t=T),
                                        gate[:].rearrange("p t (h b) -> p t h b", b=3)[:, :, :, 0], ALU.mult)\
                    .then_inc(c_step, 1)
                dve.wait_ge(c_step, upto(c_step, l, 8))
                nc.vector.tensor_tensor(cE[:], cE[:], c_rec[:].unsqueeze(2).broadcast_to([P, NR, NCP]),
                                        ALU.mult).then_inc(c_step, 1)
                for n in range(NU):
                    for k in UNIT_ITEMS[n]:
                        for unit, p in pairs_at(k - 2):
                            factors(unit, p)
                        p_rest(k)
                        for unit, p in pairs_at(k):
                            maxima(unit, p)
                        if k - 2 in LAST_OF_V.values():
                            out_sum(ITEMS[k - 2][1])
                out_sum(T * NKV - 1)

                for what, t in MID_NORMS:
                    if what == "post":
                        add_branch(l, 3 * t, t, g_rest[:, 0, :], RS_MID[what, t], 4 * t + 1)
                    else:
                        dve.wait_ge(x_step, upto(x_step, l, 3 * t + 3))
                        normalise(l, 4 + t, t, g_rest[:, 1, :], RS_MID[what, t], 4 * t + 2)
                        if t:
                            act_rests(l, 4 + t - 1, t - 1)
                act_rests(l, 4 + T - 1, T - 1)

                taps = par[:, Q_CV:Q_CV + 8 * KF].rearrange("p (n q) -> p n q", q=4)
                with dve.Fori(0, KF // 2) as it:
                    for p in range(2):
                        for s in range(2):
                            col = it * 2 + (s * KF + p)
                            y = cv[:, p, s, :]
                            u = bank[:, 2 * p + s, :]
                            dve.wait_ge(cv0, l * (2 * KF) + it * 4 + (2 * p + s + 1))
                            nc.vector.scalar_tensor_tensor(
                                out=y[:, 1:SEQ], in0=u[:, 0:SEQ - 1], scalar=taps[:, bass.ds(col, 1), 1],
                                in1=y[:, 1:SEQ], op0=ALU.mult, op1=ALU.add).then_inc(cv_step, 1)
                            dve.wait_ge(cv_step, l * (4 * KF) + it * 8 + (4 * p + 2 * s + 1 + AHEAD))
                            nc.vector.scalar_tensor_tensor(
                                out=y[:, 2:SEQ], in0=u[:, 0:SEQ - 2], scalar=taps[:, bass.ds(col, 1), 0],
                                in1=y[:, 2:SEQ], op0=ALU.mult, op1=ALU.add).then_inc(cv_step, 1)
                        dve.wait_ge(cv_step, l * (4 * KF) + it * 8 + (4 * p + 4 + AHEAD))
                        dve.wait_ge(gelu_done, l * KF + it * 2 + (p + 1))
                        nc.vector.tensor_tensor(gff[:, bass.ds(it * 2 + p, 1), :].rearrange("p a c -> p (a c)"),
                                                cv[:, p, 0, :], cv[:, p, 1, :], ALU.mult).then_inc(g_ready, 1)
                for k in range(KF):
                    dve.wait_ge(gh, upto(gh, l, k + 1))
                    minus(act_lo[:, k % KD, :], gff[:, k, :], r32(act_hi[:, k % KD, :])).then_inc(gl, 1)
                for t in range(T):
                    add_branch(l, 12 + 3 * t, t, g_rest[:, 2, :], RS_POST2(t), 4 * t + 3)

        @block.tensor
        def _(pe):
            mm = nc.tensor.matmul

            def arrived(layer, c):
                pe.wait_ge(lo_ready, upto(lo_ready, layer, c + 1))

            def passes(a, b):
                return ((a[0], b[0]), (a[0], b[1]), (a[1], b[0]))

            def turn_h(layer, n, t):
                pe.wait_ge(h_ready, upto(h_ready, layer, n + 1))
                for k in range(KD):
                    last = nc.tensor.transpose(bank[:, t + 4 * (k // 4), (k % 4) * P:(k % 4 + 1) * P],
                                               h[:, t % 2, k * P:(k + 1) * P], ident)
                last.then_inc(h_turned, 1)

            def token_block(layer, first, width, b0, done, before, by_tile=False, turn=None):
                order = [(c, t) for t in range(T) for c in range(4)] if by_tile else \
                        [(c, t) for c in range(4) for t in range(T)]
                for c, t in order:
                    if c == 0 and turn:
                        turn(t)
                    arrived(layer, first + c)
                    if c == 0:
                        before(t)
                    for kk in range(2):
                        k = 2 * c + kk
                        s = (first + c) % RING
                        cols = slice(kk * width, (kk + 1) * width)
                        rows = (act_hi[:, k, t * P:(t + 1) * P], act_lo[:, k, t * P:(t + 1) * P])
                        w = (w_hi[:, s, cols], w_lo[:, s, cols])
                        for n, (a, b) in enumerate(passes(rows, w)):
                            last = mm(bank[:, b0 + t, 0:width], a, b, start=(k == 0 and n == 0),
                                      stop=(k == KD - 1 and n == 2))
                    if t == T - 1:
                        last.then_inc(w_used, 1)
                    elif c == 3:
                        last.then_inc(done, 1)

            def feature_tile(layer, c, b):
                s = c % RING
                arrived(layer, c)
                for k in range(KD):
                    cols = slice(k * P, (k + 1) * P)
                    for n, (a, v) in enumerate(passes((w_hi[:, s, cols], w_lo[:, s, cols]),
                                                      (act_hi[:, k, :], act_lo[:, k, :]))):
                        last = mm(bank[:, b, :], a, v, start=(k == 0 and n == 0), stop=(k == KD - 1 and n == 2))
                last.then_inc(w_used, 1)

            pe.sem_inc(w_used, RING)
            pe.wait_ge(const_loaded, 16 * (1 + T))
            pe.wait_ge(const_cast, 3)
            with pe.Fori(0, DEPTH) as l:
                def turn_pre1(t):
                    pe.wait_ge(x_step, upto(x_step, l, 3 * (t + 1) - 12))
                    turn_h(l, t, t)

                turn_pre1(0)
                def before_t(blk):
                    def f(t):
                        if blk == 0:
                            pe.wait_ge(act_l, upto(act_l, l, 2 * t + 2))
                        if blk == 1:
                            pe.wait_ge(act_l, upto(act_l, l, 8))
                        if blk == 2:
                            pe.wait_ge(rot_step, upto(rot_step, l, 4 * t + 3))
                        if blk == 3:
                            pe.wait_ge(rot_step, upto(rot_step, l, 16 + 4 * t + 3))
                        if blk == 4:
                            pe.wait_ge(rv_ready, upto(rv_ready, l, t + 1))
                    return f
                token_block(l, C_T, 512, 4, t_done, before_t(0), by_tile=True,
                            turn=lambda t: turn_pre1(t + 1) if t + 1 < T else None)
                for blk in range(1, 4):
                    token_block(l, C_T + 4 * blk, 512, 4 if blk % 2 == 0 else 0, t_done, before_t(blk))
                token_block(l, C_TV, NTV, 4, t_done, before_t(4))

                def turn_qk(n):
                    pe.wait_ge(sg_ready, upto(sg_ready, l, 4))
                    if n:
                        pe.wait_ge(qk_copied, upto(qk_copied, l, 2 * n))
                        pe.wait_ge(qx_ready, upto(qx_ready, l, n))
                    else:
                        pe.wait_ge(rot_step, upto(rot_step, l, 32))
                    for m, src in ((0, qr), (1, kr)):
                        for a in range(4):
                            last = nc.tensor.transpose(bank[:, 2 + m, a * P:(a + 1) * P],
                                                       src[:, n, a * P:(a + 1) * P], ident)
                        last.then_inc(qk_turned, 1)

                def scores(n):
                    pe.wait_ge(qk_copied, upto(qk_copied, l, 2 * n + 2))
                    if n:
                        pe.wait_ge(st_masked, upto(st_masked, l, 2 * n))
                    else:
                        pe.wait_ge(vg_dve, upto(vg_dve, l, 8))
                    for hd in range(RH):
                        rows = slice((hd % 2) * DK, (hd % 2 + 1) * DK)
                        last = mm(bank[:, 4 + hd % 2, (hd // 2) * P:(hd // 2 + 1) * P],
                                  kT[rows, hd // 2, :], qT[rows, hd // 2, :], start=True, stop=True)
                        if hd >= RH - 2:
                            last.then_inc(st_done, 1)

                def ret_out(n):
                    if n:
                        pe.wait_ge(state_step, upto(state_step, l, 3 * n - 2))
                    if n < T - 1:
                        pe.wait_ge(vz_ready, upto(vz_ready, l, n + 1))
                        for a in range(4):
                            last = mm(bank[:, 7, a * P:(a + 1) * P], kr[:, n, a * P:(a + 1) * P],
                                      vz[:, a * P:(a + 1) * P], start=True, stop=True)
                        last.then_inc(kv_done, 1)
                    pe.wait_ge(rv_ready, upto(rv_ready, l, n + 1))
                    pe.wait_ge(st_masked, upto(st_masked, l, 2 * n + 2))
                    pe.wait_ge(qx_ready, upto(qx_ready, l, n + 1))
                    if n:
                        pe.wait_ge(y_step, upto(y_step, l, 2 * n - 1))
                    for a in range(4):
                        if n:
                            mm(bank[:, 6, a * P:(a + 1) * P], qxT[:, a, :], state[:, a, :], start=True,
                               stop=False, skip_group_check=True)
                        for m in range(2):
                            hd = 2 * a + m
                            last = mm(bank[:, 6, hd * DK:(hd + 1) * DK], stm[:, hd, :],
                                      rv[:, n, hd * DK:(hd + 1) * DK], start=(n == 0), stop=True,
                                      skip_group_check=True)
                    last.then_inc(ro_done, 1)

                def first_layer(s, c):
                    j = c - (C_W1K, C_W1V)[s]
                    arrived(l, c)
                    if j == 0:
                        pe.wait_ge(z_l, upto(z_l, l, s + 1))
                        if s == 0:
                            pe.wait_ge(z_step, upto(z_step, l, 17))
                        else:
                            pe.wait_ge(hid_ready, upto(hid_ready, l, 2))
                    for m in range(2):
                        for kk in range(4):
                            k = 4 * j + kk
                            cols = slice(kk * HID + m * P, kk * HID + (m + 1) * P)
                            zc = slice(k * NKV * NCP, (k + 1) * NKV * NCP)
                            for n, (a, v) in enumerate(passes((w_hi[:, c % RING, cols], w_lo[:, c % RING, cols]),
                                                              (z_hi[:, zc], z_lo[:, zc]))):
                                last = mm(bank[:, m, 0:NKV * NCP], a, v,
                                          start=(k == 0 and n == 0), stop=(k == 15 and n == 2))
                        if j == 3 and m == 0:
                            last.then_inc(w1_done, 1)
                    last.then_inc(w_used, 1)

                for what, n in MIDDLE:
                    if what == "turn":
                        turn_qk(n)
                    if what == "score":
                        scores(n)
                    if what == "out":
                        ret_out(n)
                    if what == "chunk":
                        if n <= C_F1:
                            feature_tile(l, n, n - C_F0)
                        elif n < C_W1V:
                            first_layer(0, n)
                        else:
                            first_layer(1, n)
                pe.wait_ge(par_loaded, upto(par_loaded, l, 48))
                pe.wait_ge(hid_ready, upto(hid_ready, l, 4))
                pe.wait_ge(y_step, upto(y_step, l, 7))
                w2 = par[:, Q_W2:Q_B2K].rearrange("p (s m d) -> p s m d", s=2, m=2)
                for m in range(2):
                    last = mm(bank[0:DH, 6, 0:NKV * NCP], w2[:, 0, m, :], hid[:, 0, m, :], start=(m == 0), stop=(m == 1))
                last.then_inc(kc_done, 1)
                for g in range(NKV):
                    for m in range(2):
                        last = mm(bank[0:NCP, 7, g * DH:(g + 1) * DH], hid[:, 1, m, g * NCP:(g + 1) * NCP],
                                  w2[:, 1, m, :], start=(m == 0), stop=(m == 1))
                last.then_inc(vc_done, 1)
                for f in range(6):
                    if f < 2:
                        pe.wait_ge(qk_copied, upto(qk_copied, l, 8))
                        pe.wait_ge(qx_ready, upto(qx_ready, l, 4))
                    elif f < 4:
                        pe.wait_ge(hid_ready, upto(hid_ready, l, 4))
                    else:
                        pe.wait_ge(q_l, upto(q_l, l, 2 * (f - 3)))
                    feature_tile(l, C_F2 + f, 2 + f if f < 2 else f % 2)
                pe.wait_ge(st_masked, upto(st_masked, l, 8))
                pe.wait_ge(y_step, upto(y_step, l, 8))
                pe.wait_ge(k_l, upto(k_l, l, 8))
                for n in range(T):
                    for a in range(4):
                        last = nc.tensor.transpose(bank[:, Y_BANK[n], a * P:(a + 1) * P],
                                                   qr[:, n, a * P:(a + 1) * P], ident)
                    last.then_inc(y_turned, 1)
                def compressed_scores(a):
                    pe.wait_ge(kc_l, upto(kc_l, l, 2))
                    pe.wait_ge(vc_f, upto(vc_f, l, 1))
                    mask = cmask_b[:, 2 * a * NCP:(2 * a + 2) * NCP].rearrange("p (t c) -> p t c", t=2)
                    mm(bank[:, 6 + a, :], ident_b[:], mask.unsqueeze(2).broadcast_to([P, 2, NH, NCP]),
                       start=True, stop=False, skip_group_check=True)
                    for t2 in range(2):
                        for hd in range(NH):
                            g = hd // G
                            at = (t2 * NH + hd) * NCP
                            q = QS[:, hd, (2 * a + t2) * P:(2 * a + t2 + 1) * P]
                            for m, key in enumerate((KcH, KcL)):
                                last = mm(bank[:, 6 + a, at:at + NCP], q, key[:, g * NCP:(g + 1) * NCP],
                                          start=False, stop=(m == 1), skip_group_check=True)
                    last.then_inc(cs_done, 1)

                def pair_scores(n, p):
                    i, g, b = UNITS[n]
                    if n:
                        pe.wait_ge(e_done, upto(e_done, l, G * (n - 1) + 2 * p + 2))
                    elif p == 0:
                        pe.wait_ge(q_l, upto(q_l, l, 8))
                    else:
                        pe.wait_ge(y_l, upto(y_l, l, 4))
                    for r in (2 * p, 2 * p + 1):
                        q = QS[:, G * g + r, i * P:(i + 1) * P]
                        dst = bank[:, r, 0:P * (i + 1)]
                        mm(bank[:, r, P * i:P * (i + 1)], ident_b[:], causal_b[:], start=True, stop=False,
                           skip_group_check=True)
                        mm(dst, q, KH[:, 2 * b + g, 0:P * (i + 1)], start=False, stop=False, skip_group_check=True)
                        last = mm(dst, q, KL[:, 2 * b + g, 0:P * (i + 1)], start=False, stop=True,
                                  skip_group_check=True)
                    last.then_inc(s_done, 1)

                def turn_p(k):
                    n, v, j = ITEMS[k]
                    if k >= 2:
                        pe.wait_ge(ptl, upto(ptl, l, k - 1))
                    else:
                        pe.wait_ge(y_l, upto(y_l, l, 4))
                    if n is None:
                        pe.wait_ge(c_step, upto(c_step, l, 9))
                        for r in range(G):
                            last = nc.tensor.transpose(bank[0:NCP, 4 + k % 2, r * P:(r + 1) * P],
                                                       cE[:, v * G + r, :], ident)
                    else:
                        for r in range(G):
                            if j == 0:
                                pe.wait_ge(p_scaled, upto(p_scaled, l, G * n + r + 1))
                            last = nc.tensor.transpose(bank[:, 4 + k % 2, r * P:(r + 1) * P],
                                                       E[:, n % EB, r, j * P:(j + 1) * P], ident)
                    last.then_inc(pt_done, 1)

                def product(k):
                    n, v, j = ITEMS[k]
                    first = k == FIRST_OF_V[v]
                    o = bank[:, 6 + v % 2, :]
                    if first:
                        if v >= 2:
                            pe.wait_ge(of_done, upto(of_done, l, 2 * (v - 1)))
                        else:
                            pe.wait_ge(c_step, upto(c_step, l, 4))
                    if n is None:
                        pe.wait_ge(vc_l, upto(vc_l, l, 1))
                        g = v % NKV
                        w, rows = VcS[:, g, :], NCP
                    else:
                        i, g, b = UNITS[n]
                        w, rows = VS[:, j, 2 * b + g, :], P
                    pe.wait_ge(ptl, upto(ptl, l, k + 1))
                    mm(o, w, pt_h[0:rows, k % 2, :], start=first, stop=False)
                    mm(o, w, pt_l[0:rows, k % 2, :], start=False, stop=(k == LAST_OF_V[v])).then_inc(pv_done, 1)

                for n in range(2):
                    for p in range(2):
                        pair_scores(n, p)
                        if n == 0:
                            compressed_scores(p)
                for n in range(NU):
                    for k in UNIT_ITEMS[n]:
                        turn_p(k)
                        for unit, p in pairs_at(k):
                            pair_scores(unit, p)
                        if k:
                            product(k - 1)
                product(NI - 1)

                for half in range(2):
                    def before(t, half=half):
                        if half == 0 and t == 0:
                            pe.wait_ge(ol_done, upto(ol_done, l, T * NKV))
                            pe.wait_ge(e_done, upto(e_done, l, G * NU))
                            pe.wait_ge(ptl, upto(ptl, l, NI))
                    def turn_done(t):
                        if t == T - 1:
                            pe.wait_ge(x_step, upto(x_step, l, 2))
                            turn_h(l, 4, 0)
                    token_block(l, C_WO + 4 * half, 512, 4 * half, wo_done, before, by_tile=(half == 1),
                                turn=turn_done if half else None)
                for t in range(1, T):
                    pe.wait_ge(x_step, upto(x_step, l, 3 * t + 2))
                    turn_h(l, 4 + t, t)
                with pe.Fori(0, KF // 2) as it:
                    for s in range(RING):
                        pe.wait_ge(act_l, upto(act_l, l, 16))
                        pe.wait_ge(lo_ready, l * NCH + it * RING + (C_UP + s + 1 + RING))
                        pe.wait_ge(cv_step, l * (4 * KF) + it * 8 + (2 * s + 2))
                        for k in range(KD):
                            cols = slice(k * P, (k + 1) * P)
                            for n, (a, v) in enumerate(passes((w_hi[:, s, cols], w_lo[:, s, cols]),
                                                              (act_hi[:, k, :], act_lo[:, k, :]))):
                                last = mm(bank[:, s, :], a, v, start=(k == 0 and n == 0),
                                          stop=(k == KD - 1 and n == 2))
                        last.then_inc(w_used, 1)
                pe.wait_ge(cv_step, upto(cv_step, l, 4 * KF))
                head = [(k, t) for k in range(KF - RING) for t in range(T)]
                tail = [(k, t) for t in range(T) for k in range(KF - RING, KF)]
                for k, t in head + tail:
                    s = (C_DN + k) % RING
                    if t == 0:
                        arrived(l, C_DN + k)
                        pe.wait_ge(gl, upto(gl, l, k + 1))
                    rows = (act_hi[:, k % KD, t * P:(t + 1) * P], act_lo[:, k % KD, t * P:(t + 1) * P])
                    for half in range(2):
                        cols = slice(512 * half, 512 * half + 512)
                        for n, (a, b) in enumerate(passes(rows, (w_hi[:, s, cols], w_lo[:, s, cols]))):
                            last = mm(bank[:, t + 4 * half, :], a, b, start=(k == 0 and n == 0),
                                      stop=(k == KF - 1 and n == 2))
                    if t == T - 1:
                        last.then_inc(w_used, 1)
                    elif k == KF - 1:
                        last.then_inc(dn_done, 1)


def _constants():
    f = np.float32
    out = np.zeros((P, NCONST), f)
    inv = f(1.0) / f(10000.0) ** np.linspace(0.0, 1.0, DK // 2, dtype=f)
    ang = (np.arange(SEQ, dtype=f)[:, None] * inv[None, :]).astype(f)
    tab = lambda a: a.astype(f).reshape(T, P, DK // 2).transpose(1, 0, 2).reshape(P, -1)
    out[:, O_COS:O_SIN], out[:, O_SIN:O_NSIN], out[:, O_NSIN:O_DM] = tab(np.cos(ang)), tab(np.sin(ang)), tab(-np.sin(ang))
    log_g = np.log(f(1.0) - f(2.0) ** (f(-5.0) - np.arange(RH, dtype=f))).astype(f)
    i = np.arange(P, dtype=f)
    diff = i[None, :] - i[:, None]
    scale = f(DK ** -0.5)
    dm = np.where(diff >= 0, np.exp(np.maximum(diff, 0)[None] * log_g[:, None, None]), 0).astype(f)
    out[:, O_DM:O_XI] = (dm * scale).transpose(1, 0, 2).reshape(P, -1)
    xi = np.exp((i + 1)[None, :] * log_g[:, None]).astype(f)
    out[:, O_XI:O_ZE] = np.repeat(xi.reshape(4, 2, 1, P), DK, axis=2).reshape(4, P, P).transpose(1, 0, 2).reshape(P, -1)
    out[:, O_ZE:O_BD] = np.exp((P - 1 - i)[:, None] * log_g[None, :])
    out[:DK, O_BD:O_BD + DK] = scale
    out[DK:, O_BD + DK:O_DE] = scale
    out[:, O_DE:O_ID] = np.repeat(np.exp(P * log_g).astype(f).reshape(4, 2), DK, axis=1).T
    out[:, O_ID:O_CA] = np.eye(P, dtype=f)
    out[:, O_CA:O_CM] = np.where(np.arange(P)[None, :] <= np.arange(P)[:, None], 0, NEG)
    tok = np.arange(SEQ).reshape(T, P).T[:, :, None]
    c = np.arange(NCP)[None, None, :]
    out[:, O_CM:] = np.where((c < NC) & (c * CS + CB - 1 <= tok), 0, NEG).reshape(P, -1)
    return out


def _stream(w_in, w_out, kw1, vw1, w_up, w_down):
    st = np.zeros((DEPTH, NCH, P, CW), np.float32)

    def token(c0, w):
        n = w.shape[-1]
        st[:, c0:c0 + 4, :, :2 * n] = w.reshape(DEPTH, 4, 2, P, n).transpose(0, 1, 3, 2, 4).reshape(DEPTH, 4, P, 2 * n)

    def feature(c, w):
        st[:, c] = w.reshape(DEPTH, KD, P, P).transpose(0, 2, 1, 3).reshape(DEPTH, P, CW)

    r = RH * DK
    for b in range(4):
        token(C_T + 4 * b, w_in[:, :, b * r:(b + 1) * r])
    nq, kv = 4 * r, 4 * r + NH * DH
    col = lambda s: w_in[:, :, kv + s * NKV * DH:kv + (s + 1) * NKV * DH]
    token(C_TV, np.concatenate([col(3), col(5), w_in[:, :, kv + 6 * NKV * DH:]], axis=-1))
    feature(C_F0, col(0))
    feature(C_F1, col(1))
    for c0, w in ((C_W1K, kw1), (C_W1V, vw1)):
        st[:, c0:c0 + 4] = w.reshape(DEPTH, 4, 4, P, HID).transpose(0, 1, 3, 2, 4).reshape(DEPTH, 4, P, CW)
    feature(C_F2, col(2))
    feature(C_F2 + 1, col(4))
    for f in range(4):
        feature(C_F2 + 2 + f, w_in[:, :, nq + f * P:nq + (f + 1) * P])
    for half in range(2):
        token(C_WO + 4 * half, w_out[:, :, half * 512:(half + 1) * 512])
    for n in range(KF):
        feature(C_UP + 2 * n, w_up[:, :, n * P:(n + 1) * P])
        feature(C_UP + 2 * n + 1, w_up[:, :, FF + n * P:FF + (n + 1) * P])
    st[:, C_DN:] = w_down.reshape(DEPTH, KF, P, D)
    return st


def _parameters(kpos, vpos, kb1, vb1, kw2, vw2, kb2, conv_w, conv_b):
    out = np.zeros((DEPTH, P, NPAR), np.float32)
    for s, pos in enumerate((kpos, vpos)):
        out[:, :, Q_POS + 16 * s:Q_POS + 16 * s + 16] = pos.reshape(DEPTH, 16, P).transpose(0, 2, 1)
    for s, b in enumerate((kb1, vb1)):
        out[:, :, Q_B1 + 2 * s:Q_B1 + 2 * s + 2] = b.reshape(DEPTH, 2, P).transpose(0, 2, 1)
    for s, w in enumerate((kw2, vw2)):
        out[:, :, Q_W2 + 2 * DH * s:Q_W2 + 2 * DH * (s + 1)] = w.reshape(DEPTH, 2, P, DH).transpose(0, 2, 1, 3).reshape(DEPTH, P, -1)
    out[:, :DH, Q_B2K] = kb2
    taps = np.concatenate([conv_w, conv_b[:, None]], axis=1)
    out[:, :, Q_CV:] = taps.reshape(DEPTH, 4, 2 * KF, P).transpose(0, 3, 2, 1).reshape(DEPTH, P, -1)
    return out


def kernel(x, ln_mix_pre, ln_mix_post, ln_ffn_pre, ln_ffn_post, w_in, w_out, cmp_k_pos, cmp_k_w1, cmp_k_b1,
           cmp_k_w2, cmp_k_b2, cmp_v_pos, cmp_v_w1, cmp_v_b1, cmp_v_w2, cmp_v_b2, ffn_w_up, ffn_conv_w,
           ffn_conv_b, ffn_w_down):
    import concourse.bacc as bacc
    from concourse.bass_utils import run_bass_kernel_spmd

    a = lambda v: np.asarray(v)
    gains = np.zeros((DEPTH + 1, 2, 3 * D), np.float32)
    gains[:DEPTH, 0, :D] = a(ln_mix_pre)
    gains[:DEPTH, 1, :D], gains[:DEPTH, 1, D:2 * D] = a(ln_mix_post), a(ln_ffn_pre)
    gains[:DEPTH, 1, 2 * D:] = a(ln_ffn_post)
    arrays = {
        "x_in": a(x).reshape(SEQ, D),
        "wstream": _stream(a(w_in), a(w_out), a(cmp_k_w1), a(cmp_v_w1), a(ffn_w_up), a(ffn_w_down)),
        "gains": gains,
        "pars": _parameters(a(cmp_k_pos), a(cmp_v_pos), a(cmp_k_b1), a(cmp_v_b1), a(cmp_k_w2), a(cmp_v_w2),
                            a(cmp_k_b2), a(ffn_conv_w), a(ffn_conv_b)),
        "b2v_in": a(cmp_v_b2).reshape(DEPTH, 1, DH),
        "consts": _constants(),
    }
    nc = bacc.Bacc("TRN2", target_bir_lowering=False, num_devices=1)
    args = {n: nc.dram_tensor(n, v.shape, mybir.dt.from_np(v.dtype), kind="ExternalInput").ap()
            for n, v in arrays.items()}
    x_out = nc.dram_tensor("x_out", (SEQ, D), F32, kind="ExternalOutput").ap()
    build(nc, **args, x_out=x_out)
    r = run_bass_kernel_spmd(nc, [arrays], core_ids=[0])
    return r.results[0]["x_out"].reshape(1, SEQ, D)
```

```python
from contextlib import ExitStack

import numpy as np

import concourse.bass as bass
from concourse import mybir

F32 = mybir.dt.float32
F32R = mybir.dt.float32r
BF16 = mybir.dt.bfloat16
ACT = mybir.ActivationFunctionType
ALU = mybir.AluOpType
AXX = mybir.AxisListType.X

P = 128
DEPTH, SEQ, D = 2, 512, 1024
T = SEQ // P
KD = D // P
RH, DK = 8, 64
NH, NKV, DH = 8, 2, 64
G = NH // NKV
CB, CS = 32, 16
NC = (SEQ - CB) // CS + 1
NCP = 32
HID = 4 * DH
FF = 2816
KF = FF // P
EPS = 1e-6
NEG = -1e30
NEG_GUARD = -1e29
SM = DH ** -0.5
EB = 3
SB = 8

CW = 1024
RING = 4
C_T = 0
C_TV = C_T + 16
NTV = 2 * NKV * DH + 3 * NH
C_F0 = C_TV + 4
C_F1 = C_F0 + 1
C_W1K = C_F1 + 1
C_W1V = C_W1K + 4
C_F2 = C_W1V + 4
C_WO = C_F2 + 6
C_UP = C_WO + 8
C_DN = C_UP + 2 * KF
NCH = C_DN + KF

O_COS, O_SIN, O_NSIN = 0, 128, 256
O_DM = 384
O_XI = O_DM + RH * P
O_ZE = O_XI + 4 * P
O_BD = O_ZE + RH
O_DE = O_BD + P
O_ID = O_DE + 4
O_CA = O_ID + P
O_CM = O_CA + P
O_II = O_CM + T * NCP
NCONST = O_II + P // 2

Q_POS = 0
Q_B1 = Q_POS + 2 * 16
Q_W2 = Q_B1 + 4
Q_B2K = Q_W2 + 4 * DH
Q_CV = Q_B2K + 2
NPAR = Q_CV + 2 * KF * 4


MIDDLE = [("turn", 0), ("chunk", C_F0), ("score", 0), ("chunk", C_F1), ("out", 0), ("turn", 1),
          ("chunk", C_W1K), ("score", 1), ("chunk", C_W1K + 1), ("norm", 0), ("chunk", C_W1K + 2),
          ("chunk", C_W1K + 3), ("out", 1), ("hidden", 0), ("turn", 2), ("chunk", C_W1V), ("score", 2),
          ("norm", 1), ("chunk", C_W1V + 1), ("out", 2), ("turn", 3), ("chunk", C_W1V + 2),
          ("score", 3), ("norm", 2), ("chunk", C_W1V + 3), ("hidden", 1), ("out", 3), ("norm", 3)]
RET_NORM_AFTER = {C_W1K + 1: 0, C_W1V + 1: 1, C_W1V + 3: 2, C_F2 + 1: 3}


def build(nc, x_in, wstream, gains, pars, b2v_in, consts, x_out):
    ctx = ExitStack()
    with ctx:
        def sb(name, shape, dt=F32, stack=ctx):
            return stack.enter_context(nc.sbuf_tensor(name, shape, dt))

        sems = {}

        def sem(name, per_layer, start=0):
            s = ctx.enter_context(nc.semaphore(name))
            sems[name] = (s, per_layer, start)
            return s

        def upto(s, layer, count):
            per, start = next((n, f) for q, n, f in sems.values() if q is s)
            assert count + start > 0, s
            return layer * per + (count + start)

        const = sb("const", [P, NCONST])
        ident_b = sb("ident_b", [P, P], BF16)
        causal_b = sb("causal_b", [P, P], BF16)
        cmask_b = sb("cmask_b", [P, T * NCP], BF16)
        x = sb("x", [P, T, D])
        act_hi = sb("act_hi", [P, KD, SEQ], F32R)
        act_lo = sb("act_lo", [P, KD, SEQ], F32R)
        raw = sb("raw", [P, RING, CW])
        w_hi = sb("w_hi", [P, RING, CW], F32R)
        w_lo = sb("w_lo", [P, RING, CW], F32R)
        g_mix_pre = sb("g_mix_pre", [P, D])
        g_rest = sb("g_rest", [P, 3, D])
        par = sb("par", [P, NPAR])
        b2v = sb("b2v", [NCP, DH])
        gate = sb("gate", [P, T, 3 * NH])
        sq_sum = sb("sq_sum", [P, 24])
        mean = sb("mean", [P, 4 * T])
        mean_eps = sb("mean_eps", [P, 4 * T])
        rstd = sb("rstd", [P, 4 * T])
        head_eps = sb("head_eps", [P, RH])
        head_rstd = sb("head_rstd", [P, RH])
        minus_half = sb("minus_half", [P, RH])
        eps1 = sb("eps1", [P, 1])
        eps4 = sb("eps4", [P, RH])
        head_ms = sb("head_ms", [P, RH])
        s_bias = sb("s_bias", [P, SB, G])
        s_sum = sb("s_sum", [P, SB, G])
        s_rec = sb("s_rec", [P, SB, G])
        minus_one = sb("minus_one", [P, 2])
        gate_inv = sb("gate_inv", [P, T, 3 * NH])
        c_stat = sb("c_stat", [P, NH * T])
        c_rec = sb("c_rec", [P, NH * T])
        VS = sb("VS", [P, T, 2 * NKV, 2 * DH], F32R)
        KcH = sb("KcH", [P, NKV * NCP], F32R)
        KcL = sb("KcL", [P, NKV * NCP], F32R)
        VcS = sb("VcS", [NCP, NKV, 2 * DH], F32R)
        kcf = sb("kcf", [DH, NKV * NCP])
        vcf = sb("vcf", [NCP, NKV, DH])
        with ExitStack() as ret:
            qr = sb("qr", [P, T, RH * DK], F32, ret)
            kr = sb("kr", [P, T, RH * DK], F32, ret)
            rv = sb("rv", [P, T, RH * DK], F32, ret)
            sg = sb("sg", [P, T, RH * DK], F32, ret)
            qT = sb("qT", [P, 4, P], F32, ret)
            qxT = sb("qxT", [P, 4, P], F32, ret)
            kT = sb("kT", [P, 4, P], F32, ret)
            stm = sb("stm", [P, RH, P], F32, ret)
            vz = sb("vz", [P, RH * DK], F32, ret)
            state = sb("state", [P, 4, P], F32, ret)
            kvt = sb("kvt", [P, 4, P], F32, ret)
            rtmp = sb("rtmp", [P, RH * DK], F32, ret)
            th = sb("th", [P, RH * DK], F32, ret)
            osq = sb("osq", [P, RH * DK], F32, ret)
            with ExitStack() as early:
                h = sb("h", [P, 2, D], F32, early)
                mix = sb("mix", [P, D], F32, early)
                junk = sb("junk", [P, D], BF16, early)
            zf = sb("zf", [P, 16, NKV, NCP], F32, ret)
            zs = sb("zs", [P, 16, 2, NKV * NCP], F32R, ret)
            hraw = sb("hraw", [P, HID], F32, ret)
            hid = sb("hid", [P, 2, 2, NKV * NCP], F32, ret)
        with ExitStack() as att:
            pt_h = sb("pt_h", [P, 2, G * P], F32R, att)
            pt_l = sb("pt_l", [P, 2, G * P], F32R, att)
            E = sb("E", [P, EB, G, SEQ], F32, att)
            QS = sb("QS", [P, NH, SEQ], F32R, att)
            KH = sb("KH", [P, 2 * NKV, SEQ], F32R, att)
            KL = sb("KL", [P, 2 * NKV, SEQ], F32R, att)
            o_a = sb("o_a", [DH, G * P], F32, att)
            o_f = sb("o_f", [P, 2, P], F32, att)
            cE = sb("cE", [P, T * NKV * G, NCP], F32, att)
        with ExitStack() as ffn:
            gff = sb("gff", [P, KF, SEQ], F32, ffn)
            cv = sb("cv", [P, 2, 2, SEQ], F32, ffn)
            g_hi = sb("g_hi", [P, 2, SEQ], F32R, ffn)
            g_lo = sb("g_lo", [P, 2, SEQ], F32R, ffn)
        bank = ctx.enter_context(nc.psum_tensor("bank", [P, 8, 512], F32))

        cos = const[:, O_COS:O_SIN].rearrange("p (t f) -> p t f", t=T)
        sin = const[:, O_SIN:O_NSIN].rearrange("p (t f) -> p t f", t=T)
        nsin = const[:, O_NSIN:O_DM].rearrange("p (t f) -> p t f", t=T)
        dmask = const[:, O_DM:O_XI].rearrange("p (h c) -> p h c", h=RH)
        xi = const[:, O_XI:O_ZE].rearrange("p (a c) -> p a c", a=4)
        zeta = const[:, O_ZE:O_BD]
        bdiag = const[:, O_BD:O_DE]
        decay = const[:, O_DE:O_ID]
        ident = const[:, O_ID:O_CA]
        fold = const[:, O_II:NCONST]
        r32 = lambda ap: ap.bitcast(F32)

        AHEAD = 8
        raw_loaded = [sem(f"raw_loaded{s}", 16 * len(range(s, NCH, RING))) for s in range(RING)]
        hi_ready = sem("hi_ready", NCH)
        lo_ready = sem("lo_ready", NCH, start=RING)
        w_used = sem("w_used", NCH, start=RING)
        x_loaded = [sem(f"x_loaded{t}", 0) for t in range(T)]
        masks_loaded = sem("masks_loaded", 0)
        tables_loaded = sem("tables_loaded", 0)
        const_cast = sem("const_cast", 0)
        half_set = sem("half_set", 0)
        mixpre_loaded = sem("mixpre_loaded", 16)
        par_loaded = sem("par_loaded", 48)
        sq_done = sem("sq_done", 24, start=1)
        rstd_step = sem("rstd_step", 48, start=1)
        h_ready = sem("h_ready", 8, start=1)
        h_turned = sem("h_turned", 8)
        act_h = sem("act_h", 16)
        act_l = sem("act_l", 16)
        x_step = sem("x_step", 24, start=13)
        t_done = sem("t_done", 15)
        rot_step = sem("rot_step", 32, start=1)
        rv_ready = sem("rv_ready", 4)
        th_ready = sem("th_ready", 4)
        sg_ready = sem("sg_ready", 4)
        vg_act = sem("vg_act", 8)
        vg_dve = sem("vg_dve", 8)
        inv_ready = sem("inv_ready", 1)
        z_step = sem("z_step", 17)
        z_h = sem("z_h", 2)
        z_l = sem("z_l", 2)
        hraw_ready = sem("hraw_ready", 2)
        hid_turned = sem("hid_turned", 2)
        hid_ready = sem("hid_ready", 4)
        kc_done = sem("kc_done", 1)
        vc_done = sem("vc_done", 1)
        kc_f = sem("kc_f", 1)
        kc_h = sem("kc_h", 2)
        kc_l = sem("kc_l", 2)
        vc_f = sem("vc_f", 1)
        vc_h = sem("vc_h", 1)
        vc_l = sem("vc_l", 1)
        qk_turned = sem("qk_turned", 8)
        qk_copied = sem("qk_copied", 8)
        qx_ready = sem("qx_ready", 4)
        st_done = sem("st_done", 8)
        st_masked = sem("st_masked", 8)
        vz_ready = sem("vz_ready", 3)
        kv_done = sem("kv_done", 3)
        ro_done = sem("ro_done", 4)
        state_step = sem("state_step", 7)
        osq_ready = sem("osq_ready", 4)
        head_sum = sem("head_sum", 4)
        y_step = sem("y_step", 8)
        y_turned = sem("y_turned", 4)
        y_h = sem("y_h", 4)
        y_l = sem("y_l", 4)
        k_h = sem("k_h", 8)
        k_l = sem("k_l", 8)
        q_h = sem("q_h", 8)
        q_l = sem("q_l", 8)
        cs_done = sem("cs_done", 2)
        c_step = sem("c_step", 9)
        c_exp = sem("c_exp", 1)
        NU = T * NKV * 2
        JOBS = []
        for n in range(NU):
            per_bank = SEQ // (P * (T - n // (2 * NKV)))
            JOBS += [(n, r, per_bank) for r in range(0, G, per_bank)]
        heads_through = [G * n + r + count for n, r, count in JOBS]
        s_done = sem("s_done", len(JOBS))
        m_step = sem("m_step", 2 * len(JOBS))
        e_done = sem("e_done", G * NU)
        r_step = sem("r_step", 2 * NU)
        rec_done = sem("rec_done", 2 * NU)
        p_scaled = sem("p_scaled", G * NU)
        NI = T * NKV + 2 * NKV * T * (T + 1) // 2
        pt_done = sem("pt_done", NI)
        pth = sem("pth", NI)
        ptl = sem("ptl", NI)
        pv_done = sem("pv_done", NI)
        oa_done = sem("oa_done", T * NKV)
        of_done = sem("of_done", 2 * T * NKV)
        oh_done = sem("oh_done", T * NKV)
        ol_done = sem("ol_done", T * NKV)
        wo_done = sem("wo_done", 6)
        cv0 = sem("cv0", 2 * KF)
        cv_step = sem("cv_step", 4 * KF, start=AHEAD)
        gelu_done = sem("gelu_done", KF)
        g_ready = sem("g_ready", KF, start=1)
        gh = sem("gh", KF)
        gl = sem("gl", KF)
        dn_done = sem("dn_done", T - 1)
        stored = sem("stored", 0)

        Y_BANK = (5, 3, 4, 5)

        KC_AT = HID + 2 * NKV * NCP
        ff_hi = lambda k: g_hi[:, k, :] if k < 2 else act_hi[:, (k - 2) % KD, :]
        ff_lo = lambda k: g_lo[:, k, :] if k < 2 else act_lo[:, (k - 2) % KD, :]
        WO_CHUNK_AT = {NI - 4: C_WO + 2, NI - 2: C_WO + 3}
        Q_BANK = (4, 5, 3, 4)
        EARLY_JOBS = {1: (0, 1), 2: (2, 3, 4), 3: (5, 6, 7)}

        UNITS = [(i, g, b) for i in reversed(range(T)) for g in range(NKV) for b in range(2)]
        query_tile = lambda v: (T - 1 - v // NKV, v % NKV)
        ITEMS = []
        UNIT_ITEMS = []
        for n, (i, g, b) in enumerate(UNITS):
            at = len(ITEMS)
            ITEMS += [(n, n // 2, j) for j in range(i + 1)]
            if b == 1:
                ITEMS.append((None, n // 2, 0))
            UNIT_ITEMS.append(range(at, len(ITEMS)))
        assert len(ITEMS) == NI
        FIRST_OF_V = {v: min(k for k, it in enumerate(ITEMS) if it[1] == v) for v in range(T * NKV)}
        LAST_OF_V = {v: max(k for k, it in enumerate(ITEMS) if it[1] == v) for v in range(T * NKV)}
        last_turn = lambda n: max(k for k, it in enumerate(ITEMS) if it[0] == n)

        E_AT, E_AFTER, last_user, slot, room = [], [], {}, -1, 0
        for n, (i, g, b) in enumerate(UNITS):
            width = P * (i + 1)
            if room < width or 2 * width > SEQ:
                slot, room, after = (slot + 1) % EB, SEQ, last_user.get((slot + 1) % EB)
            E_AT.append((slot, SEQ - room))
            E_AFTER.append(after)
            room -= width
            last_user[slot] = n

        SCORES_AT = {}
        for z, (n, r, count) in enumerate(JOBS):
            if n >= 2:
                before = UNIT_ITEMS[n - 2]
                at = before[0] + r * len(before) // G
                if count > 1:
                    at = UNIT_ITEMS[n - 4][0]
                SCORES_AT[z] = max(at, SCORES_AT.get(z - 1, -1) + (1 if count > 1 else 0),
                                   SCORES_AT.get(z - 2, -1) + 1,
                                   last_turn(E_AFTER[n]) if E_AFTER[n] is not None else 0)
                assert SCORES_AT[z] + 2 <= UNIT_ITEMS[n][0]
        jobs_at = lambda k: [z for z, at in SCORES_AT.items() if at == k]
        pairs_at = lambda k: [(JOBS[z][0], p) for z in jobs_at(k) for p in range(2)
                              if JOBS[z][1] < 2 * p + 2 <= JOBS[z][1] + JOBS[z][2]]

        RS_PRE1 = lambda t: 2 * t
        RS_RET = lambda n: 8 + 2 * n
        RS_POST2 = lambda t: 36 + 3 * t
        SQ_PRE1 = lambda t: t
        SQ_POST2 = lambda t: 16 + 2 * t
        MID_NORMS = [("post", 0), ("pre", 0), ("post", 1), ("post", 2), ("pre", 1), ("pre", 2), ("post", 3), ("pre", 3)]
        ACT_MID = [("post", 0), ("pre", 0), ("post", 1), ("post", 2), ("pre", 1), ("halves", 0), ("pre", 2),
                   ("chunks", 3), ("post", 3), ("halves", 1), ("halves", 2), ("pre", 3), ("halves", 3)]
        DVE_MID = [("post", 0), ("pre", 0), ("post", 1), ("post", 2), ("pre", 1), ("halves", 0), ("pre", 2),
                   ("halves", 1), ("halves", 2), ("post", 3), ("pre", 3), ("halves", 3)]
        RS_MID, SQ_MID, rs, sq = {}, {}, 16, 4
        for what in MID_NORMS:
            RS_MID[what], SQ_MID[what] = rs, sq
            rs, sq = (rs + 3, sq + 2) if what[0] == "post" else (rs + 2, sq + 1)

        def slot_free(eng, s, layer, c):
            before = c - RING if c >= RING else max(range(c, NCH, RING)) - NCH
            eng.wait_ge(s, layer * NCH + (before + 1 + RING))

        def chunk_used(eng, layer, c):
            eng.wait_ge(w_used, layer * NCH + (c + 1 + RING))

        def tile_done(eng, layer, done, block_no, t, last_chunk):
            if t < T - 1:
                eng.wait_ge(done, upto(done, layer, (T - 1) * block_no + t + 1))
            else:
                chunk_used(eng, layer, last_chunk)

        block = ctx.enter_context(nc.Block())

        @block.sync
        def _(sp):
            sp.dma_start(x[:, 0, :], x_in[0:P, :]).then_inc(x_loaded[0], 16)
            sp.dma_start(g_mix_pre[:], gains[0, 0:1, 0:D].broadcast_to([P, D])).then_inc(mixpre_loaded, 16)
            sp.dma_start(const[:, O_ID:NCONST], consts[:, O_ID:NCONST]).then_inc(masks_loaded, 16)
            for t in range(T):
                sp.dma_start(raw[:, t, :], wstream[t]).then_inc(raw_loaded[t], 16)
                if t + 1 < T:
                    sp.dma_start(x[:, t + 1, :], x_in[(t + 1) * P:(t + 2) * P, :]).then_inc(x_loaded[t + 1], 16)
            sp.dma_start(const[:, 0:O_ID], consts[:, 0:O_ID]).then_inc(tables_loaded, 16)

            def load_quad(layer, quad):
                for s in range(RING):
                    sp.wait_ge(lo_ready, layer * NCH + quad * RING + (s + 1))
                    sp.dma_start(raw[:, s, :], wstream[layer * NCH + quad * RING + s]).then_inc(raw_loaded[s], 16)

            with sp.Fori(0, DEPTH) as l:
                sp.wait_ge(x_step, upto(x_step, l, 0))
                sp.dma_start(par[:], pars[l]).then_inc(par_loaded, 16)
                sp.dma_start(b2v[:], b2v_in[l, 0:1, :].broadcast_to([NCP, DH])).then_inc(par_loaded, 16)
                sp.dma_start(g_rest[:].rearrange("p a d -> p (a d)"),
                             gains[l, 1:2, :].broadcast_to([P, 3 * D])).then_inc(par_loaded, 16)
                with sp.Fori(1, C_UP // RING) as quad:
                    load_quad(l, quad)
                sp.wait_ge(h_ready, upto(h_ready, l, 4))
                sp.dma_start(g_mix_pre[:], gains[l + 1, 0:1, 0:D].broadcast_to([P, D]))\
                    .then_inc(mixpre_loaded, 16)
                with sp.Fori(C_UP // RING, NCH // RING) as quad:
                    load_quad(l, quad)
                for c in range(NCH // RING * RING, NCH):
                    slot_free(sp, lo_ready, l, c)
                    sp.dma_start(raw[:, c % RING, :], wstream[l * NCH + c]).then_inc(raw_loaded[c % RING], 16)
                for c in range(RING):
                    slot_free(sp, lo_ready, l + 1, c)
                    sp.dma_start(raw[:, c, :], wstream[(l + 1) * NCH + c]).then_inc(raw_loaded[c], 16)
            for t in range(T):
                sp.wait_ge(x_step, upto(x_step, DEPTH - 1, 12 + 3 * (t + 1)))
                sp.dma_start(x_out[t * P:(t + 1) * P, :], x[:, t, :]).then_inc(stored, 16)
            sp.wait_ge(stored, 16 * T)
            for s in range(RING):
                sp.wait_ge(raw_loaded[s], upto(raw_loaded[s], DEPTH, 16))
            sp.wait_ge(mixpre_loaded, 16 * (DEPTH + 1))

        @block.gpsimd
        def _(pool):
            pool.sem_inc(lo_ready, RING)
            pool.sem_inc(rstd_step, 1)
            nc.gpsimd.memset(minus_half[:], -0.5).then_inc(half_set, 1)
            nc.gpsimd.memset(eps1[:], EPS).then_inc(half_set, 1)
            nc.gpsimd.memset(eps4[:], 4.0 * EPS).then_inc(half_set, 1)
            nc.gpsimd.memset(minus_one[:], -1.0).then_inc(half_set, 1)
            pool.wait_ge(half_set, 4)

            def split_lo(layer, c):
                s = c % RING
                pool.wait_ge(hi_ready, upto(hi_ready, layer, c + 1))
                slot_free(pool, w_used, layer, c)
                nc.gpsimd.tensor_tensor(w_lo[:, s, :], raw[:, s, :], r32(w_hi[:, s, :]), ALU.subtract)\
                    .then_inc(lo_ready, 1)

            def split_lo_quad(layer, quad):
                for s in range(RING):
                    pool.wait_ge(hi_ready, layer * NCH + quad * RING + (s + 1))
                    pool.wait_ge(w_used, layer * NCH + quad * RING + (s + 1))
                    nc.gpsimd.tensor_tensor(w_lo[:, s, :], raw[:, s, :], r32(w_hi[:, s, :]),
                                            ALU.subtract).then_inc(lo_ready, 1)

            def inv_root(layer, step, source, eps, with_eps, out):
                nc.gpsimd.tensor_tensor(with_eps, source, eps, ALU.add).then_inc(rstd_step, 1)
                pool.wait_ge(rstd_step, upto(rstd_step, layer, step + 1))
                nc.gpsimd.tensor_tensor(out, with_eps, minus_half[:, 0:out.shape[-1]], ALU.pow)\
                    .then_inc(rstd_step, 1)

            def inv_root_pre(layer, step, sq, col):
                pool.wait_ge(sq_done, upto(sq_done, layer, sq + 1))
                inv_root(layer, step, sq_sum[:, sq:sq + 1], eps1[:], mean_eps[:, col:col + 1], rstd[:, col:col + 1])

            def inv_root_post(layer, step, sq, col):
                pool.wait_ge(sq_done, upto(sq_done, layer, sq + 2))
                nc.gpsimd.tensor_tensor(mean[:, col:col + 1], sq_sum[:, sq:sq + 1], sq_sum[:, sq + 1:sq + 2],
                                        ALU.add).then_inc(rstd_step, 1)
                pool.wait_ge(rstd_step, upto(rstd_step, layer, step + 1))
                inv_root(layer, step + 1, mean[:, col:col + 1], eps1[:], mean_eps[:, col:col + 1],
                         rstd[:, col:col + 1])

            with pool.Fori(0, DEPTH) as l:
                for t in range(T):
                    inv_root_pre(l, RS_PRE1(t), SQ_PRE1(t), 4 * t)
                    split_lo(l, t)
                with pool.Fori(1, C_F0 // RING) as quad:
                    split_lo_quad(l, quad)
                for c in range(C_F0, C_F2 + 4):
                    split_lo(l, c)
                    if c in RET_NORM_AFTER:
                        n = RET_NORM_AFTER[c]
                        pool.wait_ge(head_sum, upto(head_sum, l, n + 1))
                        if n:
                            pool.wait_ge(y_step, upto(y_step, l, 2 * n - 1))
                            pool.wait_ge(rstd_step, upto(rstd_step, l, RS_RET(n)))
                        inv_root(l, RS_RET(n), head_ms[:], eps4[:], head_eps[:], head_rstd[:])
                for c in range(C_F2 + 4, C_WO + 2):
                    split_lo(l, c)
                def scale(n, p):
                    i = UNITS[n][0]
                    slot, col = E_AT[n]
                    heads = slice(2 * p, 2 * p + 2)
                    if n >= SB:
                        pool.wait_ge(p_scaled, upto(p_scaled, l, G * (n - SB) + 2 * p + 2))
                    pool.wait_ge(r_step, upto(r_step, l, 2 * n + p + 1))
                    nc.gpsimd.tensor_tensor(s_rec[:, n % SB, heads], s_sum[:, n % SB, heads], minus_one[:],
                                            ALU.pow).then_inc(rec_done, 1)
                    pool.wait_ge(rec_done, upto(rec_done, l, 2 * n + p + 1))
                    for r in (2 * p, 2 * p + 1):
                        e = E[:, slot, r, col:col + P * (i + 1)]
                        nc.gpsimd.tensor_tensor(e, e, s_rec[:, n % SB, r:r + 1].broadcast_to([P, P * (i + 1)]),
                                                ALU.mult).then_inc(p_scaled, 1)

                def out_rest(v):
                    i, g = query_tile(v)
                    dst = (slice(None), slice(4 + 2 * g, 6 + 2 * g), slice(i * P, (i + 1) * P))
                    pool.wait_ge(oh_done, upto(oh_done, l, v + 1))
                    nc.gpsimd.tensor_tensor(act_lo[dst], o_f[:], r32(act_hi[dst]), ALU.subtract).then_inc(ol_done, 1)

                for n in range(2):
                    for p in range(2):
                        scale(n, p)
                for k in range(NI + 4):
                    if k in WO_CHUNK_AT:
                        split_lo(l, WO_CHUNK_AT[k])
                    for unit, p in pairs_at(k - 2):
                        scale(unit, p)
                    if k - 4 in LAST_OF_V.values():
                        out_rest(ITEMS[k - 4][1])
                for c in range(C_WO + RING, C_UP):
                    split_lo(l, c)
                for what, t in MID_NORMS:
                    if (what, t) == ("post", T - 1):
                        split_lo(l, C_UP)
                        split_lo(l, C_UP + 1)
                    if what == "post":
                        inv_root_post(l, RS_MID[what, t], SQ_MID[what, t], 4 * t + 1)
                    else:
                        inv_root_pre(l, RS_MID[what, t], SQ_MID[what, t], 4 * t + 2)
                for c in range(C_UP + 2, C_UP + RING):
                    split_lo(l, c)
                with pool.Fori(C_UP // RING + 1, NCH // RING) as quad:
                    split_lo_quad(l, quad)
                for c in range(NCH // RING * RING, NCH):
                    split_lo(l, c)
                for t in range(T):
                    inv_root_post(l, RS_POST2(t), SQ_POST2(t), 4 * t + 3)

        @block.scalar
        def _(act):
            def hi(layer, c):
                s = c % RING
                act.wait_ge(raw_loaded[s], upto(raw_loaded[s], layer, 16 * (c // RING + 1)))
                slot_free(act, w_used, layer, c)
                nc.scalar.activation(w_hi[:, s, :], raw[:, s, :], ACT.Copy).then_inc(hi_ready, 1)

            def hi_quad(layer, quad, s):
                act.wait_ge(raw_loaded[s], layer * sems[f"raw_loaded{s}"][1] + quad * 16 + 16)
                act.wait_ge(w_used, layer * NCH + quad * RING + (s + 1))
                nc.scalar.activation(w_hi[:, s, :], raw[:, s, :], ACT.Copy).then_inc(hi_ready, 1)

            def square_pre(layer, t, sq):
                act.wait_ge(sq_done, upto(sq_done, layer, sq))
                nc.scalar.activation(junk[:], x[:, t, :], ACT.Square, scale=D ** -0.5,
                                     accum_out=sq_sum[:, sq:sq + 1]).then_inc(sq_done, 1)

            def square_post(layer, t, sq):
                for half in range(2):
                    act.wait_ge(sq_done, upto(sq_done, layer, sq + half))
                    nc.scalar.activation(junk[:, 0:512], bank[:, t + 4 * half, :], ACT.Square, scale=D ** -0.5,
                                         accum_out=sq_sum[:, sq + half:sq + half + 1]).then_inc(sq_done, 1)

            def act_halves(layer, n, t):
                act.wait_ge(h_turned, upto(h_turned, layer, n + 1))
                for k2 in range(2):
                    nc.scalar.activation(act_hi[:, 4 * k2:4 * k2 + 4, t * P:(t + 1) * P],
                                         bank[:, t + 4 * k2, :].rearrange("p (k c) -> p k c", k=4),
                                         ACT.Copy).then_inc(act_h, 1)

            act.sem_inc(sq_done, 1)
            with act.Fori(0, DEPTH) as l:
                for t in range(T):
                    act.wait_ge(x_loaded[t], 16)
                    act.wait_ge(x_step, upto(x_step, l, 3 * (t + 1) - 12))
                    square_pre(l, t, SQ_PRE1(t))
                    hi(l, t)
                    if t:
                        act_halves(l, t - 1, t - 1)
                act_halves(l, T - 1, T - 1)
                for blk in range(5):
                    for c in range(4 * blk + 4, 4 * blk + 8):
                        hi(l, c)
                    if blk == 2:
                        for t in range(T):
                            tile_done(act, l, t_done, 2, t, 11)
                            nc.scalar.activation(rv[:, t, :], bank[:, 4 + t, :], ACT.Copy).then_inc(rv_ready, 1)
                    if blk == 3:
                        for t in range(T):
                            tile_done(act, l, t_done, 3, t, 15)
                            if t:
                                act.wait_ge(sg_ready, upto(sg_ready, l, t))
                            nc.scalar.activation(th[:], bank[:, t, :], ACT.Tanh, scale=0.5).then_inc(th_ready, 1)
                    if blk == 4:
                        for t in range(T):
                            tile_done(act, l, t_done, 4, t, 19)
                            nc.scalar.activation(
                                VS[:, t, :, 0:DH], bank[:, 4 + t, 0:4 * DH].rearrange("p (a d) -> p a d", a=4),
                                ACT.Copy).then_inc(vg_act, 1)
                            nc.scalar.activation(gate[:, t, :], bank[:, 4 + t, 4 * DH:NTV], ACT.Tanh, scale=0.5)\
                                .then_inc(vg_act, 1)

                def turned_copies(n):
                    for m, dst in ((0, qT), (1, kT)):
                        act.wait_ge(qk_turned, upto(qk_turned, l, 2 * n + m + 1))
                        if n and m == 0:
                            act.wait_ge(ro_done, upto(ro_done, l, n))
                        nc.scalar.activation(dst[:].rearrange("p a c -> p (a c)"), bank[:, 2 + m, :], ACT.Copy)\
                            .then_inc(qk_copied, 1)

                def out_squares(n):
                    act.wait_ge(ro_done, upto(ro_done, l, n + 1))
                    if n:
                        act.wait_ge(head_sum, upto(head_sum, l, n))
                    nc.scalar.activation(osq[:], bank[:, 6, :], ACT.Square, scale=2.0 * DK ** -0.5).then_inc(osq_ready, 1)

                def z_round(s):
                    act.wait_ge(z_step, upto(z_step, l, 1 + 8 * (s + 1)))
                    if s:
                        chunk_used(act, l, C_W1K + 3)
                    nc.scalar.activation(zs[:, :, 0, :], zf[:].rearrange("p m g c -> p m (g c)"), ACT.Copy)\
                        .then_inc(z_h, 1)

                def hidden(s):
                    act.wait_ge(hid_turned, upto(hid_turned, l, s + 1))
                    for m in range(2):
                        nc.scalar.activation(hid[:, s, m, :], bank[:, s, HID + m * 64:HID + (m + 1) * 64],
                                             ACT.Gelu_apprx_tanh,
                                             bias=par[:, Q_B1 + 2 * s + m:Q_B1 + 2 * s + m + 1])\
                            .then_inc(hid_ready, 1)

                act.wait_ge(par_loaded, upto(par_loaded, l, 48))
                for what, n in MIDDLE:
                    if what == "chunk" and n + RING < C_F2 + 2:
                        hi(l, n + RING)
                    if what == "turn":
                        turned_copies(n)
                    if what == "out":
                        out_squares(n)
                    if what == "chunk" and n == C_F0:
                        z_round(0)
                    if what == "chunk" and n == C_W1K + 3:
                        z_round(1)
                    if what == "hidden":
                        hidden(n)
                act.wait_ge(kc_done, upto(kc_done, l, 1))
                nc.scalar.activation(kcf[:], bank[0:DH, 0, KC_AT:KC_AT + NKV * NCP], ACT.Identity,
                                     bias=par[0:DH, Q_B2K:Q_B2K + 1]).then_inc(kc_f, 1)
                act.wait_ge(kc_f, upto(kc_f, l, 1))
                for half in range(2):
                    nc.scalar.activation(KcH[half * DH:(half + 1) * DH, :], kcf[:], ACT.Copy).then_inc(kc_h, 1)
                act.wait_ge(vc_f, upto(vc_f, l, 1))
                nc.scalar.activation(VcS[:, :, 0:DH], vcf[:], ACT.Copy).then_inc(vc_h, 1)
                act.wait_ge(y_step, upto(y_step, l, 8))
                for f in range(2):
                    hi(l, C_F2 + f + 2)
                    chunk_used(act, l, C_F2 + f)
                    for g in range(NKV):
                        for half in range(2):
                            nc.scalar.activation(KH[half * DH:(half + 1) * DH, 2 * f + g, :],
                                                 bank[g * DH:(g + 1) * DH, 2 + f, :], ACT.Copy).then_inc(k_h, 1)
                def exps(z):
                    n, first, count = JOBS[z]
                    slot, col = E_AT[n]
                    width = P * (UNITS[n][0] + 1)
                    act.wait_ge(m_step, upto(m_step, l, 2 * z + 2))
                    if E_AFTER[n] is not None:
                        act.wait_ge(pt_done, upto(pt_done, l, last_turn(E_AFTER[n]) + 1))
                    if n >= SB:
                        act.wait_ge(rec_done, upto(rec_done, l, 2 * (n - SB) + (first + count + 1) // 2))
                    for q in range(count):
                        r = first + q
                        nc.scalar.activation(E[:, slot, r, col:col + width], bank[:, z % 3, q * width:(q + 1) * width],
                                             ACT.Exp, bias=s_bias[:, n % SB, r:r + 1], scale=SM,
                                             accum_out=s_sum[:, n % SB, r:r + 1]).then_inc(e_done, 1)

                def y_round(n):
                    act.wait_ge(y_turned, upto(y_turned, l, n + 1))
                    nc.scalar.activation(act_hi[:, 0:4, n * P:(n + 1) * P],
                                         bank[:, Y_BANK[n], :].rearrange("p (k c) -> p k c", k=4),
                                         ACT.Copy).then_inc(y_h, 1)

                for f in range(4):
                    hi(l, C_F2 + f + 4)
                    chunk_used(act, l, C_F2 + 2 + f)
                    for m in range(2):
                        nc.scalar.activation(QS[m * DH:(m + 1) * DH, 2 * f + m, :],
                                             bank[m * DH:(m + 1) * DH, Q_BANK[f], :], ACT.Copy).then_inc(q_h, 1)
                    if f == 3:
                        y_round(0)
                        y_round(1)
                    for z in EARLY_JOBS.get(f, ()):
                        exps(z)
                for n in (2, 3):
                    y_round(n)

                def p_round(k):
                    rows = NCP if ITEMS[k][0] is None else P
                    act.wait_ge(pt_done, upto(pt_done, l, k + 1))
                    if k >= 2:
                        act.wait_ge(pv_done, upto(pv_done, l, k - 1))
                    nc.scalar.activation(pt_h[0:rows, k % 2, :], bank[0:rows, 3 + k % 3, :], ACT.Copy)\
                        .then_inc(pth, 1)

                def out_first(v):
                    act.wait_ge(pv_done, upto(pv_done, l, LAST_OF_V[v] + 1))
                    if v:
                        act.wait_ge(of_done, upto(of_done, l, 2 * v))
                    nc.scalar.activation(o_a[:], bank[0:DH, 6 + v % 2, :], ACT.Copy).then_inc(oa_done, 1)

                def out_round(v):
                    i, g = query_tile(v)
                    act.wait_ge(of_done, upto(of_done, l, 2 * v + 2))
                    nc.scalar.activation(act_hi[:, 4 + 2 * g:6 + 2 * g, i * P:(i + 1) * P], o_f[:], ACT.Copy)\
                        .then_inc(oh_done, 1)

                for k in range(NI + 4):
                    if k + 1 in WO_CHUNK_AT:
                        hi(l, WO_CHUNK_AT[k + 1])
                    if k < NI:
                        p_round(k)
                    if k == 1:
                        act.wait_ge(c_step, upto(c_step, l, 4))
                        nc.scalar.activation(cE[:], cE[:], ACT.Exp, scale=SM).then_inc(c_exp, 1)
                    for z in jobs_at(k - 1):
                        exps(z)
                    if k - 3 in LAST_OF_V.values():
                        out_first(ITEMS[k - 3][1])
                    if k - 4 in LAST_OF_V.values():
                        out_round(ITEMS[k - 4][1])

                for c in range(C_WO + RING, C_UP):
                    hi(l, c)
                for what, t in ACT_MID:
                    if what == "chunks":
                        for c in range(C_UP, C_UP + t):
                            hi(l, c)
                    elif what == "post":
                        tile_done(act, l, wo_done, 1, t, C_WO + 7)
                        square_post(l, t, SQ_MID[what, t])
                    elif what == "pre":
                        act.wait_ge(x_step, upto(x_step, l, 3 * t + 3))
                        square_pre(l, t, SQ_MID[what, t])
                    else:
                        act_halves(l, 4 + t, t)
                hi(l, C_UP + 3)

                def conv_first(it, p, s):
                    act.wait_ge(w_used, l * NCH + it * RING + (C_UP + 2 * p + s + 1 + RING))
                    act.wait_ge(g_ready, l * KF + it * 2 + 1)
                    col = it * 2 + (s * KF + p)
                    w2 = par[:, Q_CV:Q_CV + 8 * KF].rearrange("p (n q) -> p n q", q=4)
                    nc.scalar.activation(cv[:, p, s, :], bank[:, 2 * p + s, :], ACT.Identity,
                                         bias=w2[:, bass.ds(col, 1), 3], scale=w2[:, bass.ds(col, 1), 2])\
                        .then_inc(cv0, 1)

                def gelu(it, p):
                    act.wait_ge(cv_step, l * (4 * KF) + it * 8 + (4 * p + 2 + AHEAD))
                    nc.scalar.activation(cv[:, p, 0, :], cv[:, p, 0, :], ACT.Gelu_apprx_tanh)\
                        .then_inc(gelu_done, 1)

                def ff_round(k):
                    act.wait_ge(g_ready, upto(g_ready, l, k + 1))
                    nc.scalar.activation(ff_hi(k), gff[:, k, :], ACT.Copy).then_inc(gh, 1)

                def conv_step(it):
                    for p in range(2):
                        for s in range(2):
                            conv_first(it, p, s)
                            hi_quad(l, it + (C_UP // RING + 1), 2 * p + s)
                        gelu(it, p)

                with act.Fori(0, KF // 2 - 1) as it:
                    conv_step(it)
                ff_round(0)
                ff_round(1)
                conv_step(KF // 2 - 1)
                for k in range(2, KF):
                    act.wait_ge(w_used, upto(w_used, l, C_DN + max(k - 1 - KD, 0)))
                    ff_round(k)
                    if C_DN + k + RING - 3 < NCH and k >= 3:
                        hi(l, C_DN + k + RING - 3)
                for t in range(T):
                    tile_done(act, l, dn_done, 0, t, NCH - 1)
                    square_post(l, t, SQ_POST2(t))

        @block.vector
        def _(dve):
            def minus(out, a, b):
                return nc.vector.tensor_tensor(out, a, b, ALU.subtract)

            def normalise(layer, n, t, gain, rs, col):
                if n % 4 >= 2:
                    dve.wait_ge(h_turned, upto(h_turned, layer, n - 1))
                dve.wait_ge(rstd_step, upto(rstd_step, layer, rs + 2))
                nc.vector.scalar_tensor_tensor(out=h[:, t % 2, :], in0=x[:, t, :], scalar=rstd[:, col:col + 1],
                                               in1=gain, op0=ALU.mult, op1=ALU.mult).then_inc(h_ready, 1)

            def act_rests(layer, n, t):
                for k2 in range(2):
                    dve.wait_ge(act_h, upto(act_h, layer, 2 * n + k2 + 1))
                    minus(act_lo[:, 4 * k2:4 * k2 + 4, t * P:(t + 1) * P],
                          bank[:, t + 4 * k2, :].rearrange("p (k c) -> p k c", k=4),
                          r32(act_hi[:, 4 * k2:4 * k2 + 4, t * P:(t + 1) * P])).then_inc(act_l, 1)

            def add_branch(layer, base, t, gain, rs, col):
                dve.wait_ge(x_step, upto(x_step, layer, base))
                dve.wait_ge(rstd_step, upto(rstd_step, layer, rs + 3))
                for half in range(2):
                    cols = slice(512 * half, 512 * half + 512)
                    nc.vector.scalar_tensor_tensor(out=mix[:, cols], in0=bank[:, t + 4 * half, :],
                                                   scalar=rstd[:, col:col + 1], in1=gain[:, cols],
                                                   op0=ALU.mult, op1=ALU.mult).then_inc(x_step, 1)
                dve.wait_ge(x_step, upto(x_step, layer, base + 2))
                nc.vector.tensor_tensor(x[:, t, :], x[:, t, :], mix[:], ALU.add).then_inc(x_step, 1)

            dve.sem_inc(cv_step, AHEAD)
            for s in (rot_step, h_ready, g_ready):
                dve.sem_inc(s, 1)
            dve.sem_inc(x_step, 13)
            dve.wait_ge(masks_loaded, 16)
            nc.vector.tensor_copy(ident_b[:], ident).then_inc(const_cast, 1)
            nc.vector.tensor_copy(causal_b[:], const[:, O_CA:O_CM]).then_inc(const_cast, 1)
            nc.vector.tensor_copy(cmask_b[:], const[:, O_CM:O_II]).then_inc(const_cast, 1)

            with dve.Fori(0, DEPTH) as l:
                dve.wait_ge(mixpre_loaded, upto(mixpre_loaded, l, 16))
                for t in range(T):
                    normalise(l, t, t, g_mix_pre[:], RS_PRE1(t), 4 * t)
                    if t:
                        act_rests(l, t - 1, t - 1)
                act_rests(l, T - 1, T - 1)

                dve.wait_ge(tables_loaded, 16)

                def rotate(m, dst, t, b):
                    at = 16 * m + 4 * t
                    src = bank[:, b, :].rearrange("p (h a f) -> p h a f", h=RH, a=2)
                    tmp = rtmp[:].rearrange("p (h a f) -> p h a f", h=RH, a=2)
                    wide = lambda tab: tab[:, t, :].unsqueeze(1).broadcast_to([P, RH, DK // 2])
                    tile_done(dve, l, t_done, m, t, 4 * m + 3)
                    nc.vector.tensor_tensor(
                        dst[:, t, :].rearrange("p (h f) -> p h f", f=DK // 2),
                        bank[:, b, :].rearrange("p (h f) -> p h f", f=DK // 2),
                        cos[:, t, :].unsqueeze(1).broadcast_to([P, 2 * RH, DK // 2]), ALU.mult)\
                        .then_inc(rot_step, 1)
                    dve.wait_ge(rot_step, upto(rot_step, l, at))
                    nc.vector.tensor_tensor(tmp[:, :, 0, :], src[:, :, 1, :], wide(nsin), ALU.mult)\
                        .then_inc(rot_step, 1)
                    nc.vector.tensor_tensor(tmp[:, :, 1, :], src[:, :, 0, :], wide(sin), ALU.mult)\
                        .then_inc(rot_step, 1)
                    dve.wait_ge(rot_step, upto(rot_step, l, at + 3))
                    nc.vector.tensor_tensor(dst[:, t, :], dst[:, t, :], rtmp[:], ALU.add).then_inc(rot_step, 1)

                for t in range(T):
                    rotate(0, qr, t, 4 + t)
                for t in range(T):
                    rotate(1, kr, t, t)
                for t in range(T):
                    dve.wait_ge(th_ready, upto(th_ready, l, t + 1))
                    nc.vector.scalar_tensor_tensor(out=sg[:, t, :], in0=th[:], scalar=1.0, in1=bank[:, t, :],
                                                   op0=ALU.add, op1=ALU.mult).then_inc(sg_ready, 1)
                for t in range(T):
                    dve.wait_ge(vg_act, upto(vg_act, l, 2 * t + 2))
                    minus(VS[:, t, :, DH:2 * DH], bank[:, 4 + t, 0:4 * DH].rearrange("p (a d) -> p a d", a=4),
                          r32(VS[:, t, :, 0:DH])).then_inc(vg_dve, 1)
                    nc.vector.tensor_scalar(gate[:, t, :], gate[:, t, :], 0.5, 0.5, ALU.mult, ALU.add)\
                        .then_inc(vg_dve, 1)
                dve.wait_ge(vg_dve, upto(vg_dve, l, 8))
                nc.vector.reciprocal(gate_inv[:], gate[:]).then_inc(inv_ready, 1)

                def turned(n):
                    dve.wait_ge(qk_copied, upto(qk_copied, l, 2 * n + 1))
                    if n:
                        dve.wait_ge(ro_done, upto(ro_done, l, n))
                    nc.vector.tensor_tensor(qxT[:], bank[:, 2, :].rearrange("p (a c) -> p a c", a=4), xi,
                                            ALU.mult).then_inc(qx_ready, 1)
                    if n < T - 1:
                        if n:
                            dve.wait_ge(kv_done, upto(kv_done, l, n))
                        else:
                            dve.wait_ge(rv_ready, upto(rv_ready, l, 4))
                        nc.vector.tensor_tensor(vz[:].rearrange("p (h e) -> p h e", h=RH),
                                                rv[:, n, :].rearrange("p (h e) -> p h e", h=RH),
                                                zeta.unsqueeze(2).broadcast_to([P, RH, DK]), ALU.mult)\
                            .then_inc(vz_ready, 1)

                def mask_scores(n):
                    if n:
                        dve.wait_ge(ro_done, upto(ro_done, l, n))
                    for a in range(2):
                        dve.wait_ge(st_done, upto(st_done, l, 2 * n + a + 1))
                        nc.vector.tensor_tensor(stm[:, a:RH:2, :],
                                                bank[:, 4 + a, :].rearrange("p (h c) -> p h c", h=4),
                                                dmask[:, a:RH:2, :], ALU.mult).then_inc(st_masked, 1)

                def states(n):
                    if n == T - 1:
                        return
                    dve.wait_ge(kv_done, upto(kv_done, l, n + 1))
                    kv = bank[:, 7, :].rearrange("p (a c) -> p a c", a=4)
                    bd = bdiag.unsqueeze(1).broadcast_to([P, 4, P])
                    if n == 0:
                        nc.vector.tensor_tensor(state[:], kv, bd, ALU.mult).then_inc(state_step, 1)
                        return
                    at = 3 * n - 2
                    dve.wait_ge(state_step, upto(state_step, l, at))
                    nc.vector.tensor_tensor(kvt[:], kv, bd, ALU.mult).then_inc(state_step, 1)
                    dve.wait_ge(ro_done, upto(ro_done, l, n + 1))
                    nc.vector.tensor_tensor(state[:], state[:], decay.unsqueeze(2).broadcast_to([P, 4, P]),
                                            ALU.mult).then_inc(state_step, 1)
                    dve.wait_ge(state_step, upto(state_step, l, at + 2))
                    nc.vector.tensor_tensor(state[:], state[:], kvt[:], ALU.add).then_inc(state_step, 1)

                def head_norms(n):
                    dve.wait_ge(osq_ready, upto(osq_ready, l, n + 1))
                    if n:
                        dve.wait_ge(rstd_step, upto(rstd_step, l, RS_RET(n - 1) + 1))
                    nc.vector.reduce_sum(head_ms[:], osq[:].rearrange("p (h e) -> p h e", h=RH), AXX)\
                        .then_inc(head_sum, 1)

                def outputs(n):
                    dve.wait_ge(rstd_step, upto(rstd_step, l, RS_RET(n) + 2))
                    y = qr[:, n, :].rearrange("p (h e) -> p h e", h=RH)
                    nc.vector.tensor_tensor(y, bank[:, 6, :].rearrange("p (h e) -> p h e", h=RH),
                                            head_rstd[:].unsqueeze(2).broadcast_to([P, RH, DK]), ALU.mult)\
                        .then_inc(y_step, 1)
                    dve.wait_ge(y_step, upto(y_step, l, 2 * n + 1))
                    nc.vector.tensor_tensor(qr[:, n, :], qr[:, n, :], sg[:, n, :], ALU.mult).then_inc(y_step, 1)

                def z_build(s):
                    if s == 0:
                        nc.vector.memset(zf[:, :, :, NC:NCP], 0.0).then_inc(z_step, 1)
                    else:
                        dve.wait_ge(z_l, upto(z_l, l, 1))
                    chunk_used(dve, l, C_F0 + s)
                    for half in range(2):
                        rows = slice(half * DH, (half + 1) * DH)
                        for g in range(NKV):
                            src = bank[g * DH:(g + 1) * DH, s, :].rearrange("p (c m a) -> p m a c", m=8, a=2)
                            for m8 in range(2):
                                pos = par[rows, Q_POS + 16 * s + 8 * m8:Q_POS + 16 * s + 8 * m8 + 8]
                                nc.vector.tensor_tensor(
                                    zf[rows, 8 * m8:8 * m8 + 8, g, 0:NC], src[:, :, half, m8:m8 + NC],
                                    pos.unsqueeze(2).broadcast_to([DH, 8, NC]), ALU.add).then_inc(z_step, 1)

                def z_rest(s):
                    dve.wait_ge(z_step, upto(z_step, l, 1 + 8 * (s + 1)))
                    dve.wait_ge(z_h, upto(z_h, l, s + 1))
                    minus(zs[:, :, 1, :], zf[:].rearrange("p m g c -> p m (g c)"), r32(zs[:, :, 0, :])).then_inc(z_l, 1)

                dve.wait_ge(par_loaded, upto(par_loaded, l, 48))
                for what, n in MIDDLE:
                    if what == "turn":
                        turned(n)
                    if what == "score":
                        mask_scores(n)
                    if what == "out":
                        states(n)
                        head_norms(n)
                    if what == "norm":
                        outputs(n)
                    if what == "chunk" and n == C_F0:
                        z_build(0)
                        z_rest(0)
                    if what == "chunk" and n == C_F1:
                        z_build(1)
                    if what == "chunk" and n in (C_W1K + 3, C_W1V + 3):
                        which = 0 if n == C_W1K + 3 else 1
                        chunk_used(dve, l, n)
                        if which:
                            dve.wait_ge(hid_turned, upto(hid_turned, l, 1))
                        nc.vector.tensor_copy(hraw[:], bank[:, which, 0:HID]).then_inc(hraw_ready, 1)
                    if what == "chunk" and n == C_W1K + 3:
                        z_rest(1)
                dve.wait_ge(vc_done, upto(vc_done, l, 1))
                nc.vector.tensor_tensor(vcf[:], bank[0:NCP, 1, KC_AT:KC_AT + NKV * DH].rearrange("p (g d) -> p g d", g=NKV),
                                        b2v[:].unsqueeze(1).broadcast_to([NCP, NKV, DH]), ALU.add)\
                    .then_inc(vc_f, 1)
                dve.wait_ge(kc_h, upto(kc_h, l, 2))
                for half in range(2):
                    minus(KcL[half * DH:(half + 1) * DH, :], kcf[:], r32(KcH[0:DH, :])).then_inc(kc_l, 1)
                dve.wait_ge(vc_h, upto(vc_h, l, 1))
                minus(VcS[:, :, DH:2 * DH], vcf[:], r32(VcS[:, :, 0:DH])).then_inc(vc_l, 1)
                l = nc.snap(l, engines=[mybir.EngineType.DVE], donate=False)
                for f in range(2):
                    for g in range(NKV):
                        for half in range(2):
                            if g + half == 0:
                                dve.wait_ge(k_h, upto(k_h, l, 4 * (f + 1)))
                            rows = slice(half * DH, (half + 1) * DH)
                            minus(KL[rows, 2 * f + g, :], bank[g * DH:(g + 1) * DH, 2 + f, :],
                                  r32(KH[rows, 2 * f + g, :])).then_inc(k_l, 1)
                def maxima(z):
                    n, first, count = JOBS[z]
                    width = P * (UNITS[n][0] + 1)
                    bias = s_bias[:, n % SB, first:first + count]
                    dve.wait_ge(s_done, upto(s_done, l, z + 1))
                    if n >= SB:
                        dve.wait_ge(e_done, upto(e_done, l, heads_through[z] - G * SB))
                    nc.vector.reduce_max(bias, bank[:, z % 3, 0:count * width].rearrange("p (q c) -> p q c", q=count),
                                         AXX).then_inc(m_step, 1)
                    dve.wait_ge(m_step, upto(m_step, l, 2 * z + 1))
                    nc.vector.tensor_scalar(bias, bias, NEG_GUARD, -SM, ALU.max, ALU.mult).then_inc(m_step, 1)

                dve.wait_ge(inv_ready, upto(inv_ready, l, 1))

                def factors(n, p):
                    i, g, b = UNITS[n]
                    sums = s_sum[:, n % SB, 2 * p:2 * p + 2]
                    dve.wait_ge(e_done, upto(e_done, l, G * n + 2 * p + 2))
                    gs = gate_inv[:, i, :].rearrange("p (h b) -> p h b", b=3)[:, G * g + 2 * p:G * g + 2 * p + 2, b + 1]
                    nc.vector.scalar_tensor_tensor(out=sums, in0=sums, scalar=1e-30, in1=gs, op0=ALU.max,
                                                   op1=ALU.mult).then_inc(r_step, 1)

                def y_rest(n):
                    dve.wait_ge(y_h, upto(y_h, l, n + 1))
                    minus(act_lo[:, 0:4, n * P:(n + 1) * P], bank[:, Y_BANK[n], :].rearrange("p (k c) -> p k c", k=4),
                          r32(act_hi[:, 0:4, n * P:(n + 1) * P])).then_inc(y_l, 1)

                for f in range(4):
                    if f == 3:
                        factors(0, 1)
                    for m in range(2):
                        if m == 0:
                            dve.wait_ge(q_h, upto(q_h, l, 2 * (f + 1)))
                        minus(QS[(1 - m) * DH:(2 - m) * DH, 2 * f + m, :], bank[m * DH:(m + 1) * DH, Q_BANK[f], :],
                              r32(QS[m * DH:(m + 1) * DH, 2 * f + m, :])).then_inc(q_l, 1)
                    for n, z in enumerate(EARLY_JOBS.get(f, ())):
                        maxima(z)
                        if f == 3 and n < 2:
                            y_rest(n)
                    if f == 2:
                        factors(0, 0)
                factors(1, 0)
                factors(1, 1)
                for n in (2, 3):
                    y_rest(n)

                def p_rest(k):
                    rows = NCP if ITEMS[k][0] is None else P
                    dve.wait_ge(pth, upto(pth, l, k + 1))
                    minus(pt_l[0:rows, k % 2, :], bank[0:rows, 3 + k % 3, :], r32(pt_h[0:rows, k % 2, :]))\
                        .then_inc(ptl, 1)

                def out_sum(v):
                    i, g = query_tile(v)
                    dve.wait_ge(oa_done, upto(oa_done, l, v + 1))
                    if v:
                        dve.wait_ge(ol_done, upto(ol_done, l, v))
                    for m in range(2):
                        view = lambda ap: ap.rearrange("p (a b c) -> p a b c", a=2, b=2)[:, :, m, :]
                        nc.vector.tensor_tensor(o_f[m * DH:(m + 1) * DH, :, :],
                                                view(bank[DH:P, 6 + v % 2, :]), view(o_a[:]), ALU.add)\
                            .then_inc(of_done, 1)

                NR = T * NKV * G

                def compressed_maxima(a):
                    dve.wait_ge(cs_done, upto(cs_done, l, a + 1))
                    nc.vector.reduce_max(c_stat[:, a * 16:a * 16 + 16],
                                         bank[:, 6 + a, :].rearrange("p (r c) -> p r c", c=NCP), AXX)\
                        .then_inc(c_step, 1)

                compressed_maxima(0)
                compressed_maxima(1)
                dve.wait_ge(c_step, upto(c_step, l, 2))
                nc.vector.tensor_scalar(c_stat[:], c_stat[:], NEG_GUARD, None, ALU.max).then_inc(c_step, 1)
                dve.wait_ge(c_step, upto(c_step, l, 3))
                for a in range(2):
                    last = nc.vector.tensor_tensor(
                        cE[:, a * 16:a * 16 + 16, :], bank[:, 6 + a, :].rearrange("p (r c) -> p r c", c=NCP),
                        c_stat[:, a * 16:a * 16 + 16].unsqueeze(2).broadcast_to([P, 16, NCP]), ALU.subtract)
                last.then_inc(c_step, 1)
                def compressed_step(k):
                    if k == 2:
                        dve.wait_ge(c_exp, upto(c_exp, l, 1))
                        nc.vector.reduce_sum(c_rec[:], cE[:], AXX).then_inc(c_step, 1)
                    if k == 3:
                        dve.wait_ge(c_step, upto(c_step, l, 5))
                        nc.vector.tensor_scalar(c_rec[:], c_rec[:], 1e-30, None, ALU.max).then_inc(c_step, 1)
                    if k == 4:
                        dve.wait_ge(c_step, upto(c_step, l, 6))
                        nc.vector.reciprocal(c_rec[:], c_rec[:]).then_inc(c_step, 1)
                    if k == 5:
                        dve.wait_ge(c_step, upto(c_step, l, 7))
                        nc.vector.tensor_tensor(c_rec[:].rearrange("p (t h) -> p t h", t=T),
                                                c_rec[:].rearrange("p (t h) -> p t h", t=T),
                                                gate[:].rearrange("p t (h b) -> p t h b", b=3)[:, :, :, 0], ALU.mult)\
                            .then_inc(c_step, 1)
                    if k == 6:
                        dve.wait_ge(c_step, upto(c_step, l, 8))
                        nc.vector.tensor_tensor(cE[:], cE[:], c_rec[:].unsqueeze(2).broadcast_to([P, NR, NCP]),
                                                ALU.mult).then_inc(c_step, 1)

                for k in range(NI + 3):
                    for unit, p in pairs_at(k - 2):
                        factors(unit, p)
                    if k < NI:
                        p_rest(k)
                    compressed_step(k)
                    for z in jobs_at(k):
                        maxima(z)
                    if k - 3 in LAST_OF_V.values():
                        out_sum(ITEMS[k - 3][1])

                for what, t in DVE_MID:
                    if what == "post":
                        add_branch(l, 3 * t, t, g_rest[:, 0, :], RS_MID[what, t], 4 * t + 1)
                    elif what == "pre":
                        dve.wait_ge(x_step, upto(x_step, l, 3 * t + 3))
                        normalise(l, 4 + t, t, g_rest[:, 1, :], RS_MID[what, t], 4 * t + 2)
                    else:
                        act_rests(l, 4 + t, t)

                taps = par[:, Q_CV:Q_CV + 8 * KF].rearrange("p (n q) -> p n q", q=4)
                def ff_rest(k):
                    dve.wait_ge(gh, upto(gh, l, k + 1))
                    minus(ff_lo(k), gff[:, k, :], r32(ff_hi(k))).then_inc(gl, 1)

                def conv_step(it):
                    for p in range(2):
                        for s in range(2):
                            col = it * 2 + (s * KF + p)
                            y = cv[:, p, s, :]
                            u = bank[:, 2 * p + s, :]
                            dve.wait_ge(cv0, l * (2 * KF) + it * 4 + (2 * p + s + 1))
                            nc.vector.scalar_tensor_tensor(
                                out=y[:, 1:SEQ], in0=u[:, 0:SEQ - 1], scalar=taps[:, bass.ds(col, 1), 1],
                                in1=y[:, 1:SEQ], op0=ALU.mult, op1=ALU.add).then_inc(cv_step, 1)
                            dve.wait_ge(cv_step, l * (4 * KF) + it * 8 + (4 * p + 2 * s + 1 + AHEAD))
                            nc.vector.scalar_tensor_tensor(
                                out=y[:, 2:SEQ], in0=u[:, 0:SEQ - 2], scalar=taps[:, bass.ds(col, 1), 0],
                                in1=y[:, 2:SEQ], op0=ALU.mult, op1=ALU.add).then_inc(cv_step, 1)
                        dve.wait_ge(cv_step, l * (4 * KF) + it * 8 + (4 * p + 4 + AHEAD))
                        dve.wait_ge(gelu_done, l * KF + it * 2 + (p + 1))
                        nc.vector.tensor_tensor(gff[:, bass.ds(it * 2 + p, 1), :].rearrange("p a c -> p (a c)"),
                                                cv[:, p, 0, :], cv[:, p, 1, :], ALU.mult).then_inc(g_ready, 1)

                with dve.Fori(0, KF // 2 - 1) as it:
                    conv_step(it)
                ff_rest(0)
                ff_rest(1)
                conv_step(KF // 2 - 1)
                for k in range(2, KF):
                    ff_rest(k)
                for t in range(T):
                    add_branch(l, 12 + 3 * t, t, g_rest[:, 2, :], RS_POST2(t), 4 * t + 3)

        @block.tensor
        def _(pe):
            mm = nc.tensor.matmul

            def arrived(layer, c):
                pe.wait_ge(lo_ready, upto(lo_ready, layer, c + 1))

            def passes(a, b):
                return ((a[0], b[0]), (a[0], b[1]), (a[1], b[0]))

            def turn_h(layer, n, t):
                pe.wait_ge(h_ready, upto(h_ready, layer, n + 1))
                for k in range(KD):
                    last = nc.tensor.transpose(bank[:, t + 4 * (k // 4), (k % 4) * P:(k % 4 + 1) * P],
                                               h[:, t % 2, k * P:(k + 1) * P], ident)
                last.then_inc(h_turned, 1)

            def token_block(layer, first, width, b0, done, before, by_tile=False, turn=None):
                order = [(c, t) for t in range(T) for c in range(4)] if by_tile else \
                        [(c, t) for c in range(4) for t in range(T)]
                for c, t in order:
                    if c == 0 and turn:
                        turn(t)
                    arrived(layer, first + c)
                    before(c, t)
                    for kk in range(2):
                        k = 2 * c + kk
                        s = (first + c) % RING
                        cols = slice(kk * width, (kk + 1) * width)
                        rows = (act_hi[:, k, t * P:(t + 1) * P], act_lo[:, k, t * P:(t + 1) * P])
                        w = (w_hi[:, s, cols], w_lo[:, s, cols])
                        for n, (a, b) in enumerate(passes(rows, w)):
                            last = mm(bank[:, b0 + t, 0:width], a, b, start=(k == 0 and n == 0),
                                      stop=(k == KD - 1 and n == 2))
                    if t == T - 1:
                        last.then_inc(w_used, 1)
                    elif c == 3:
                        last.then_inc(done, 1)

            def feature_tile(layer, c, b):
                s = c % RING
                arrived(layer, c)
                for k in range(KD):
                    cols = slice(k * P, (k + 1) * P)
                    for n, (a, v) in enumerate(passes((w_hi[:, s, cols], w_lo[:, s, cols]),
                                                      (act_hi[:, k, :], act_lo[:, k, :]))):
                        last = mm(bank[:, b, :], a, v, start=(k == 0 and n == 0), stop=(k == KD - 1 and n == 2))
                last.then_inc(w_used, 1)

            pe.sem_inc(w_used, RING)
            pe.wait_ge(masks_loaded, 16)
            pe.wait_ge(const_cast, 3)
            with pe.Fori(0, DEPTH) as l:
                def turn_pre1(t):
                    pe.wait_ge(x_step, upto(x_step, l, 3 * (t + 1) - 12))
                    turn_h(l, t, t)

                turn_pre1(0)
                def before_t(blk):
                    def f(c, t):
                        if c:
                            return
                        if blk == 0:
                            pe.wait_ge(act_l, upto(act_l, l, 2 * t + 2))
                        if blk == 1:
                            pe.wait_ge(act_l, upto(act_l, l, 8))
                        if blk == 2:
                            pe.wait_ge(rot_step, upto(rot_step, l, 4 * t + 3))
                        if blk == 3:
                            pe.wait_ge(rot_step, upto(rot_step, l, 16 + 4 * t + 3))
                        if blk == 4:
                            pe.wait_ge(rv_ready, upto(rv_ready, l, t + 1))
                    return f
                token_block(l, C_T, 512, 4, t_done, before_t(0), by_tile=True,
                            turn=lambda t: turn_pre1(t + 1) if t + 1 < T else None)
                for blk in range(1, 4):
                    token_block(l, C_T + 4 * blk, 512, 4 if blk % 2 == 0 else 0, t_done, before_t(blk))
                token_block(l, C_TV, NTV, 4, t_done, before_t(4))

                def turn_qk(n):
                    pe.wait_ge(sg_ready, upto(sg_ready, l, 4))
                    if n:
                        pe.wait_ge(qk_copied, upto(qk_copied, l, 2 * n))
                        pe.wait_ge(qx_ready, upto(qx_ready, l, n))
                    else:
                        pe.wait_ge(rot_step, upto(rot_step, l, 32))
                    for m, src in ((0, qr), (1, kr)):
                        for a in range(4):
                            last = nc.tensor.transpose(bank[:, 2 + m, a * P:(a + 1) * P],
                                                       src[:, n, a * P:(a + 1) * P], ident)
                        last.then_inc(qk_turned, 1)

                def scores(n):
                    pe.wait_ge(qk_copied, upto(qk_copied, l, 2 * n + 2))
                    if n:
                        pe.wait_ge(st_masked, upto(st_masked, l, 2 * n))
                    else:
                        pe.wait_ge(vg_dve, upto(vg_dve, l, 8))
                    for hd in range(RH):
                        rows = slice((hd % 2) * DK, (hd % 2 + 1) * DK)
                        last = mm(bank[:, 4 + hd % 2, (hd // 2) * P:(hd // 2 + 1) * P],
                                  kT[rows, hd // 2, :], qT[rows, hd // 2, :], start=True, stop=True)
                        if hd >= RH - 2:
                            last.then_inc(st_done, 1)

                def ret_out(n):
                    if n:
                        pe.wait_ge(state_step, upto(state_step, l, 3 * n - 2))
                    if n < T - 1:
                        pe.wait_ge(vz_ready, upto(vz_ready, l, n + 1))
                        for a in range(4):
                            last = mm(bank[:, 7, a * P:(a + 1) * P], kr[:, n, a * P:(a + 1) * P],
                                      vz[:, a * P:(a + 1) * P], start=True, stop=True)
                        last.then_inc(kv_done, 1)
                    pe.wait_ge(rv_ready, upto(rv_ready, l, n + 1))
                    pe.wait_ge(st_masked, upto(st_masked, l, 2 * n + 2))
                    pe.wait_ge(qx_ready, upto(qx_ready, l, n + 1))
                    if n:
                        pe.wait_ge(y_step, upto(y_step, l, 2 * n - 1))
                    for a in range(4):
                        if n:
                            mm(bank[:, 6, a * P:(a + 1) * P], qxT[:, a, :], state[:, a, :], start=True,
                               stop=False, skip_group_check=True)
                        for m in range(2):
                            hd = 2 * a + m
                            last = mm(bank[:, 6, hd * DK:(hd + 1) * DK], stm[:, hd, :],
                                      rv[:, n, hd * DK:(hd + 1) * DK], start=(n == 0), stop=True,
                                      skip_group_check=True)
                    last.then_inc(ro_done, 1)

                def first_layer(s, c):
                    j = c - (C_W1K, C_W1V)[s]
                    arrived(l, c)
                    if j == 0:
                        pe.wait_ge(z_l, upto(z_l, l, s + 1))
                        if s:
                            pe.wait_ge(z_step, upto(z_step, l, 17))
                    for kk in range(4):
                        k = 4 * j + kk
                        cols = slice(kk * HID, (kk + 1) * HID)
                        z = zs[:, k].rearrange("p a c -> p (a c)")
                        mm(bank[:, s, 0:HID], z, w_hi[:, c % RING, cols], start=(k == 0), stop=False)
                        last = mm(bank[:, s, 0:HID], z, w_lo[:, c % RING, cols], start=False, stop=(k == 15))
                    last.then_inc(w_used, 1)

                def turn_hidden(s):
                    pe.wait_ge(hraw_ready, upto(hraw_ready, l, s + 1))
                    for m in range(2):
                        last = mm(bank[:, s, HID + m * 64:HID + (m + 1) * 64], hraw[:, m * P:(m + 1) * P], fold,
                                  start=True, stop=True)
                    last.then_inc(hid_turned, 1)

                for what, n in MIDDLE:
                    if what == "turn":
                        turn_qk(n)
                    if what == "score":
                        scores(n)
                    if what == "out":
                        ret_out(n)
                    if what == "hidden":
                        turn_hidden(n)
                    if what == "chunk":
                        if n <= C_F1:
                            feature_tile(l, n, n - C_F0)
                        elif n < C_W1V:
                            first_layer(0, n)
                        else:
                            first_layer(1, n)
                def second_layer():
                    pe.wait_ge(hid_ready, upto(hid_ready, l, 4))
                    w2 = par[:, Q_W2:Q_B2K].rearrange("p (s m d) -> p s m d", s=2, m=2)
                    for m in range(2):
                        last = mm(bank[0:DH, 0, KC_AT:KC_AT + NKV * NCP], w2[:, 0, m, :], hid[:, 0, m, :],
                                  start=(m == 0), stop=(m == 1))
                    last.then_inc(kc_done, 1)
                    for g in range(NKV):
                        for m in range(2):
                            last = mm(bank[0:NCP, 1, KC_AT + g * DH:KC_AT + (g + 1) * DH],
                                      hid[:, 1, m, g * NCP:(g + 1) * NCP], w2[:, 1, m, :],
                                      start=(m == 0), stop=(m == 1))
                    last.then_inc(vc_done, 1)

                def job_scores(z):
                    n, first, count = JOBS[z]
                    i, g, b = UNITS[n]
                    width = P * (i + 1)
                    if z >= 3:
                        pe.wait_ge(e_done, upto(e_done, l, heads_through[z - 3]))
                    else:
                        pe.wait_ge(kc_f, upto(kc_f, l, 1))
                        pe.wait_ge(vc_f, upto(vc_f, l, 1))
                        pe.wait_ge(k_l, upto(k_l, l, 8))
                    if z < 2 * G:
                        pe.wait_ge(q_l, upto(q_l, l, 2 * (first // 2 + 1)))
                    diagonal = bank[:, z % 3, 0:count * width].rearrange("p (q c) -> p q c", q=count)[:, :, P * i:width]
                    mm(diagonal, ident_b[:], causal_b[:].unsqueeze(1).broadcast_to([P, count, P]), start=True,
                       stop=False, skip_group_check=True)
                    for q in range(count):
                        query = QS[:, G * g + first + q, i * P:(i + 1) * P]
                        dst = bank[:, z % 3, q * width:(q + 1) * width]
                        mm(dst, query, KH[:, 2 * b + g, 0:width], start=False, stop=False, skip_group_check=True)
                        last = mm(dst, query, KL[:, 2 * b + g, 0:width], start=False, stop=True,
                                  skip_group_check=True)
                    last.then_inc(s_done, 1)

                def compressed_scores(f):
                    if f == 0:
                        pe.wait_ge(kc_l, upto(kc_l, l, 2))
                        pe.wait_ge(y_step, upto(y_step, l, 7))
                        for a in range(2):
                            mask = cmask_b[:, 2 * a * NCP:(2 * a + 2) * NCP].rearrange("p (t c) -> p t c", t=2)
                            mm(bank[:, 6 + a, :], ident_b[:], mask.unsqueeze(2).broadcast_to([P, 2, NH, NCP]),
                               start=True, stop=False, skip_group_check=True)
                    pe.wait_ge(q_l, upto(q_l, l, 2 * (f + 1)))
                    for t in range(T):
                        for hd in (2 * f, 2 * f + 1):
                            g = hd // G
                            at = (t % 2 * NH + hd) * NCP
                            q = QS[:, hd, t * P:(t + 1) * P]
                            for m, key in enumerate((KcH, KcL)):
                                last = mm(bank[:, 6 + t // 2, at:at + NCP], q, key[:, g * NCP:(g + 1) * NCP],
                                          start=False, stop=(m == 1), skip_group_check=True)
                        if f == 3 and t % 2:
                            last.then_inc(cs_done, 1)

                for f in range(2):
                    pe.wait_ge(qk_copied, upto(qk_copied, l, 8))
                    pe.wait_ge(qx_ready, upto(qx_ready, l, 4))
                    feature_tile(l, C_F2 + f, 2 + f)
                    if f == 0:
                        pe.wait_ge(par_loaded, upto(par_loaded, l, 48))
                        second_layer()
                pe.wait_ge(st_masked, upto(st_masked, l, 8))
                for f in range(4):
                    if f == 2:
                        pe.wait_ge(k_l, upto(k_l, l, 8))
                    if f == 3:
                        pe.wait_ge(q_l, upto(q_l, l, 2))
                    feature_tile(l, C_F2 + 2 + f, Q_BANK[f])
                    for z in EARLY_JOBS.get(f, ()):
                        job_scores(z)
                    if f:
                        compressed_scores(f - 1)
                pe.wait_ge(y_step, upto(y_step, l, 8))
                for n in range(T):
                    if n == 2:
                        compressed_scores(3)
                    if n < 3:
                        pe.wait_ge(q_l, upto(q_l, l, 2 * n + 4))
                    else:
                        pe.wait_ge(y_l, upto(y_l, l, 1))
                    for a in range(4):
                        last = nc.tensor.transpose(bank[:, Y_BANK[n], a * P:(a + 1) * P],
                                                   qr[:, n, a * P:(a + 1) * P], ident)
                    last.then_inc(y_turned, 1)
                def turn_p(k):
                    n, v, j = ITEMS[k]
                    if k >= 3:
                        pe.wait_ge(ptl, upto(ptl, l, k - 2))
                    else:
                        pe.wait_ge(y_l, upto(y_l, l, 4))
                    if n is None:
                        pe.wait_ge(c_step, upto(c_step, l, 9))
                        for r in range(G):
                            last = nc.tensor.transpose(bank[0:NCP, 3 + k % 3, r * P:(r + 1) * P],
                                                       cE[:, query_tile(v)[0] * NH + v % NKV * G + r, :], ident)
                    else:
                        for r in range(G):
                            if j == 0:
                                pe.wait_ge(p_scaled, upto(p_scaled, l, G * n + r + 1))
                            last = nc.tensor.transpose(bank[:, 3 + k % 3, r * P:(r + 1) * P],
                                                       E[:, E_AT[n][0], r, E_AT[n][1] + j * P:E_AT[n][1] + (j + 1) * P], ident)
                    last.then_inc(pt_done, 1)

                def product(k):
                    n, v, j = ITEMS[k]
                    first = k == FIRST_OF_V[v]
                    o = bank[:, 6 + v % 2, :]
                    if first:
                        if v >= 2:
                            pe.wait_ge(of_done, upto(of_done, l, 2 * (v - 1)))
                        else:
                            pe.wait_ge(c_step, upto(c_step, l, 4))
                    if n is None:
                        pe.wait_ge(vc_l, upto(vc_l, l, 1))
                        g = v % NKV
                        w, rows = VcS[:, g, :], NCP
                    else:
                        i, g, b = UNITS[n]
                        w, rows = VS[:, j, 2 * b + g, :], P
                    pe.wait_ge(ptl, upto(ptl, l, k + 1))
                    mm(o, w, pt_h[0:rows, k % 2, :], start=first, stop=False)
                    mm(o, w, pt_l[0:rows, k % 2, :], start=False, stop=(k == LAST_OF_V[v])).then_inc(pv_done, 1)

                for k in range(NI):
                    turn_p(k)
                    if k >= 2:
                        product(k - 2)
                    for z in jobs_at(k):
                        job_scores(z)
                product(NI - 2)
                product(NI - 1)

                for half in range(2):
                    def before(c, t, half=half):
                        if half == 0 and t == 0 and c == 0:
                            pe.wait_ge(e_done, upto(e_done, l, G * NU))
                            pe.wait_ge(ptl, upto(ptl, l, NI))
                        if half == 0 and t == 0 and c == 2:
                            pe.wait_ge(ol_done, upto(ol_done, l, T * NKV))
                    def turn_done(t):
                        if t == T - 1:
                            pe.wait_ge(x_step, upto(x_step, l, 2))
                            turn_h(l, 4, 0)
                    token_block(l, C_WO + 4 * half, 512, 4 * half, wo_done, before, by_tile=(half == 1),
                                turn=turn_done if half else None)
                def turn_next(t):
                    pe.wait_ge(x_step, upto(x_step, l, 3 * t + 2))
                    turn_h(l, 4 + t, t)

                def up_tile(s, first, end):
                    for k in range(KD):
                        cols = slice(k * P, (k + 1) * P)
                        for n, (a, v) in enumerate(passes((w_hi[:, s, cols], w_lo[:, s, cols]),
                                                          (act_hi[:, k, first:end], act_lo[:, k, first:end]))):
                            last = mm(bank[:, s, first:end], a, v, start=(k == 0 and n == 0),
                                      stop=(k == KD - 1 and n == 2))
                    return last

                early = SEQ - P
                turn_next(1)
                turn_next(2)
                pe.wait_ge(act_l, upto(act_l, l, 14))
                for s in range(3):
                    arrived(l, C_UP + s)
                    up_tile(s, 0, early)
                    if s == 1:
                        turn_next(3)
                pe.wait_ge(act_l, upto(act_l, l, 16))
                for s in range(3):
                    up_tile(s, early, SEQ).then_inc(w_used, 1)
                arrived(l, C_UP + 3)
                up_tile(3, 0, SEQ).then_inc(w_used, 1)
                with pe.Fori(1, KF // 2) as it:
                    for s in range(RING):
                        pe.wait_ge(lo_ready, l * NCH + it * RING + (C_UP + s + 1 + RING))
                        pe.wait_ge(cv_step, l * (4 * KF) + it * 8 + (2 * s + 2))
                        up_tile(s, 0, SEQ).then_inc(w_used, 1)
                def down(k, t, half):
                    s = (C_DN + k) % RING
                    if t == 0:
                        arrived(l, C_DN + k)
                        pe.wait_ge(gl, upto(gl, l, k + 1))
                    rows = (ff_hi(k)[:, t * P:(t + 1) * P], ff_lo(k)[:, t * P:(t + 1) * P])
                    cols = slice(512 * half, 512 * half + 512)
                    for n, (a, b) in enumerate(passes(rows, (w_hi[:, s, cols], w_lo[:, s, cols]))):
                        last = mm(bank[:, t + 4 * half, :], a, b, start=(k == 0 and n == 0),
                                  stop=(k == KF - 1 and n == 2))
                    return last

                for k in range(2):
                    for t in range(T):
                        down(k, t, 1)
                pe.wait_ge(cv_step, upto(cv_step, l, 4 * KF))
                for k in range(2):
                    for t in range(T):
                        last = down(k, t, 0)
                    last.then_inc(w_used, 1)
                head = [(k, t) for k in range(2, KF - RING) for t in range(T)]
                tail = [(k, t) for t in range(T) for k in range(KF - RING, KF)]
                for k, t in head + tail:
                    down(k, t, 0)
                    last = down(k, t, 1)
                    if t == T - 1:
                        last.then_inc(w_used, 1)
                    elif k == KF - 1:
                        last.then_inc(dn_done, 1)


def _constants():
    f = np.float32
    out = np.zeros((P, NCONST), f)
    inv = f(1.0) / f(10000.0) ** np.linspace(0.0, 1.0, DK // 2, dtype=f)
    ang = (np.arange(SEQ, dtype=f)[:, None] * inv[None, :]).astype(f)
    tab = lambda a: a.astype(f).reshape(T, P, DK // 2).transpose(1, 0, 2).reshape(P, -1)
    out[:, O_COS:O_SIN], out[:, O_SIN:O_NSIN], out[:, O_NSIN:O_DM] = tab(np.cos(ang)), tab(np.sin(ang)), tab(-np.sin(ang))
    log_g = np.log(f(1.0) - f(2.0) ** (f(-5.0) - np.arange(RH, dtype=f))).astype(f)
    i = np.arange(P, dtype=f)
    diff = i[None, :] - i[:, None]
    scale = f(DK ** -0.5)
    dm = np.where(diff >= 0, np.exp(np.maximum(diff, 0)[None] * log_g[:, None, None]), 0).astype(f)
    out[:, O_DM:O_XI] = (dm * scale).transpose(1, 0, 2).reshape(P, -1)
    xi = np.exp((i + 1)[None, :] * log_g[:, None]).astype(f)
    out[:, O_XI:O_ZE] = np.repeat(xi.reshape(4, 2, 1, P), DK, axis=2).reshape(4, P, P).transpose(1, 0, 2).reshape(P, -1)
    out[:, O_ZE:O_BD] = np.exp((P - 1 - i)[:, None] * log_g[None, :])
    out[:DK, O_BD:O_BD + DK] = scale
    out[DK:, O_BD + DK:O_DE] = scale
    out[:, O_DE:O_ID] = np.repeat(np.exp(P * log_g).astype(f).reshape(4, 2), DK, axis=1).T
    out[:, O_ID:O_CA] = np.eye(P, dtype=f)
    out[:, O_CA:O_CM] = np.where(np.arange(P)[None, :] <= np.arange(P)[:, None], 0, NEG)
    tok = np.arange(SEQ).reshape(T, P).T[:, :, None]
    c = np.arange(NCP)[None, None, :]
    out[:, O_II:] = np.tile(np.eye(P // 2, dtype=f), (2, 1))
    out[:, O_CM:O_II] = np.where((c < NC) & (c * CS + CB - 1 <= tok), 0, NEG).reshape(P, -1)
    return out


def _stream(w_in, w_out, kw1, vw1, w_up, w_down):
    stream = np.zeros((DEPTH * NCH + RING, P, CW), np.float32)
    st = stream[:DEPTH * NCH].reshape(DEPTH, NCH, P, CW)

    def token(c0, w):
        n = w.shape[-1]
        st[:, c0:c0 + 4, :, :2 * n] = w.reshape(DEPTH, 4, 2, P, n).transpose(0, 1, 3, 2, 4).reshape(DEPTH, 4, P, 2 * n)

    def feature(c, w):
        st[:, c] = w.reshape(DEPTH, KD, P, P).transpose(0, 2, 1, 3).reshape(DEPTH, P, CW)

    r = RH * DK
    for b in range(4):
        token(C_T + 4 * b, w_in[:, :, b * r:(b + 1) * r])
    nq, kv = 4 * r, 4 * r + NH * DH
    col = lambda s: w_in[:, :, kv + s * NKV * DH:kv + (s + 1) * NKV * DH]
    token(C_TV, np.concatenate([col(3), col(5), w_in[:, :, kv + 6 * NKV * DH:]], axis=-1))
    feature(C_F0, col(0))
    feature(C_F1, col(1))
    for c0, w in ((C_W1K, kw1), (C_W1V, vw1)):
        st[:, c0:c0 + 4] = w.reshape(DEPTH, 4, 4, P, HID).transpose(0, 1, 3, 2, 4).reshape(DEPTH, 4, P, CW)
    feature(C_F2, col(2))
    feature(C_F2 + 1, col(4))
    for f in range(4):
        feature(C_F2 + 2 + f, w_in[:, :, nq + f * P:nq + (f + 1) * P])
    for half in range(2):
        token(C_WO + 4 * half, w_out[:, :, half * 512:(half + 1) * 512])
    for n in range(KF):
        feature(C_UP + 2 * n, w_up[:, :, n * P:(n + 1) * P])
        feature(C_UP + 2 * n + 1, w_up[:, :, FF + n * P:FF + (n + 1) * P])
    st[:, C_DN:] = w_down.reshape(DEPTH, KF, P, D)
    return stream


def _parameters(kpos, vpos, kb1, vb1, kw2, vw2, kb2, conv_w, conv_b):
    out = np.zeros((DEPTH, P, NPAR), np.float32)
    for s, pos in enumerate((kpos, vpos)):
        out[:, :, Q_POS + 16 * s:Q_POS + 16 * s + 16] = pos.reshape(DEPTH, 16, P).transpose(0, 2, 1)
    for s, b in enumerate((kb1, vb1)):
        out[:, :, Q_B1 + 2 * s:Q_B1 + 2 * s + 2] = b.reshape(DEPTH, 2, P).transpose(0, 2, 1)
    for s, w in enumerate((kw2, vw2)):
        out[:, :, Q_W2 + 2 * DH * s:Q_W2 + 2 * DH * (s + 1)] = w.reshape(DEPTH, 2, P, DH).transpose(0, 2, 1, 3).reshape(DEPTH, P, -1)
    out[:, :DH, Q_B2K] = kb2
    taps = np.concatenate([conv_w, conv_b[:, None]], axis=1)
    out[:, :, Q_CV:] = taps.reshape(DEPTH, 4, 2 * KF, P).transpose(0, 3, 2, 1).reshape(DEPTH, P, -1)
    return out


def kernel(x, ln_mix_pre, ln_mix_post, ln_ffn_pre, ln_ffn_post, w_in, w_out, cmp_k_pos, cmp_k_w1, cmp_k_b1,
           cmp_k_w2, cmp_k_b2, cmp_v_pos, cmp_v_w1, cmp_v_b1, cmp_v_w2, cmp_v_b2, ffn_w_up, ffn_conv_w,
           ffn_conv_b, ffn_w_down):
    import concourse.bacc as bacc
    from concourse.bass_utils import run_bass_kernel_spmd

    a = lambda v: np.asarray(v)
    gains = np.zeros((DEPTH + 1, 2, 3 * D), np.float32)
    gains[:DEPTH, 0, :D] = a(ln_mix_pre)
    gains[:DEPTH, 1, :D], gains[:DEPTH, 1, D:2 * D] = a(ln_mix_post), a(ln_ffn_pre)
    gains[:DEPTH, 1, 2 * D:] = a(ln_ffn_post)
    arrays = {
        "x_in": a(x).reshape(SEQ, D),
        "wstream": _stream(a(w_in), a(w_out), a(cmp_k_w1), a(cmp_v_w1), a(ffn_w_up), a(ffn_w_down)),
        "gains": gains,
        "pars": _parameters(a(cmp_k_pos), a(cmp_v_pos), a(cmp_k_b1), a(cmp_v_b1), a(cmp_k_w2), a(cmp_v_w2),
                            a(cmp_k_b2), a(ffn_conv_w), a(ffn_conv_b)),
        "b2v_in": a(cmp_v_b2).reshape(DEPTH, 1, DH),
        "consts": _constants(),
    }
    nc = bacc.Bacc("TRN2", target_bir_lowering=False, num_devices=1)
    args = {n: nc.dram_tensor(n, v.shape, mybir.dt.from_np(v.dtype), kind="ExternalInput").ap()
            for n, v in arrays.items()}
    x_out = nc.dram_tensor("x_out", (SEQ, D), F32, kind="ExternalOutput").ap()
    build(nc, **args, x_out=x_out)
    r = run_bass_kernel_spmd(nc, [arrays], core_ids=[0])
    return r.results[0]["x_out"].reshape(1, SEQ, D)
```
